# Optimizing a Trainium2 kernel written in Bass

```python
import math
import jax, jax.numpy as jnp
from jax import lax
import numpy as np

D_MODEL = 1024
BATCH = 1
SEQ = 256
DEPTH = 2

CHUNK = 64
Q_BLOCK = 128
EPS = 1e-6
N_A_LAYERS = DEPTH // 2
N_B_LAYERS = DEPTH - N_A_LAYERS

A_HEADS = 6
A_HEAD_DIM = 128
A_WIDTH = A_HEADS * A_HEAD_DIM
CONV_K = 4

B_HEADS = 6
QK_NOPE = 128
QK_ROPE = 64
V_HEAD = 128
Q_LORA = 256
KV_LORA = 256
B_WIDTH = B_HEADS * V_HEAD
ROPE_THETA = 10000.0

N_MEM = 256
MEM_HEADS = 4
MEM_HEAD_DIM = 64
MEM_WIDTH = MEM_HEADS * MEM_HEAD_DIM

D_FF = 2816

MIX_WIDTH = A_WIDTH + MEM_WIDTH
A_IN = 4 * A_WIDTH + 2 * A_HEADS + MEM_WIDTH
B_IN = Q_LORA + MEM_WIDTH


def rms_norm(x, g):
    xf = x.astype(jnp.float32)
    y = xf * lax.rsqrt(jnp.mean(xf * xf, axis=-1, keepdims=True) + EPS)
    return (y * g.astype(jnp.float32)).astype(x.dtype)

def l2_norm(x):
    xf = x.astype(jnp.float32)
    return (xf * lax.rsqrt(jnp.sum(xf * xf, axis=-1, keepdims=True) + EPS)).astype(x.dtype)

def swiglu(x, w_gu, w_down):
    gate, up = jnp.split(x @ w_gu, 2, axis=-1)
    return (jax.nn.silu(gate) * up) @ w_down

def rope_tables(positions, dim):
    inv = ROPE_THETA ** (-jnp.arange(0, dim, 2, dtype=jnp.float32) / dim)
    ang = positions.astype(jnp.float32)[..., None] * inv
    return jnp.cos(ang), jnp.sin(ang)

def apply_rope(x, cos, sin):
    xf = x.astype(jnp.float32)
    x1, x2 = jnp.split(xf, 2, axis=-1)
    c, s = cos[:, :, None, :], sin[:, :, None, :]
    return jnp.concatenate([x1 * c - x2 * s, x1 * s + x2 * c], axis=-1).astype(x.dtype)

def causal_depthwise_conv(x, w):
    k = w.shape[0]
    return lax.conv_general_dilated(
        x, w[:, None, :].astype(x.dtype), window_strides=(1,), padding=[(k - 1, 0)],
        dimension_numbers=("NWC", "WIO", "NWC"), feature_group_count=x.shape[-1])

def chunked_gated_delta_rule(q, k, v, beta, g):
    b, s, h, dk = q.shape
    dv = v.shape[-1]
    n = s // CHUNK
    f32 = jnp.float32

    def chunks(t):
        return t.astype(f32).reshape(b, n, CHUNK, h, -1).transpose(0, 3, 1, 2, 4)

    q, k, v = chunks(q), chunks(k), chunks(v)
    beta = chunks(beta[..., None])[..., 0]
    g_cum = jnp.cumsum(chunks(g[..., None])[..., 0], axis=-1)
    causal = jnp.tril(jnp.ones((CHUNK, CHUNK), dtype=bool))
    strict = jnp.tril(jnp.ones((CHUNK, CHUNK), dtype=bool), -1)
    diff = g_cum[..., :, None] - g_cum[..., None, :]
    decay = jnp.where(causal, jnp.exp(jnp.where(causal, diff, 0.0)), 0.0)
    k_beta = k * beta[..., None]
    t_mat = jnp.where(strict, jnp.einsum("bhnid,bhnjd->bhnij", k_beta, k) * decay, 0.0) \
        + jnp.eye(CHUNK, dtype=f32)
    u = lax.linalg.triangular_solve(t_mat, v * beta[..., None], left_side=True,
                                    lower=True, unit_diagonal=True)
    w = lax.linalg.triangular_solve(t_mat, k_beta * jnp.exp(g_cum)[..., None], left_side=True,
                                    lower=True, unit_diagonal=True)
    qk = jnp.einsum("bhnid,bhnjd->bhnij", q, k) * decay
    g_last = g_cum[..., -1:]
    q_dec = q * jnp.exp(g_cum)[..., None]
    k_dec = k * jnp.exp(g_last - g_cum)[..., None]
    chunk_decay = jnp.exp(g_last[..., 0])
    xs = tuple(jnp.moveaxis(t, 2, 0) for t in (q_dec, k_dec, w, u, qk, chunk_decay))

    def step(state, inp):
        q_c, k_c, w_c, u_c, qk_c, d_c = inp
        v_new = u_c - jnp.einsum("bhcd,bhde->bhce", w_c, state)
        out = jnp.einsum("bhcd,bhde->bhce", q_c, state) + jnp.einsum("bhij,bhje->bhie", qk_c, v_new)
        state = state * d_c[..., None, None] + jnp.einsum("bhcd,bhce->bhde", k_c, v_new)
        return state, out

    _, o = lax.scan(step, jnp.zeros((b, h, dk, dv), f32), xs)
    return o.transpose(1, 0, 3, 2, 4).reshape(b, s, h, dv)

def gated_deltanet(qkv, gate, b_raw, a_raw, conv_w, A_log, dt_bias, out_gain):
    b, s, _ = qkv.shape
    qkv = jax.nn.silu(causal_depthwise_conv(qkv, conv_w))
    q, k, v = (t.reshape(b, s, A_HEADS, A_HEAD_DIM) for t in jnp.split(qkv, 3, axis=-1))
    q = l2_norm(q) * A_HEAD_DIM ** -0.5
    k = l2_norm(k)
    beta = jax.nn.sigmoid(b_raw.astype(jnp.float32))
    g = -jnp.exp(A_log.astype(jnp.float32)) * jax.nn.softplus(
        a_raw.astype(jnp.float32) + dt_bias.astype(jnp.float32))
    o = chunked_gated_delta_rule(q, k, v, beta, g).astype(qkv.dtype)
    o = rms_norm(o, out_gain) * jax.nn.silu(gate.reshape(b, s, A_HEADS, A_HEAD_DIM))
    return o.reshape(b, s, A_WIDTH)

def mla_attention(q_nope, q_rope, k_nope, k_rope, v):
    b, s, h, _ = q_nope.shape
    nb = s // Q_BLOCK
    scale = (QK_NOPE + QK_ROPE) ** -0.5
    key_chunk = jnp.arange(s) // CHUNK
    qn = q_nope.reshape(b, nb, Q_BLOCK, h, QK_NOPE).swapaxes(0, 1)
    qr = q_rope.reshape(b, nb, Q_BLOCK, h, QK_ROPE).swapaxes(0, 1)

    def block(args):
        i, qn_b, qr_b = args
        sc = (jnp.einsum("bqhd,bkhd->bhqk", qn_b, k_nope)
              + jnp.einsum("bqhd,bkd->bhqk", qr_b, k_rope)).astype(jnp.float32) * scale
        q_chunk = (i * Q_BLOCK + jnp.arange(Q_BLOCK)) // CHUNK
        mask = key_chunk[None, :] <= q_chunk[:, None]
        p = jax.nn.softmax(jnp.where(mask, sc, -jnp.inf), axis=-1).astype(v.dtype)
        return jnp.einsum("bhqk,bkhd->bqhd", p, v)

    out = lax.map(block, (jnp.arange(nb), qn, qr))
    return out.swapaxes(0, 1).reshape(b, s, h * V_HEAD)

def memory_attention(q, mem_kv):
    b, s, _ = q.shape
    q = q.reshape(b, s, MEM_HEADS, MEM_HEAD_DIM)
    k, v = (t.reshape(b, N_MEM, MEM_HEADS, MEM_HEAD_DIM) for t in jnp.split(mem_kv, 2, axis=-1))
    sc = jnp.einsum("bqhd,bmhd->bhqm", q, k).astype(jnp.float32) * MEM_HEAD_DIM ** -0.5
    p = jax.nn.softmax(sc, axis=-1).astype(v.dtype)
    return jnp.einsum("bhqm,bmhd->bqhd", p, v).reshape(b, s, MEM_WIDTH)

def first_inputs(seed: int = 0) -> dict:
    key = jax.random.key(seed)
    ks = iter(jax.random.split(key, 40))
    f32 = jnp.float32

    def dense(shape, fan_in):
        return jax.random.normal(next(ks), shape, f32) * fan_in ** -0.5

    def gain(shape):
        return 1.0 + 0.02 * jax.random.normal(next(ks), shape, f32)

    x = jax.random.normal(next(ks), (BATCH, SEQ, D_MODEL), f32)
    mem = jax.random.normal(next(ks), (BATCH, N_MEM, D_MODEL), f32)
    offset = jax.random.randint(next(ks), (BATCH, 1), 0, 64, dtype=jnp.int32) * CHUNK
    positions = (offset + jnp.arange(SEQ, dtype=jnp.int32)[None, :]).astype(jnp.int32)

    ffn1_norm = gain((DEPTH, D_MODEL))
    ffn1_w_gu = dense((DEPTH, D_MODEL, 2 * D_FF), D_MODEL)
    ffn1_w_down = dense((DEPTH, D_FF, D_MODEL), D_FF)
    mix_norm = gain((DEPTH, D_MODEL))
    ffn2_norm = gain((DEPTH, D_MODEL))
    ffn2_w_gu = dense((DEPTH, D_MODEL, 2 * D_FF), D_MODEL)
    ffn2_w_down = dense((DEPTH, D_FF, D_MODEL), D_FF)
    w_out = dense((DEPTH, MIX_WIDTH, D_MODEL), MIX_WIDTH)
    mem_norm = gain((D_MODEL,))
    w_mem_kv = dense((DEPTH, D_MODEL, 2 * MEM_WIDTH), D_MODEL)

    a_w_in = dense((N_A_LAYERS, D_MODEL, A_IN), D_MODEL)
    a_conv = dense((N_A_LAYERS, CONV_K, 3 * A_WIDTH), CONV_K)
    a_A_log = jnp.log(jax.random.uniform(next(ks), (N_A_LAYERS, A_HEADS), f32, 1.0, 16.0))
    dt = jnp.exp(jax.random.uniform(next(ks), (N_A_LAYERS, A_HEADS), f32,
                                    math.log(1e-3), math.log(1e-1)))
    a_dt_bias = dt + jnp.log(-jnp.expm1(-dt))
    a_out_norm = gain((N_A_LAYERS, A_HEAD_DIM))

    b_w_in = dense((N_B_LAYERS, D_MODEL, B_IN), D_MODEL)
    b_q_norm = gain((N_B_LAYERS, Q_LORA))
    b_w_uq = dense((N_B_LAYERS, Q_LORA, B_HEADS * (QK_NOPE + QK_ROPE)), Q_LORA)

    kv_in_norm = gain((D_MODEL,))
    w_dkv = dense((D_MODEL, KV_LORA + QK_ROPE), D_MODEL)
    kv_lat_norm = gain((KV_LORA,))
    w_ukv = dense((KV_LORA, B_HEADS * (QK_NOPE + V_HEAD)), KV_LORA)
    final_norm = gain((D_MODEL,))

    return {"x": x, "mem": mem, "positions": positions,
            "ffn1_norm": ffn1_norm, "ffn1_w_gu": ffn1_w_gu, "ffn1_w_down": ffn1_w_down,
            "mix_norm": mix_norm,
            "ffn2_norm": ffn2_norm, "ffn2_w_gu": ffn2_w_gu, "ffn2_w_down": ffn2_w_down,
            "w_out": w_out, "mem_norm": mem_norm, "w_mem_kv": w_mem_kv,
            "a_w_in": a_w_in, "a_conv": a_conv, "a_A_log": a_A_log, "a_dt_bias": a_dt_bias,
            "a_out_norm": a_out_norm,
            "b_w_in": b_w_in, "b_q_norm": b_q_norm, "b_w_uq": b_w_uq,
            "kv_in_norm": kv_in_norm, "w_dkv": w_dkv, "kv_lat_norm": kv_lat_norm, "w_ukv": w_ukv,
            "final_norm": final_norm}

def first_block(x, mem, positions, ffn1_norm, ffn1_w_gu, ffn1_w_down, mix_norm,
              ffn2_norm, ffn2_w_gu, ffn2_w_down, w_out, mem_norm, w_mem_kv,
              a_w_in, a_conv, a_A_log, a_dt_bias, a_out_norm,
              b_w_in, b_q_norm, b_w_uq, kv_in_norm, w_dkv, kv_lat_norm, w_ukv, final_norm):
    b, s, _ = x.shape
    mem_n = rms_norm(mem, mem_norm)
    cos, sin = rope_tables(positions, QK_ROPE)

    for i in range(N_A_LAYERS):
        l = i
        x = x + 0.5 * swiglu(rms_norm(x, ffn1_norm[l]), ffn1_w_gu[l], ffn1_w_down[l])
        h = rms_norm(x, mix_norm[l]) @ a_w_in[i]
        qkv, gate, b_raw, a_raw, q_mem = jnp.split(
            h, [3 * A_WIDTH, 4 * A_WIDTH, 4 * A_WIDTH + A_HEADS, 4 * A_WIDTH + 2 * A_HEADS], axis=-1)
        o_a = gated_deltanet(qkv, gate, b_raw, a_raw, a_conv[i], a_A_log[i], a_dt_bias[i], a_out_norm[i])
        o_m = memory_attention(q_mem, mem_n @ w_mem_kv[l])
        x = x + jnp.concatenate([o_a, o_m], axis=-1) @ w_out[l]
        x = x + 0.5 * swiglu(rms_norm(x, ffn2_norm[l]), ffn2_w_gu[l], ffn2_w_down[l])

    ckr = rms_norm(x, kv_in_norm) @ w_dkv
    c_kv = rms_norm(ckr[..., :KV_LORA], kv_lat_norm)
    k_rope = apply_rope(ckr[..., None, KV_LORA:], cos, sin)[:, :, 0]
    k_nope, v_mla = jnp.split((c_kv @ w_ukv).reshape(b, s, B_HEADS, QK_NOPE + V_HEAD), [QK_NOPE], axis=-1)

    for j in range(N_B_LAYERS):
        l = N_A_LAYERS + j
        x = x + 0.5 * swiglu(rms_norm(x, ffn1_norm[l]), ffn1_w_gu[l], ffn1_w_down[l])
        h = rms_norm(x, mix_norm[l]) @ b_w_in[j]
        cq, q_mem = jnp.split(h, [Q_LORA], axis=-1)
        q = (rms_norm(cq, b_q_norm[j]) @ b_w_uq[j]).reshape(b, s, B_HEADS, QK_NOPE + QK_ROPE)
        q_nope, q_rope = jnp.split(q, [QK_NOPE], axis=-1)
        q_rope = apply_rope(q_rope, cos, sin)
        o_b = mla_attention(q_nope, q_rope, k_nope, k_rope, v_mla)
        o_m = memory_attention(q_mem, mem_n @ w_mem_kv[l])
        x = x + jnp.concatenate([o_b, o_m], axis=-1) @ w_out[l]
        x = x + 0.5 * swiglu(rms_norm(x, ffn2_norm[l]), ffn2_w_gu[l], ffn2_w_down[l])

    return rms_norm(x, final_norm)


DEPTH_2 = 1

D_MIX = D_MODEL
W_POOL = D_MIX // 4
W_SCONV = D_MIX // 4
W_CONF = D_MIX // 4
W_ATTN = D_MIX // 4
POOL_WINDOWS = (2, 4, 8, 16)
N_POOL_GROUPS = len(POOL_WINDOWS)
POOL_GROUP = W_POOL // N_POOL_GROUPS
SCONV_K = 3
CONF_K = 31
N_HEADS = 4
HEAD_V = W_ATTN // N_HEADS
HEAD_QK = HEAD_V // 2
SPLIT_SIZES = (W_POOL, W_SCONV, W_SCONV, W_SCONV, W_CONF, W_CONF, W_ATTN, W_ATTN, W_ATTN)
D_IN = sum(SPLIT_SIZES)
D_FF_2 = ((8 * D_MODEL + 3 * 256 - 1) // (3 * 256)) * 256
REL_BUCKETS = 32
REL_MAX_EXACT = REL_BUCKETS // 2
REL_MAX_DIST = 128
NEG_INF = -1e30


def rms_norm_2(x, g):
    xf = x.astype(jnp.float32)
    y = xf * lax.rsqrt(jnp.mean(xf * xf, axis=-1, keepdims=True) + EPS)
    return (y * g.astype(jnp.float32)).astype(x.dtype)

def layer_norm(x, g, b):
    xf = x.astype(jnp.float32)
    mu = jnp.mean(xf, axis=-1, keepdims=True)
    xc = xf - mu
    y = xc * lax.rsqrt(jnp.mean(xc * xc, axis=-1, keepdims=True) + EPS)
    return (y * g.astype(jnp.float32) + b.astype(jnp.float32)).astype(x.dtype)

def causal_dwconv(u, w):
    k = w.shape[0]
    return lax.conv_general_dilated(
        u, w[:, None, :].astype(u.dtype), window_strides=(1,), padding=[(k - 1, 0)],
        dimension_numbers=('NWC', 'WIO', 'NWC'), feature_group_count=u.shape[-1])

def pool_mixer(u, pool_w, pool_scale):
    b, s, _ = u.shape
    c = jnp.cumsum(u.astype(jnp.float32), axis=1)
    pos1 = jnp.arange(1, s + 1)
    parts = []
    for g, win in enumerate(POOL_WINDOWS):
        cg = c[..., g * POOL_GROUP:(g + 1) * POOL_GROUP]
        shifted = jnp.pad(cg, ((0, 0), (win, 0), (0, 0)))[:, :s]
        cnt = jnp.minimum(pos1, win).astype(jnp.float32)[:, None]
        parts.append((cg - shifted) / cnt)
    pooled = jnp.concatenate(parts, axis=-1).astype(u.dtype) - u
    y = jnp.einsum('bsgc,gcd->bsgd', pooled.reshape(b, s, N_POOL_GROUPS, POOL_GROUP), pool_w)
    return y.reshape(b, s, W_POOL) * pool_scale

def rel_bucket(n):
    nf = jnp.maximum(n, 1).astype(jnp.float32)
    large = REL_MAX_EXACT + (jnp.log(nf / REL_MAX_EXACT) / math.log(REL_MAX_DIST / REL_MAX_EXACT)
                             * (REL_BUCKETS - REL_MAX_EXACT)).astype(jnp.int32)
    large = jnp.minimum(large, REL_BUCKETS - 1)
    return jnp.where(n < REL_MAX_EXACT, n, large)

def diff_attention(q, k, v, q_norm_g, k_norm_g, lam, lam_init, subln_g, rel_bias):
    b, s = q.shape[:2]
    q = rms_norm_2(q, q_norm_g)
    k = rms_norm_2(k, k_norm_g)
    scale = HEAD_QK ** -0.5
    nb = s // Q_BLOCK
    qb = q.reshape(b, nb, Q_BLOCK, N_HEADS, 2, HEAD_QK).transpose(1, 0, 2, 3, 4, 5)
    starts = jnp.arange(nb, dtype=jnp.int32) * Q_BLOCK
    kpos = jnp.arange(s, dtype=jnp.int32)

    def block(args):
        qblk, start = args
        qpos = start + jnp.arange(Q_BLOCK, dtype=jnp.int32)
        dist = qpos[:, None] - kpos[None, :]
        bias = rel_bias[rel_bucket(jnp.maximum(dist, 0))].astype(jnp.float32)
        bias = bias.transpose(2, 0, 1)[:, None]
        sc = jnp.einsum('bqhmd,bkhmd->bhmqk', qblk, k).astype(jnp.float32) * scale + bias
        sc = jnp.where(dist >= 0, sc, NEG_INF)
        p = jax.nn.softmax(sc, axis=-1)
        a = p[:, :, 0] - lam * p[:, :, 1]
        return jnp.einsum('bhqk,bkhd->bqhd', a.astype(v.dtype), v)

    o = lax.map(block, (qb, starts))
    o = o.transpose(1, 0, 2, 3, 4).reshape(b, s, N_HEADS, HEAD_V)
    o = rms_norm_2(o, subln_g) * (1.0 - lam_init)
    return o.reshape(b, s, W_ATTN)

def hybrid_layer(x, norm1_g, w_in, pool_w, pool_scale, sconv_w, conf_dw_w, conf_dw_b,
                 conf_ln_g, conf_ln_b, q_norm_g, k_norm_g, lam_q1, lam_k1, lam_q2, lam_k2,
                 subln_g, w_out, norm2_g, w_gate, w_up, w_down, rel_bias, lam_init):
    b, s, _ = x.shape
    h = rms_norm_2(x, norm1_g)
    z = h @ w_in
    idx = [int(i) for i in np.cumsum(SPLIT_SIZES)[:-1]]
    z_pool, s_b, s_c, s_h, c_a, c_g, zq, zk, zv = jnp.split(z, idx, axis=-1)
    y_pool = pool_mixer(z_pool, pool_w, pool_scale)
    y_sconv = s_b * causal_dwconv(s_c * s_h, sconv_w)
    u = c_a * jax.nn.sigmoid(c_g)
    u = causal_dwconv(u, conf_dw_w) + conf_dw_b
    y_conf = jax.nn.silu(layer_norm(u, conf_ln_g, conf_ln_b))
    lam = (jnp.exp(jnp.sum(lam_q1.astype(jnp.float32) * lam_k1.astype(jnp.float32)))
           - jnp.exp(jnp.sum(lam_q2.astype(jnp.float32) * lam_k2.astype(jnp.float32))) + lam_init)
    q = zq.reshape(b, s, N_HEADS, 2, HEAD_QK)
    k = zk.reshape(b, s, N_HEADS, 2, HEAD_QK)
    v = zv.reshape(b, s, N_HEADS, HEAD_V)
    y_attn = diff_attention(q, k, v, q_norm_g, k_norm_g, lam, lam_init, subln_g, rel_bias)
    mix = jnp.concatenate([y_pool, y_sconv, y_conf, y_attn], axis=-1)
    x = x + mix @ w_out
    h2 = rms_norm_2(x, norm2_g)
    x = x + (jax.nn.silu(h2 @ w_gate) * (h2 @ w_up)) @ w_down
    return x

def second_inputs(seed: int = 0) -> dict:
    key = jax.random.key(seed)
    ks = jax.random.split(key, 24)
    f32 = jnp.float32
    nrm = lambda k, shape, sc: jax.random.normal(k, shape, f32) * sc
    L = DEPTH_2
    return {
        'x': nrm(ks[0], (BATCH, SEQ, D_MODEL), 1.0),
        'norm1_g': 1.0 + nrm(ks[1], (L, D_MODEL), 0.05),
        'w_in': nrm(ks[2], (L, D_MODEL, D_IN), D_MODEL ** -0.5),
        'pool_w': nrm(ks[3], (L, N_POOL_GROUPS, POOL_GROUP, POOL_GROUP), POOL_GROUP ** -0.5),
        'pool_scale': 1.0 + nrm(ks[4], (L, W_POOL), 0.1),
        'sconv_w': nrm(ks[5], (L, SCONV_K, W_SCONV), SCONV_K ** -0.5),
        'conf_dw_w': nrm(ks[6], (L, CONF_K, W_CONF), CONF_K ** -0.5),
        'conf_dw_b': nrm(ks[7], (L, W_CONF), 0.02),
        'conf_ln_g': 1.0 + nrm(ks[8], (L, W_CONF), 0.05),
        'conf_ln_b': nrm(ks[9], (L, W_CONF), 0.02),
        'q_norm_g': 1.0 + nrm(ks[10], (L, HEAD_QK), 0.05),
        'k_norm_g': 1.0 + nrm(ks[11], (L, HEAD_QK), 0.05),
        'lam_q1': nrm(ks[12], (L, HEAD_QK), 0.1),
        'lam_k1': nrm(ks[13], (L, HEAD_QK), 0.1),
        'lam_q2': nrm(ks[14], (L, HEAD_QK), 0.1),
        'lam_k2': nrm(ks[15], (L, HEAD_QK), 0.1),
        'subln_g': 1.0 + nrm(ks[16], (L, HEAD_V), 0.05),
        'w_out': nrm(ks[17], (L, D_MIX, D_MODEL), D_MIX ** -0.5),
        'norm2_g': 1.0 + nrm(ks[18], (L, D_MODEL), 0.05),
        'w_gate': nrm(ks[19], (L, D_MODEL, D_FF_2), D_MODEL ** -0.5),
        'w_up': nrm(ks[20], (L, D_MODEL, D_FF_2), D_MODEL ** -0.5),
        'w_down': nrm(ks[21], (L, D_FF_2, D_MODEL), D_FF_2 ** -0.5),
        'rel_bias': nrm(ks[22], (REL_BUCKETS, N_HEADS), 0.5),
    }

def second_block(x, norm1_g, w_in, pool_w, pool_scale, sconv_w, conf_dw_w, conf_dw_b, conf_ln_g,
              conf_ln_b, q_norm_g, k_norm_g, lam_q1, lam_k1, lam_q2, lam_k2, subln_g, w_out,
              norm2_g, w_gate, w_up, w_down, rel_bias):
    for l in range(DEPTH_2):
        lam_init = 0.8 - 0.6 * math.exp(-0.3 * l)
        x = hybrid_layer(x, norm1_g[l], w_in[l], pool_w[l], pool_scale[l], sconv_w[l],
                         conf_dw_w[l], conf_dw_b[l], conf_ln_g[l], conf_ln_b[l], q_norm_g[l],
                         k_norm_g[l], lam_q1[l], lam_k1[l], lam_q2[l], lam_k2[l], subln_g[l],
                         w_out[l], norm2_g[l], w_gate[l], w_up[l], w_down[l], rel_bias, lam_init)
    return x


def setup_inputs(seed=0):
    out = dict(first_inputs(seed))
    for name, value in second_inputs(seed + 1).items():
        if name != "x":
            out[name + "_2"] = value
    return out


def reference(
    x, mem, positions, ffn1_norm, ffn1_w_gu, ffn1_w_down, mix_norm, ffn2_norm, ffn2_w_gu,
    ffn2_w_down, w_out, mem_norm, w_mem_kv, a_w_in, a_conv, a_A_log, a_dt_bias, a_out_norm,
    b_w_in, b_q_norm, b_w_uq, kv_in_norm, w_dkv, kv_lat_norm, w_ukv, final_norm, norm1_g_2,
    w_in_2, pool_w_2, pool_scale_2, sconv_w_2, conf_dw_w_2, conf_dw_b_2, conf_ln_g_2,
    conf_ln_b_2, q_norm_g_2, k_norm_g_2, lam_q1_2, lam_k1_2, lam_q2_2, lam_k2_2, subln_g_2,
    w_out_2, norm2_g_2, w_gate_2, w_up_2, w_down_2, rel_bias_2,
):
    x = first_block(
        x, mem, positions, ffn1_norm, ffn1_w_gu, ffn1_w_down, mix_norm, ffn2_norm, ffn2_w_gu,
        ffn2_w_down, w_out, mem_norm, w_mem_kv, a_w_in, a_conv, a_A_log, a_dt_bias, a_out_norm,
        b_w_in, b_q_norm, b_w_uq, kv_in_norm, w_dkv, kv_lat_norm, w_ukv, final_norm,
    )
    return second_block(
        x, norm1_g_2, w_in_2, pool_w_2, pool_scale_2, sconv_w_2, conf_dw_w_2, conf_dw_b_2,
        conf_ln_g_2, conf_ln_b_2, q_norm_g_2, k_norm_g_2, lam_q1_2, lam_k1_2, lam_q2_2,
        lam_k2_2, subln_g_2, w_out_2, norm2_g_2, w_gate_2, w_up_2, w_down_2, rel_bias_2,
    )


_drawn_inputs = setup_inputs


def setup_inputs(seed=0):
    import zlib

    import numpy as np

    out = dict(_drawn_inputs(seed))
    spreads = {}
    factors = {'ffn1_norm': 3.597,
     'ffn2_norm': 4.316,
     'mem_norm': 8.0,
     'a_out_norm': 4.748,
     'b_q_norm': 8.0,
     'kv_in_norm': 8.0,
     'kv_lat_norm': 8.0,
     'conf_dw_b_2': 5.305,
     'conf_ln_g_2': 3.932,
     'conf_ln_b_2': 8.0,
     'q_norm_g_2': 4.413,
     'k_norm_g_2': 4.621,
     'lam_q2_2': 2.791,
     'lam_k2_2': 8.0,
     'subln_g_2': 3.512,
     'pool_scale_2': 2.743,
     'norm2_g_2': 3.075}
    for name, (base, spread) in spreads.items():
        noise = np.random.default_rng([zlib.crc32(name.encode()), seed]).standard_normal(out[name].shape)
        drawn = base * np.exp(spread * noise) if base else spread * noise
        out[name] = __import__('jax').numpy.asarray(drawn.astype(out[name].dtype))
    for name, factor in factors.items():
        out[name] = (out[name] * factor).astype(out[name].dtype)
    return out
```

```python
import concourse.bass as bass
from concourse import mybir
from contextlib import ExitStack

P = 128
SEQ = 256
TB = SEQ // P
D = 1024
KB = D // P
FF = 2816
CW = 256
STEPS = FF // CW
TILE = KB * CW
RING = 3
EPS = 1e-6
NEG = -1e30
CHUNK = 64
NCHUNK = SEQ // CHUNK
AH = 6
BH = 6
MH = 4
LEVELS = 6
ROPE = 64
LAM_INIT = 0.2
TWO_PI = (6.28125, 0.0019350051879882812, 3.0199159819e-07)
ROUND = 12582912.0

PARAMS = [("ffn1_norm0", 8), ("ffn1_norm1", 8), ("ffn2_norm0", 8), ("ffn2_norm1", 8), ("mix_norm0", 8),
          ("mix_norm1", 8), ("mem_norm", 8), ("kv_in_norm", 8), ("final_norm", 8), ("norm1_2", 8),
          ("norm2_2", 8), ("b_q_norm", 2), ("kv_lat_norm", 2), ("a_out_norm", 1), ("a_conv", 72),
          ("pool_scale", 2), ("sconv", 6), ("conf_w", 62), ("conf_b", 2), ("ln_g", 2), ("ln_b", 2),
          ("q_g", 1), ("k_g", 1), ("subln", 1), ("A_log", 6), ("dt_bias", 6), ("lam", 128), ("pool_w", 256)]
CONSTS = [("ident", 128), ("ones", 128), ("seg32", 128), ("seg64", 128), ("swap", 128), ("tri", 128),
          ("after", 128), ("level", LEVELS * 128), ("half", 1), ("inv_win", 2), ("inv_cnt", 32),
          ("inv_freq", 1), ("mla_mask", 512)]

SEMS = """inputs_loaded w_loaded0 w_loaded1 w_loaded2 w_hi w_split tile_used
x_ready norm_sq norm_ms norm_sd t8_ready hi_ready act_ready zeros_ready pads_ready
act_step dve_step pool_step pe_step
mem_evac sg_ready glu_free h_hi h_ready
out_evac ain_evac conv_done silu_done l2_sq l2_sum l2_sd qk_ready
g_exp1 g_dve1 g_act2 beta_ready decay_g_ready gcol_ps rows_ps gcol_sb rows_sb
kb_ready d_pre d_exp d_ready kkt_ps lt_ready qkt_ps qd_ready tok_ps vb_ready kdec_ready
lvl_m lvl_p1 lvl_p1sb lvl_z lvl_x lvl_zt lvl_xt lvl_init vn_zeroed qm_ready pos_loaded att_done table_loaded scaled
ks_ps r_ready vn_ps vn_sb su_ps s_ready o_ps o_sb o_sq o_sum o_sd delta_done
att_s att_nm att_e att_p att_t att_pt att_o att_oe
lat_ps lat_sb lat_sq lat_sum lat_sd lat_f lat_hi lat_ready rope_in rope_ps rope_done
rope_ang rope_tab ukv_ps ukv_evac uq_ps uq_evac
in2_evac pooled_ready pool_ps conf_ready conf_mean_ps conf_mean conf_xc conf_sq conf_var_ps conf_sd conf_y conf_out
qk2_sq qk2_ps qk2_sd qk2_ready lam_prod lam_exp bias_ps bias_row bias_dma bias_ready
sub_sq sub_ps sub_sd out_done""".split()


def columns(table):
    at, where = 0, {}
    for name, width in table:
        where[name] = (at, at + width)
        at += width
    return where, at


PHASES = [("mem", 4), ("ffn0", 33), ("ain", 14), ("out0", 4), ("ffn1", 33), ("dkv", 2), ("ukv", 2),
          ("ffn2", 33), ("bin", 2), ("uq", 2), ("out1", 4), ("ffn3", 33), ("in2", 9), ("out2", 4), ("ffn4", 33)]
VERSIONS = ["mem", "ffn0", "ain", "out0", "ffn1", "dkv", "ffn2", "bin", "out1", "ffn3", "in2", "out2", "ffn4"]
NORMS = ["mem", "ffn0", "ain", "ffn1", "dkv", "ffn2", "bin", "ffn3", "final", "in2", "ffn4"]
NORM_GAIN = ["mem_norm", "ffn1_norm0", "mix_norm0", "ffn2_norm0", "kv_in_norm", "ffn1_norm1", "mix_norm1",
             "ffn2_norm1", "final_norm", "norm1_2", "norm2_2"]
IN2_ORDER = [4, 5, 0, 1, 2, 3, 6, 7, 8]
ATT = [("mem0", "mem", MH), ("mem1", "mem", MH), ("mla", "mla", BH), ("diff", "diff", MH)]


def program(nc, d, out):
    f32, f32r, bf16, i32 = mybir.dt.float32, mybir.dt.float32r, mybir.dt.bfloat16, mybir.dt.int32
    ACT, ALU, AX = mybir.ActivationFunctionType, mybir.AluOpType, mybir.AxisListType
    PC, n_par = columns(PARAMS)
    CC, n_con = columns(CONSTS)
    tile0, n_tiles = {}, 0
    for name, n in PHASES:
        tile0[name] = n_tiles
        n_tiles += n
    version = {name: v for v, name in enumerate(VERSIONS)}
    norm_no = {name: k for k, name in enumerate(NORMS)}
    free_at = {}
    ends = {name: tile0[name] + n for name, n in PHASES}
    for before, name in zip(VERSIONS, VERSIONS[1:]):
        free_at[name] = ends[before]

    ROW = MH * 2 * SEQ
    bias_rows = nc.dram_tensor("bias_rows", [P * (ROW + 1)], f32, kind="Internal")

    with ExitStack() as ctx:
        enter = ctx.enter_context

        def sb(name, shape, dt=f32):
            return enter(nc.sbuf_tensor(name, shape, dt))

        S = {n: enter(nc.semaphore(n)) for n in SEMS}
        w_loaded = [S["w_loaded0"], S["w_loaded1"], S["w_loaded2"]]

        RAW = sb("w_raw", [P, RING, TILE])
        WH = sb("w_hi_part", [P, RING, TILE], f32r)
        WL = sb("w_lo_part", [P, RING, TILE], f32r)
        X = sb("x_res", [P, KB, SEQ])
        T8 = sb("t8", [P, KB, SEQ])
        XH = sb("x_hi", [P, KB, SEQ], f32r)
        XL = sb("x_lo", [P, KB, SEQ], f32r)
        HH = sb("h_hi_part", [P, 4, SEQ], f32r)
        HL = sb("h_lo_part", [P, 4, SEQ], f32r)
        PAR = sb("params", [P, n_par])
        CON = sb("consts", [P, n_con])
        ZB = sb("zeros_bf", [P, 512], bf16)
        SD = sb("norm_dev", [P, SEQ])
        RS = sb("norm_rs", [P, SEQ])
        KM = [sb(f"mem_k{l}", [P, 2, SEQ]) for l in range(2)]
        VM2 = [sb(f"mem_v{l}", [P, TB, 2 * P]) for l in range(2)]
        QM = sb("mem_q", [P, 2, SEQ])
        SMALL = sb("small", [P, 128])
        ATTS = sb("att_small", [P, 64])
        LAMP = sb("lam_products", [P, 2, 32])
        RELB = sb("rel_bias", [32, MH])
        AR_N = 17 * 1024
        AR = sb("arena", [P, AR_N])
        PS = enter(nc.psum_tensor("ps", [P, 8, 512], f32))

        def par(name, a=0, n=None):
            lo, hi = PC[name]
            return PAR[:, lo + a:(hi if n is None else lo + a + n)]

        def con(name, a=0, n=None):
            lo, hi = CC[name]
            return CON[:, lo + a:(hi if n is None else lo + a + n)]

        def area(at, *dims):
            n = 1
            for x in dims:
                n *= x
            assert at + n <= AR_N, (at, dims)
            v = AR[:, at:at + n]
            if len(dims) == 2:
                v = v.rearrange("p (a b) -> p a b", b=dims[1])
            if len(dims) == 3:
                v = v.rearrange("p (a b c) -> p a b c", b=dims[1], c=dims[2])
            return v

        def bank(b, w=512):
            return PS[:, b, 0:w]

        def pairs(v):
            return v.rearrange("p (a b) -> p a b", b=SEQ)

        def over(v, n):
            return v.unsqueeze(1).broadcast_to([v.shape[0], n, v.shape[1]])

        U = AH * SEQ
        MEMT = area(0, KB, SEQ)
        SG = area(0, 2, SEQ)
        HF = area(2 * SEQ, 2, SEQ)
        PAD = 3
        YQKV = area(0, 18, SEQ)
        Yq, Yk, Yv = (area(i * U, AH, SEQ) for i in range(3))
        CB = area(3 * U, 18, SEQ + PAD)
        KBT = area(3 * U, AH, SEQ)
        GROW = area(4 * U, AH, SEQ)
        EGROW = area(5 * U, AH, SEQ)
        SPLIT0 = 3 * U + 18 * (SEQ + PAD) + 10
        QKS = area(SPLIT0, 12, SEQ)
        VB = area(SPLIT0, TB, AH, P)
        KD = area(SPLIT0 + U, TB, AH, P)
        LT = area(SPLIT0 + 2 * U, TB * AH, P)
        XT = area(SPLIT0 + 3 * U, TB * AH, P)
        MT = area(SPLIT0 + 4 * U, TB * AH, P)
        DT = area(2 * U, TB * AH, P)
        QD = area(4 * U, TB * AH, P)
        XM = area(U, TB * AH, P)
        P1 = area(2 * U, TB * AH, P)
        ST = area(U, AH, P)
        RR = area(U + AH * P, AH, P)
        VN = [area(SPLIT0 + 4 * U + h * AH * P, AH, P) for h in range(2)]
        OB = area(2 * U, AH, SEQ)
        OSQ = area(SPLIT0 + 2 * U, AH, SEQ)
        OSD = area(SPLIT0 + 3 * U, AH, SEQ)
        KN = area(4 * SEQ, BH, SEQ)
        VM = area(4 * SEQ + U, TB, BH, P)
        KR = area(4 * SEQ + 2 * U, SEQ)
        COS = area(5 * SEQ + 2 * U, SEQ)
        SIN = area(6 * SEQ + 2 * U, SEQ)
        LATE = 7 * SEQ + 2 * U
        LAT = area(LATE, 2, SEQ)
        LSQ = area(LATE + 2 * SEQ, 2, SEQ)
        QQ = area(LATE + 4 * SEQ, BH, 2, SEQ)
        ROT = area(LATE + 4 * SEQ + 2 * U, BH, SEQ)
        UP = area(0, 2, SEQ + 16)
        S2 = area(544, 2, SEQ + 16)
        S4 = area(1088, 2, SEQ + 16)
        S8 = area(1632, 2, SEQ + 16)
        PL = area(2176, 2, SEQ)
        SB_, SC_, SH_, CA_, CG_ = (area(2688 + 512 * i, 2, SEQ) for i in range(5))
        CS = area(5248, 2, SEQ + 2)
        CC_ = area(5764, 2, SEQ + 30)
        CV = area(6336, 2, SEQ)
        ZQ = area(6848, 4, SEQ)
        ZS = area(7872, 4, SEQ)
        ZV = area(8896, TB, 2 * P)
        XC = area(9408, 2, SEQ)
        CVS = area(9920, 2, SEQ)
        MN = area(10432, SEQ)
        BIAS = area(10688, TB, MH, SEQ)
        TABLE = area(10688, 2 * 2 * SEQ)
        BROW = area(11712, MH, 2 * SEQ)
        ATT_AT = {"mem0": 0, "mem1": LATE + 4 * SEQ + 3 * U, "mla": LATE + 4 * SEQ + 3 * U, "diff": 12736}

        def att_work(phase):
            at = ATT_AT[phase]
            sc = [[area(at + (2 * q + m) * 512, 2, SEQ) for m in range(2)] for q in range(2)]
            pt = [area(at + 2048 + q * 512, 2, SEQ) for q in range(2)]
            return sc, pt

        def loops_of(name):
            return (STEPS - 1) // 2 - (tile0[name] + 33 == n_tiles)

        def ffn_scale(name):
            return 1.0 if name == "ffn4" else 0.5

        BA = SMALL[:, 0:24].rearrange("p (a b) -> p a b", a=TB)
        BETA, GG, G1, G2, GC, ED = (SMALL[:, 24 + 12 * k:36 + 12 * k].rearrange("p (a b) -> p a b", a=TB) for k in range(6))
        EA = SMALL[:, 96:102]
        LAMS, LAM2, NLAM = SMALL[:, 104:106], SMALL[:, 106:108], SMALL[:, 108:109]
        POSI = area(LATE + 4 * SEQ, SEQ).bitcast(i32)
        ANG, TURN, ANG_S, ANG_C = (area(LATE + 5 * SEQ + k * SEQ, SEQ) for k in range(4))
        PI, PI_IN = 3.141592653589793, 3.1415925
        MEM_SCALE, MLA_SCALE, DIFF_SCALE = 64 ** -0.5, (P + ROPE) ** -0.5, 32 ** -0.5

        def stat(k, u, m):
            at = 16 * k + 8 * (u % 2) + 4 * m
            return ATTS[:, at:at + TB]

        def MX(u, m):
            return stat(0, u, m)

        def NM2(u, m):
            return stat(1, u, m)

        def NM(u, m, q):
            return stat(1, u, m)[:, q:q + 1]

        def SUM2(u, m):
            return stat(2, u, m)

        def SUM(u, m, q):
            return stat(2, u, m)[:, q:q + 1]

        def RC2(u, m):
            return stat(3, u, m)

        def RC(u, m, q):
            return stat(3, u, m)[:, q:q + 1]

        att0, att_of, u, m, g = {}, {}, 0, 0, 0
        for ph, kind, n in ATT:
            att0[ph], att_of[ph] = (u, m, g), (kind, n)
            u, m, g = u + n, m + n * (2 if kind == "diff" else 1), g + (n if kind == "mla" else n // 2)

        def matmul3(o, w_hi, w_lo, a_hi, a_lo, start, stop):
            nc.tensor.matmul(o, w_hi, a_hi, start=start, stop=False, skip_group_check=True)
            nc.tensor.matmul(o, w_hi, a_lo, start=False, stop=False, skip_group_check=True)
            return nc.tensor.matmul(o, w_lo, a_hi, start=False, stop=stop, skip_group_check=True)

        def width(n):
            if n == tile0["ain"]:
                return KB * 2 * AH
            if n == tile0["dkv"] + 1:
                return KB * P
            if tile0["ukv"] <= n < tile0["ukv"] + 2 or tile0["uq"] <= n < tile0["uq"] + 2:
                return 2 * 768
            return TILE

        block = enter(nc.Block())

        def phase(name):
            return tile0[name]

        @block.sync
        def _(sp):
            def slot_free(n, more=0):
                if n >= RING:
                    sp.wait_ge(S["w_split"], n - RING + 1 + more)

            def load(n, src, kb, cols):
                slot_free(n)
                dst = RAW[:, n % RING, 0:kb * cols].rearrange("p (k c) -> p k c", c=cols)
                sp.dma_start(dst, src).then_inc(w_loaded[n % RING], 16)

            def wide(w):
                return w.rearrange("(k p) n -> p k n", p=P)

            def load_columns(n0, w, start, count):
                v = wide(w)
                for t in range(count):
                    load(n0 + t, v[:, :, start + t * CW:start + (t + 1) * CW], KB, CW)

            def load_ffn(name, w_gate, gate_at, w_up, up_at, w_down):
                n0 = tile0[name]
                wg, wu = wide(w_gate), wide(w_up)
                wd = w_down.rearrange("(s j p) n -> s p j n", j=2, p=P)
                load(n0, wg[:, :, gate_at:gate_at + CW], KB, CW)
                load(n0 + 1, wu[:, :, up_at:up_at + CW], KB, CW)
                with nc.sync.Fori(0, (STEPS - 1) // 2) as i:
                    for j in range(2):
                        n = n0 + 2 + 3 * j
                        at = i * (2 * CW) + (j + 1) * CW
                        for k in range(3):
                            m = n + k
                            slot_free(m, i * 6)
                            dst = RAW[:, m % RING, :]
                            if k < 2:
                                src = (wg, wu)[k][:, :, bass.ds(at + (gate_at, up_at)[k], CW)]
                                dst = dst.rearrange("p (k c) -> p k c", c=CW)
                            else:
                                src = wd[bass.ds(i * 2 + j, 1), :, :, :].rearrange("s p j n -> p (s j) n")
                                dst = dst.rearrange("p (k c) -> p k c", c=D)
                            sp.dma_start(dst, src).then_inc(w_loaded[m % RING], 16)
                load(n0 + 32, wd[STEPS - 1], 2, D)

            for l in range(2):
                load_columns(2 * l, d["w_mem_kv"][l], 0, 2)
            load_ffn("ffn0", d["ffn1_w_gu"][0], 0, d["ffn1_w_gu"][0], FF, d["ffn1_w_down"][0])
            n = tile0["ain"]
            w = d["a_w_in"][0]
            load(n, wide(w)[:, :, 4 * AH * P:4 * AH * P + 2 * AH], KB, 2 * AH)
            load_columns(n + 1, w, 0, 12)
            load_columns(n + 13, w, 4 * AH * P + 2 * AH, 1)
            load_columns(tile0["out0"], d["w_out"][0], 0, 4)
            load_ffn("ffn1", d["ffn2_w_gu"][0], 0, d["ffn2_w_gu"][0], FF, d["ffn2_w_down"][0])
            load_columns(tile0["dkv"], d["w_dkv"], 0, 1)
            load(tile0["dkv"] + 1, wide(d["w_dkv"])[:, :, CW:CW + P], KB, P)
            for t in range(2):
                load(tile0["ukv"] + t, wide(d["w_ukv"])[:, :, t * 768:(t + 1) * 768], 2, 768)
            load_ffn("ffn2", d["ffn1_w_gu"][1], 0, d["ffn1_w_gu"][1], FF, d["ffn1_w_down"][1])
            load_columns(tile0["bin"], d["b_w_in"][0], 0, 2)
            for t in range(2):
                load(tile0["uq"] + t, wide(d["b_w_uq"])[:, :, t * 768:(t + 1) * 768], 2, 768)
            load_columns(tile0["out1"], d["w_out"][1], 0, 4)
            load_ffn("ffn3", d["ffn2_w_gu"][1], 0, d["ffn2_w_gu"][1], FF, d["ffn2_w_down"][1])
            for t, part in enumerate(IN2_ORDER):
                load(tile0["in2"] + t, wide(d["w_in_2"][0])[:, :, part * CW:(part + 1) * CW], KB, CW)
            load_columns(tile0["out2"], d["w_out_2"][0], 0, 4)
            load_ffn("ffn4", d["w_gate_2"][0], 0, d["w_up_2"][0], 0, d["w_down_2"][0])
            for p in range(4):
                sp.wait_ge(S["x_ready"], 4 * len(NORMS) + p + 1)
                sp.dma_start(out.rearrange("(k p) t -> p k t", p=P)[:, 2 * p:2 * p + 2, :],
                             X[:, 2 * p:2 * p + 2, :]).then_inc(S["out_done"], 16)
            sp.wait_ge(S["out_done"], 64)

        @block.scalar
        def _(act):
            step = [0]

            def link(ins):
                step[0] += 1
                ins.then_inc(S["act_step"], 1)
                act.wait_ge(S["act_step"], step[0])

            def w_hi(n, i=None):
                if n >= n_tiles:
                    return
                turn = 0 if i is None else i * 6
                act.wait_ge(w_loaded[n % RING], 16 * (n // RING + 1) + (0 if i is None else i * 32))
                if n >= RING:
                    act.wait_ge(S["tile_used"], n - RING + 1 + turn)
                w = width(n)
                nc.scalar.activation(WH[:, n % RING, 0:w], RAW[:, n % RING, 0:w], ACT.Copy).then_inc(S["w_hi"], 1)

            def norm(name, src=X):
                k = norm_no[name]
                for p in range(4):
                    act.wait_ge(S["x_ready"], 4 * k + p + 1)
                    nc.scalar.activation(T8[:, 2 * p:2 * p + 2, :], src[:, 2 * p:2 * p + 2, :],
                                         ACT.Square).then_inc(S["norm_sq"], 1)
                act.wait_ge(S["norm_ms"], k + 1)
                nc.scalar.activation(SD[:, :], bank(7, SEQ), ACT.Sqrt, bias=EPS, scale=1.0 / D).then_inc(S["norm_sd"], 1)

            def operand_hi(name):
                v = version[name]
                if v:
                    act.wait_ge(S["tile_used"], free_at[name])
                for p in range(4):
                    act.wait_ge(S["t8_ready"], 4 * v + p + 1)
                    nc.scalar.activation(XH[:, 2 * p:2 * p + 2, :], T8[:, 2 * p:2 * p + 2, :],
                                         ACT.Copy).then_inc(S["hi_ready"], 1)

            def ffn(f, name):
                n0 = tile0[name]

                def gate(s, i=None):
                    more = 0 if i is None else i * 6
                    turn = 0 if i is None else i * 2
                    act.wait_ge(S["tile_used"], n0 + (2 if isinstance(s, int) and s == 0 else 3 * s + 1) + more)
                    nc.scalar.activation(SG, PS[:, 4:6, 0:SEQ], ACT.Silu).then_inc(S["sg_ready"], 1)

                def hidden_hi(s, i=None):
                    turn = 0 if i is None else i * 2
                    act.wait_ge(S["glu_free"], STEPS * f + s + 1 + turn)
                    nc.scalar.activation(HH[:, 2 * (s % 2):2 * (s % 2) + 2, :], HF, ACT.Copy).then_inc(S["h_hi"], 1)

                def one(s, i=None):
                    w_hi(n0 + 3 * s + 2, i)
                    w_hi(n0 + 3 * s + 3, i)
                    gate(s, i)
                    hidden_hi(s, i)
                    w_hi(n0 + 3 * s + 4, i)

                w_hi(n0 + 3)
                gate(0)
                hidden_hi(0)
                w_hi(n0 + 4)
                loops = loops_of(name)
                with nc.scalar.Fori(0, loops) as i:
                    one(1, i)
                    one(2, i)
                for s in range(2 * loops + 1, STEPS):
                    one(s)
                w_hi(n0 + 3 * STEPS + 2)

            def out_linear(name):
                for t in range(4):
                    w_hi(tile0[name] + t + RING)

            def attention(ph):
                u0, m0, g0 = att0[ph]
                kind, n = att_of[ph]
                maps = 2 if kind == "diff" else 1
                sc, pt = att_work(ph)
                for u in range(n + 1):
                    if u < n:
                        for m in range(maps):
                            act.wait_ge(S["att_nm"], m0 + u * maps + m + 1)
                            if u >= 2 and kind == "mem":
                                act.wait_ge(S["att_t"], u0 + u - 1)
                            for q in range(TB):
                                src = PS[:, 2 * (u % 2) + m, q * SEQ:(q + 1) * SEQ] if kind == "mem" else sc[u % 2][m][:, q, :]
                                last = nc.scalar.activation(
                                    sc[u % 2][m][:, q, :], src, ACT.Exp, bias=NM(u, m, q),
                                    scale=(MEM_SCALE if kind == "mem" else 1.0), accum_out=SUM(u, m, q))
                            last.then_inc(S["att_e"], 1)
                    if u >= 1:
                        act.wait_ge(S["att_t"], u0 + u)
                        nc.scalar.activation(pt[(u - 1) % 2], pairs(bank(4 + (u - 1) % 2)), ACT.Copy).then_inc(S["att_pt"], 1)

            def latent(r, n):
                act.wait_ge(S["tile_used"], n + 1)
                nc.scalar.activation(LAT, pairs(bank(0)), ACT.Copy).then_inc(S["lat_sb"], 1)
                nc.scalar.activation(LSQ, pairs(bank(0)), ACT.Square).then_inc(S["lat_sq"], 1)

            def latent_rest(r):
                act.wait_ge(S["lat_sum"], r + 1)
                nc.scalar.activation(SD[:, :], bank(7, SEQ), ACT.Sqrt, bias=EPS, scale=1.0 / (2 * P)).then_inc(S["lat_sd"], 1)
                act.wait_ge(S["lat_f"], r + 1)
                nc.scalar.activation(HH[:, 0:2, :], LAT, ACT.Copy).then_inc(S["lat_hi"], 1)

            act.dma_start(PAR[:, :], d["params"]).then_inc(S["inputs_loaded"], 16)
            act.dma_start(CON[:, :], d["consts"]).then_inc(S["inputs_loaded"], 16)
            act.dma_start(MEMT, d["mem"].rearrange("(k p) t -> p k t", p=P)).then_inc(S["inputs_loaded"], 16)
            act.dma_start(X[:, :, :], d["x"].rearrange("(k p) t -> p k t", p=P)).then_inc(S["inputs_loaded"], 16)
            for n in range(RING):
                w_hi(n)

            norm("mem", MEMT)
            operand_hi("mem")
            for t in range(4):
                act.wait_ge(S["tile_used"], t + 1)
                dst = (KM, VM2)[t % 2][t // 2]
                src = pairs(bank(t))
                nc.scalar.activation(dst[:, :, :], src, ACT.Copy).then_inc(S["mem_evac"], 1)
                w_hi(t + RING)
            norm("ffn0")
            operand_hi("ffn0")
            ffn(0, "ffn0")
            norm("ain")
            operand_hi("ain")

            n0 = tile0["ain"]
            act.wait_ge(S["tile_used"], n0 + 1)
            nc.scalar.activation(BA, PS[:, 6, 0:TB * 2 * AH].rearrange("p (a b) -> p a b", a=TB), ACT.Copy).then_inc(S["g_exp1"], 1)
            w_hi(n0 + RING)

            def silu_block(j):
                act.wait_ge(S["conv_done"], j + 1)
                v = YQKV[:, 2 * j:2 * j + 2, :]
                nc.scalar.activation(v, v, ACT.Silu).then_inc(S["silu_done"], 1)

            for t in range(9):
                act.wait_ge(S["tile_used"], n0 + t + 2)
                if t == 0:
                    act.wait_ge(S["pads_ready"], 1)
                nc.scalar.activation(CB[:, 2 * t:2 * t + 2, PAD:PAD + SEQ], pairs(bank(t % 4)), ACT.Copy).then_inc(S["ain_evac"], 1)
                w_hi(n0 + t + 1 + RING)
                if t:
                    silu_block(t - 1)
            for t in range(9, 12):
                act.wait_ge(S["tile_used"], n0 + t + 2)
                nc.scalar.activation(T8[:, 2 * (t - 9):2 * (t - 9) + 2, :], pairs(bank(t % 4)), ACT.Silu).then_inc(S["ain_evac"], 1)
                w_hi(n0 + t + 1 + RING)
                if t == 9:
                    silu_block(8)
            act.wait_ge(S["tile_used"], n0 + 14)
            nc.scalar.activation(QM[:, :, :], pairs(bank(0)), ACT.Copy).then_inc(S["qm_ready"], 1)
            w_hi(n0 + 13 + RING)
            for j in range(6):
                if j == 0:
                    act.wait_ge(S["silu_done"], 6)
                nc.scalar.activation(QKS[:, 2 * j:2 * j + 2, :], YQKV[:, 2 * j:2 * j + 2, :], ACT.Square).then_inc(S["l2_sq"], 1)
            for j in range(6):
                act.wait_ge(S["l2_sum"], j + 1)
                nc.scalar.activation(QKS[:, 2 * j:2 * j + 2, :], pairs(bank(j)), ACT.Sqrt, bias=EPS).then_inc(S["l2_sd"], 1)
            act.wait_ge(S["g_exp1"], 1)
            nc.scalar.activation(EA, par("A_log"), ACT.Exp)
            nc.scalar.activation(BETA, BA[:, :, 0:AH], ACT.Exp, scale=-1.0)
            act.wait_ge(S["g_dve1"], 1)
            link(nc.scalar.activation(G2, G1, ACT.Abs))
            link(nc.scalar.activation(G2, G2, ACT.Exp, scale=-1.0))
            nc.scalar.activation(G2, G2, ACT.Ln, bias=1.0).then_inc(S["g_act2"], 1)
            act.wait_ge(S["gcol_ps"], 1)
            nc.scalar.activation(GC, PS[:, 6, 64:76].rearrange("p (a b) -> p a b", a=TB), ACT.Copy).then_inc(S["gcol_sb"], 1)
            link(nc.scalar.activation(ED, PS[:, 6, 96:108].rearrange("p (a b) -> p a b", a=TB), ACT.Exp))
            for j in range(3):
                act.wait_ge(S["rows_ps"], j + 1)
                nc.scalar.activation(GROW[:, 2 * j:2 * j + 2, :], pairs(bank(j)), ACT.Copy).then_inc(S["rows_sb"], 1)
                nc.scalar.activation(EGROW[:, 2 * j:2 * j + 2, :], pairs(bank(j)), ACT.Exp).then_inc(S["rows_sb"], 1)
            act.wait_ge(S["tok_ps"], 2)
            for m in range(TB * AH):
                tb, h = divmod(m, AH)
                last = nc.scalar.activation(KD[:, tb, h, :], PS[:, m // 4, (m % 4) * P:(m % 4 + 1) * P], ACT.Copy,
                                            scale=ED[:, tb, h:h + 1])
            last.then_inc(S["kdec_ready"], 1)
            act.wait_ge(S["d_pre"], 1)
            nc.scalar.activation(DT, DT, ACT.Exp).then_inc(S["d_exp"], 1)
            act.wait_ge(S["qd_ready"], 1)
            for s in range(LEVELS):
                for g in range(3):
                    act.wait_ge(S["lvl_p1"], 3 * s + g + 1)
                    if s:
                        act.wait_ge(S["lvl_zt"], 3 * (s - 1) + g + 1)
                    nc.scalar.activation(P1[:, 4 * g:4 * g + 4, :], bank(g).rearrange("p (a b) -> p a b", b=P),
                                         ACT.Copy).then_inc(S["lvl_p1sb"], 1)
            for c in range(NCHUNK):
                r = slice(CHUNK * (c % 2), CHUNK * (c % 2) + CHUNK)
                act.wait_ge(S["vn_ps"], c + 1)
                if c == 0:
                    act.wait_ge(S["vn_zeroed"], 1)
                for b in range(2):
                    last = nc.scalar.activation(VN[c % 2][r, 3 * b:3 * b + 3, :],
                                                PS[r, 5 + b, 0:3 * P].rearrange("p (a b) -> p a b", b=P), ACT.Copy)
                last.then_inc(S["vn_sb"], 1)
            act.wait_ge(S["o_ps"], 1)
            for j in range(3):
                nc.scalar.activation(OB[:, 2 * j:2 * j + 2, :], pairs(bank(j)), ACT.Copy).then_inc(S["o_sb"], 1)
                nc.scalar.activation(OSQ[:, 2 * j:2 * j + 2, :], pairs(bank(j)), ACT.Square).then_inc(S["o_sq"], 1)
            for j in range(3):
                act.wait_ge(S["o_sum"], j + 1)
                nc.scalar.activation(OSD[:, 2 * j:2 * j + 2, :], pairs(bank(3 + j)), ACT.Sqrt, bias=EPS,
                                     scale=1.0 / P).then_inc(S["o_sd"], 1)
            attention("mem0")
            operand_hi("out0")
            out_linear("out0")
            norm("ffn1")
            operand_hi("ffn1")
            ffn(1, "ffn1")

            norm("dkv")
            operand_hi("dkv")
            act.dma_start(POSI, d["positions"]).then_inc(S["pos_loaded"], 16)
            act.wait_ge(S["rope_ang"], 1)
            nc.scalar.activation(SIN, ANG_S, ACT.Sin).then_inc(S["rope_tab"], 1)
            nc.scalar.activation(COS, ANG_C, ACT.Sin).then_inc(S["rope_tab"], 1)
            n0 = tile0["dkv"]
            latent(0, n0)
            w_hi(n0 + RING)
            act.wait_ge(S["tile_used"], n0 + 2)
            nc.scalar.activation(KR, bank(1, SEQ), ACT.Copy).then_inc(S["rope_in"], 1)
            w_hi(n0 + 1 + RING)
            latent_rest(0)
            n0 = tile0["ukv"]
            for t in range(2):
                act.wait_ge(S["tile_used"], n0 + t + 1)
                nc.scalar.activation(KN[:, 3 * t:3 * t + 2, :], pairs(bank(4 * t)), ACT.Copy)
                nc.scalar.activation(KN[:, 3 * t + 2, :], bank(4 * t + 1, SEQ), ACT.Copy)
                for tb in range(TB):
                    last = nc.scalar.activation(VM[:, tb, 3 * t:3 * t + 3, :],
                                                bank(4 * t + 2 + tb, 3 * P).rearrange("p (a b) -> p a b", b=P), ACT.Copy)
                last.then_inc(S["ukv_evac"], 1)
                w_hi(n0 + t + RING)
            norm("ffn2")
            operand_hi("ffn2")
            ffn(2, "ffn2")

            norm("bin")
            operand_hi("bin")
            n0 = tile0["bin"]
            latent(1, n0)
            w_hi(n0 + RING)
            act.wait_ge(S["tile_used"], n0 + 2)
            nc.scalar.activation(QM[:, :, :], pairs(bank(1)), ACT.Copy).then_inc(S["qm_ready"], 1)
            w_hi(n0 + 1 + RING)
            latent_rest(1)
            n0 = tile0["uq"]
            for t in range(2):
                act.wait_ge(S["tile_used"], n0 + t + 1)
                nc.scalar.activation(QQ[:, 3 * t:3 * t + 3, :, :].rearrange("p a b c -> p a (b c)"),
                                     PS[:, 3 * t:3 * t + 3, :], ACT.Copy).then_inc(S["uq_evac"], 1)
                w_hi(n0 + t + RING)
            attention("mem1")
            attention("mla")
            operand_hi("out1")
            out_linear("out1")
            norm("ffn3")
            operand_hi("ffn3")
            ffn(3, "ffn3")
            norm("final")
            norm("in2")
            operand_hi("in2")

            n0 = tile0["in2"]
            dst = [CA_, CG_, UP[:, :, 16:16 + SEQ], SB_, SC_, SH_, ZQ[:, 0:2, :], ZQ[:, 2:4, :], ZV]
            act.wait_ge(S["pads_ready"], 2)
            for t in range(9):
                act.wait_ge(S["tile_used"], n0 + t + 1)
                nc.scalar.activation(dst[t], pairs(bank(t % 4)), ACT.Sigmoid if t == 1 else ACT.Copy).then_inc(S["in2_evac"], 1)
                w_hi(n0 + t + RING)
            act.wait_ge(S["conf_mean_ps"], 1)
            nc.scalar.activation(MN, bank(5, SEQ), ACT.Copy, scale=1.0 / (2 * P)).then_inc(S["conf_mean"], 1)
            act.wait_ge(S["in2_evac"], 9)
            nc.scalar.activation(ZS, ZQ, ACT.Square).then_inc(S["qk2_sq"], 1)
            act.wait_ge(S["conf_xc"], 1)
            nc.scalar.activation(CVS, XC, ACT.Square).then_inc(S["conf_sq"], 1)
            act.wait_ge(S["conf_var_ps"], 1)
            nc.scalar.activation(SD[:, :], bank(6, SEQ), ACT.Sqrt, bias=EPS, scale=1.0 / (2 * P)).then_inc(S["conf_sd"], 1)
            act.wait_ge(S["qk2_ps"], 1)
            nc.scalar.activation(ZS, PS[:, 0:2, :].rearrange("p a (b c) -> p (a b) c", c=SEQ), ACT.Sqrt, bias=EPS,
                                 scale=1.0 / 32).then_inc(S["qk2_sd"], 1)
            act.wait_ge(S["lam_prod"], 1)
            nc.scalar.activation(LAM2, LAMS, ACT.Exp).then_inc(S["lam_exp"], 1)
            act.wait_ge(S["conf_y"], 1)
            for b in range(2):
                nc.scalar.activation(T8[:, 4 + b, :], XC[:, b, :], ACT.Silu, bias=par("ln_b", b, 1)).then_inc(S["conf_out"], 1)
            attention("diff")
            act.wait_ge(S["att_done"], 1)
            nc.scalar.activation(CVS, T8[:, 6:8, :], ACT.Square).then_inc(S["sub_sq"], 1)
            act.wait_ge(S["sub_ps"], 1)
            nc.scalar.activation(XC, pairs(bank(5)), ACT.Sqrt, bias=EPS, scale=1.0 / 64).then_inc(S["sub_sd"], 1)
            operand_hi("out2")
            out_linear("out2")
            norm("ffn4")
            operand_hi("ffn4")
            ffn(4, "ffn4")

        @block.vector
        def _(dve):
            step = [0]

            def link(ins):
                step[0] += 1
                ins.then_inc(S["dve_step"], 1)
                dve.wait_ge(S["dve_step"], step[0])

            def poke(sem, n):
                link(nc.vector.memset(SMALL[:, 127:128], 0.0))
                nc.vector.memset(SMALL[:, 127:128], 0.0).then_inc(sem, n)

            def w_lo(n, i=None):
                if n >= n_tiles:
                    return
                dve.wait_ge(S["w_hi"], n + 1 + (0 if i is None else i * 6))
                w = width(n)
                nc.vector.tensor_tensor(WL[:, n % RING, 0:w], RAW[:, n % RING, 0:w], WH[:, n % RING, 0:w],
                                        ALU.subtract).then_inc(S["w_split"], 1)

            def operand_lo(name, p):
                dve.wait_ge(S["hi_ready"], 4 * version[name] + p + 1)
                nc.vector.tensor_tensor(XL[:, 2 * p:2 * p + 2, :], T8[:, 2 * p:2 * p + 2, :],
                                        XH[:, 2 * p:2 * p + 2, :], ALU.subtract).then_inc(S["act_ready"], 1)

            def operand_lo_all(name):
                for p in range(4):
                    operand_lo(name, p)

            def norm(name, src=X):
                k = norm_no[name]
                dve.wait_ge(S["norm_sd"], k + 1)
                link(nc.vector.reciprocal(RS[:, :], SD[:, :]))
                for p in range(4):
                    for b in (2 * p, 2 * p + 1):
                        last = nc.vector.scalar_tensor_tensor(
                            out=(X if name == "final" else T8)[:, b, :], in0=src[:, b, :],
                            scalar=par(NORM_GAIN[k], b, 1), in1=RS[:, :], op0=ALU.mult, op1=ALU.mult)
                    if name == "final":
                        last.then_inc(S["x_ready"], 1)
                        continue
                    last.then_inc(S["t8_ready"], 1)
                    if p:
                        operand_lo(name, p - 1)
                if name != "final":
                    operand_lo(name, 3)

            def ffn(f, name):
                n0 = tile0[name]

                def hidden(s, i=None):
                    turn = 0 if i is None else i * 2
                    dve.wait_ge(S["sg_ready"], STEPS * f + s + 1 + turn)
                    if f or s or i is not None:
                        dve.wait_ge(S["h_ready"], STEPS * f + s + turn)
                    nc.vector.tensor_tensor(HF, SG, PS[:, 4:6, SEQ:2 * SEQ], ALU.mult).then_inc(S["glu_free"], 1)
                    dve.wait_ge(S["h_hi"], STEPS * f + s + 1 + turn)
                    half = slice(2 * (s % 2), 2 * (s % 2) + 2)
                    nc.vector.tensor_tensor(HL[:, half, :], HF, HH[:, half, :], ALU.subtract).then_inc(S["h_ready"], 1)

                def one(s, i=None):
                    w_lo(n0 + 3 * s + 2, i)
                    w_lo(n0 + 3 * s + 3, i)
                    hidden(s, i)
                    w_lo(n0 + 3 * s + 4, i)

                w_lo(n0 + 3)
                hidden(0)
                w_lo(n0 + 4)
                loops = loops_of(name)
                with nc.vector.Fori(0, loops) as i:
                    one(1, i)
                    one(2, i)
                for s in range(2 * loops + 1, STEPS):
                    one(s)
                w_lo(n0 + 3 * STEPS + 2)
                dve.wait_ge(S["tile_used"], n0 + 3 * STEPS)
                for p in range(4):
                    nc.vector.scalar_tensor_tensor(out=X[:, 2 * p:2 * p + 2, :], in0=pairs(bank(p)), scalar=ffn_scale(name),
                                                   in1=X[:, 2 * p:2 * p + 2, :], op0=ALU.mult, op1=ALU.add).then_inc(S["x_ready"], 1)

            def out_linear(name):
                n0 = tile0[name]
                for t in range(4):
                    dve.wait_ge(S["tile_used"], n0 + t + 1)
                    nc.vector.tensor_tensor(X[:, 2 * t:2 * t + 2, :], X[:, 2 * t:2 * t + 2, :], pairs(bank(t)),
                                            ALU.add).then_inc(S["x_ready"], 1)
                    w_lo(n0 + t + RING)

            def attention(ph):
                u0, m0, g0 = att0[ph]
                kind, n = att_of[ph]
                maps = 2 if kind == "diff" else 1
                sc, pt = att_work(ph)

                def maxima(u):
                    for m in range(maps):
                        s = sc[u % 2][m]
                        dve.wait_ge(S["att_s"], m0 + u * maps + m + 1)
                        ps = pairs(bank(2 * (u % 2) + m))
                        if kind == "mem":
                            link(nc.vector.tensor_reduce(MX(u, m), ps, axis=AX.X, op=ALU.max))
                            nc.vector.tensor_scalar(NM2(u, m), MX(u, m), -MEM_SCALE, None, ALU.mult).then_inc(S["att_nm"], 1)
                            continue
                        if u >= 2:
                            dve.wait_ge(S["att_t"], u0 + u - 1)
                        added = (con("mla_mask").rearrange("p (a b) -> p a b", b=SEQ) if kind == "mla" else BIAS[:, :, u, :])
                        link(nc.vector.scalar_tensor_tensor(out=s, in0=ps, scalar=(MLA_SCALE if kind == "mla" else DIFF_SCALE),
                                                            in1=added, op0=ALU.mult, op1=ALU.add))
                        link(nc.vector.tensor_reduce(MX(u, m), s, axis=AX.X, op=ALU.max))
                        nc.vector.tensor_scalar(NM2(u, m), MX(u, m), -1.0, None, ALU.mult).then_inc(S["att_nm"], 1)

                def normalise(u):
                    dve.wait_ge(S["att_e"], m0 + (u + 1) * maps)
                    for m in range(maps):
                        link(nc.vector.reciprocal(RC2(u, m), SUM2(u, m)))
                    if kind == "diff":
                        link(nc.vector.tensor_scalar(RC2(u, 1), RC2(u, 1), NLAM, None, ALU.mult))
                    a, b = sc[u % 2]
                    for q in range(TB):
                        last = nc.vector.tensor_scalar(a[:, q, :], a[:, q, :], RC(u, 0, q), None, ALU.mult)
                        if kind == "diff":
                            link(last)
                            last = nc.vector.scalar_tensor_tensor(out=a[:, q, :], in0=b[:, q, :], scalar=RC(u, 1, q),
                                                                  in1=a[:, q, :], op0=ALU.mult, op1=ALU.add)
                    last.then_inc(S["att_p"], 1)

                def evac(g):
                    dve.wait_ge(S["att_o"], g0 + g + 1)
                    nc.vector.tensor_copy(T8[:, (g if kind == "mla" else 6 + g), :], bank(6 + g % 2, SEQ)).then_inc(S["att_oe"], 1)

                per = 1 if kind == "mla" else 2
                maxima(0)
                for u in range(n):
                    if u + 1 < n:
                        maxima(u + 1)
                    normalise(u)
                    if u >= 1 and (u % per) == 0:
                        evac(u // per - 1)
                evac(n // per - 1)

            def latent(r, gain):
                dve.wait_ge(S["lat_sd"], r + 1)
                link(nc.vector.reciprocal(RS[:, :], SD[:, :]))
                dve.wait_ge(S["lat_sb"], r + 1)
                for b in range(2):
                    last = nc.vector.scalar_tensor_tensor(out=LAT[:, b, :], in0=LAT[:, b, :], scalar=par(gain, b, 1),
                                                          in1=RS[:, :], op0=ALU.mult, op1=ALU.mult)
                last.then_inc(S["lat_f"], 1)
                dve.wait_ge(S["lat_hi"], r + 1)
                nc.vector.tensor_tensor(HL[:, 0:2, :], LAT, HH[:, 0:2, :], ALU.subtract).then_inc(S["lat_ready"], 1)

            nc.vector.memset(ZB[:, :], 0.0).then_inc(S["zeros_ready"], 1)
            dve.wait_ge(S["inputs_loaded"], 64)
            poke(S["x_ready"], 8)
            for n in range(RING):
                w_lo(n)
            norm("mem", MEMT)
            for t in range(4):
                w_lo(t + RING)
            norm("ffn0")
            ffn(0, "ffn0")
            norm("ain")

            n0 = tile0["ain"]
            w_lo(n0 + RING)
            nc.vector.memset(CB[:, :, 0:PAD], 0.0).then_inc(S["pads_ready"], 1)
            for t in range(9):
                w_lo(n0 + t + 1 + RING)
                dve.wait_ge(S["ain_evac"], t + 1)
                for tap in range(4):
                    for b in (2 * t, 2 * t + 1):
                        w = par("a_conv", 4 * b + tap, 1)
                        x = CB[:, b, tap:tap + SEQ]
                        if tap == 0:
                            last = nc.vector.tensor_scalar(YQKV[:, b, :], x, w, None, ALU.mult)
                        else:
                            last = nc.vector.scalar_tensor_tensor(out=YQKV[:, b, :], in0=x, scalar=w, in1=YQKV[:, b, :],
                                                                  op0=ALU.mult, op1=ALU.add)
                    if tap < 3:
                        link(last)
                last.then_inc(S["conv_done"], 1)
            for t in range(9, 13):
                w_lo(n0 + t + 1 + RING)
            for j in range(6):
                v, y = QKS[:, 2 * j:2 * j + 2, :], YQKV[:, 2 * j:2 * j + 2, :]
                dve.wait_ge(S["l2_sd"], j + 1)
                link(nc.vector.reciprocal(v, v))
                nc.vector.scalar_tensor_tensor(out=y, in0=y, scalar=(P ** -0.5 if j < 3 else 1.0), in1=v,
                                               op0=ALU.mult, op1=ALU.mult).then_inc(S["qk_ready"], 1)
            dve.wait_ge(S["g_exp1"], 1)
            nc.vector.tensor_tensor(G1, BA[:, :, AH:2 * AH], over(par("dt_bias"), TB), ALU.add).then_inc(S["g_dve1"], 1)
            dve.wait_ge(S["g_act2"], 1)
            link(nc.vector.tensor_scalar(BETA, BETA, 1.0, None, ALU.add))
            nc.vector.reciprocal(BETA, BETA).then_inc(S["beta_ready"], 1)
            link(nc.vector.tensor_scalar(G1, G1, 0.0, None, ALU.max))
            link(nc.vector.tensor_tensor(G1, G1, G2, ALU.add))
            nc.vector.scalar_tensor_tensor(out=GG, in0=G1, scalar=-1.0, in1=over(EA, TB), op0=ALU.mult,
                                           op1=ALU.mult).then_inc(S["decay_g_ready"], 1)
            dve.wait_ge(S["qk_ready"], 6)
            for j in range(3):
                dve.wait_ge(S["rows_ps"], 4 + j)
                nc.vector.tensor_tensor(KBT[:, 2 * j:2 * j + 2, :], Yk[:, 2 * j:2 * j + 2, :], pairs(bank(3 + j)),
                                        ALU.mult).then_inc(S["kb_ready"], 1)
            dve.wait_ge(S["beta_ready"], 1)
            dve.wait_ge(S["tok_ps"], 1)
            for m in range(TB * AH):
                tb, h = divmod(m, AH)
                last = nc.vector.tensor_scalar(VB[:, tb, h, :], PS[:, 3 + m // 4, (m % 4) * P:(m % 4 + 1) * P],
                                               BETA[:, tb, h:h + 1], None, ALU.mult)
            last.then_inc(S["vb_ready"], 1)
            dve.wait_ge(S["gcol_sb"], 1)
            dve.wait_ge(S["rows_sb"], 6)
            for m in range(TB * AH):
                tb, h = divmod(m, AH)
                last = nc.vector.tensor_scalar(DT[:, m, :], GROW[:, h, tb * P:(tb + 1) * P], GC[:, tb, h:h + 1], 0.0,
                                               ALU.subtract, ALU.min)
            last.then_inc(S["d_pre"], 1)
            dve.wait_ge(S["d_exp"], 1)
            link(nc.vector.tensor_tensor(DT, DT, over(con("tri"), TB * AH), ALU.mult))
            dve.wait_ge(S["kkt_ps"], 1)
            for j in range(3):
                last = nc.vector.tensor_tensor(LT[:, 4 * j:4 * j + 4, :], DT[:, 4 * j:4 * j + 4, :],
                                               bank(3 + j).rearrange("p (a b) -> p a b", b=P), ALU.mult)
            link(last)
            dve.wait_ge(S["qkt_ps"], 1)
            for j in range(3):
                last = nc.vector.tensor_tensor(QD[:, 4 * j:4 * j + 4, :], DT[:, 4 * j:4 * j + 4, :],
                                               bank(j).rearrange("p (a b) -> p a b", b=P), ALU.mult)
            last.then_inc(S["qd_ready"], 1)
            nc.vector.tensor_copy(XM, over(con("ident"), TB * AH))
            nc.vector.tensor_copy(XT, over(con("ident"), TB * AH)).then_inc(S["lvl_init"], 1)
            for s in range(LEVELS):
                level = con("level", s * P, P)
                for g in range(3):
                    r = slice(4 * g, 4 * g + 4)
                    if s:
                        dve.wait_ge(S["lvl_p1"], 3 * (s - 1) + g + 1)
                    nc.vector.tensor_tensor(MT[:, r, :], LT[:, r, :], over(level, 4), ALU.mult).then_inc(S["lvl_m"], 1)
                if s == 0:
                    nc.vector.tensor_tensor(KBT, KBT, EGROW, ALU.mult)
                    nc.vector.tensor_tensor(Yq, Yq, EGROW, ALU.mult).then_inc(S["scaled"], 1)
                    dve.wait_ge(S["lvl_init"], 1)
                for g in range(3):
                    r = slice(4 * g, 4 * g + 4)
                    dve.wait_ge(S["lvl_zt"], 3 * s + g + 1)
                    if s < LEVELS - 1:
                        nc.vector.tensor_tensor(XM[:, r, :], XM[:, r, :], bank(3 + g).rearrange("p (a b) -> p a b", b=P),
                                                ALU.subtract).then_inc(S["lvl_x"], 1)
                    nc.vector.tensor_tensor(XT[:, r, :], XT[:, r, :], bank(g).rearrange("p (a b) -> p a b", b=P),
                                            ALU.subtract).then_inc(S["lvl_xt"], 1)
            for v in VN:
                last = nc.vector.memset(v, 0.0)
            last.then_inc(S["vn_zeroed"], 1)
            for c in range(NCHUNK):
                tb, hf = divmod(c, 2)
                r = slice(CHUNK * hf, CHUNK * hf + CHUNK)
                if c == 0:
                    dve.wait_ge(S["vb_ready"], 1)
                    nc.vector.tensor_copy(RR, VB[:, 0, :, :]).then_inc(S["r_ready"], 1)
                else:
                    dve.wait_ge(S["ks_ps"], c)
                    for b in range(2):
                        last = nc.vector.tensor_tensor(RR[r, 3 * b:3 * b + 3, :], VB[r, tb, 3 * b:3 * b + 3, :],
                                                       PS[r, 3 + b, 0:3 * P].rearrange("p (a b) -> p a b", b=P), ALU.subtract)
                    last.then_inc(S["r_ready"], 1)
                if c == NCHUNK - 1:
                    break
                dve.wait_ge(S["su_ps"], c + 1)
                for h in range(AH):
                    su = PS[:, 3 + h // 3, (h % 3) * P:(h % 3 + 1) * P]
                    if c == 0:
                        last = nc.vector.tensor_copy(ST[:, h, :], su)
                    else:
                        last = nc.vector.scalar_tensor_tensor(out=ST[:, h, :], in0=ST[:, h, :],
                                                              scalar=EGROW[:, h, CHUNK * (c + 1) - 1:CHUNK * (c + 1)], in1=su,
                                                              op0=ALU.mult, op1=ALU.add)
                last.then_inc(S["s_ready"], 1)
            for j in range(3):
                dve.wait_ge(S["o_sd"], j + 1)
                v, o, t = OSD[:, 2 * j:2 * j + 2, :], OB[:, 2 * j:2 * j + 2, :], T8[:, 2 * j:2 * j + 2, :]
                link(nc.vector.reciprocal(v, v))
                link(nc.vector.scalar_tensor_tensor(out=o, in0=o, scalar=par("a_out_norm"), in1=v, op0=ALU.mult, op1=ALU.mult))
                nc.vector.tensor_tensor(t, t, o, ALU.mult)
            attention("mem0")
            poke(S["t8_ready"], 4)
            operand_lo_all("out0")
            out_linear("out0")
            norm("ffn1")
            ffn(1, "ffn1")

            norm("dkv")
            poke(S["x_ready"], 4)
            dve.wait_ge(S["pos_loaded"], 16)
            link(nc.vector.tensor_copy(ANG, POSI))
            link(nc.vector.tensor_scalar(ANG, ANG, con("inv_freq"), None, ALU.mult))
            link(nc.vector.tensor_scalar(TURN, ANG, 1.0 / (2 * PI), ROUND, ALU.mult, ALU.add))
            link(nc.vector.tensor_scalar(TURN, TURN, -ROUND, None, ALU.add))
            for part in TWO_PI:
                link(nc.vector.scalar_tensor_tensor(out=ANG, in0=TURN, scalar=-part, in1=ANG, op0=ALU.mult, op1=ALU.add))
            link(nc.vector.tensor_scalar(ANG_S, ANG, PI_IN, -PI_IN, ALU.min, ALU.max))
            link(nc.vector.tensor_scalar(ANG_C, ANG_S, PI / 2, None, ALU.add))
            link(nc.vector.tensor_scalar(TURN, ANG_C, PI, -2 * PI, ALU.is_gt, ALU.mult))
            link(nc.vector.tensor_tensor(ANG_C, ANG_C, TURN, ALU.add))
            nc.vector.tensor_scalar(ANG_C, ANG_C, PI_IN, -PI_IN, ALU.min, ALU.max).then_inc(S["rope_ang"], 1)
            n0 = tile0["dkv"]
            w_lo(n0 + RING)
            w_lo(n0 + 1 + RING)
            latent(0, "kv_lat_norm")
            dve.wait_ge(S["rope_tab"], 2)
            dve.wait_ge(S["rope_ps"], 1)
            nc.vector.tensor_tensor(ROT[:, 0, :], SIN, bank(2, SEQ), ALU.mult)
            link(nc.vector.tensor_tensor(KR, KR, COS, ALU.mult))
            link(nc.vector.tensor_tensor(KR, KR, ROT[:, 0, :], ALU.add))
            nc.vector.tensor_scalar(KR, KR, con("half"), None, ALU.mult).then_inc(S["rope_done"], 1)
            n0 = tile0["ukv"]
            for t in range(2):
                w_lo(n0 + t + RING)
            norm("ffn2")
            ffn(2, "ffn2")

            norm("bin")
            n0 = tile0["bin"]
            w_lo(n0 + RING)
            w_lo(n0 + 1 + RING)
            latent(1, "b_q_norm")
            n0 = tile0["uq"]
            for t in range(2):
                w_lo(n0 + t + RING)
            for j in range(3):
                dve.wait_ge(S["uq_ps"], j + 1)
                last = nc.vector.tensor_tensor(ROT[:, 2 * j:2 * j + 2, :], pairs(bank((6 + j) % 8)), over(SIN, 2), ALU.mult)
            q = QQ[:, :, 1, :]
            link(nc.vector.tensor_tensor(q, q, over(COS, BH), ALU.mult))
            nc.vector.tensor_tensor(q, q, ROT, ALU.add).then_inc(S["rope_done"], 1)
            attention("mem1")
            attention("mla")
            poke(S["t8_ready"], 4)
            operand_lo_all("out1")
            out_linear("out1")
            norm("ffn3")
            ffn(3, "ffn3")
            norm("final")
            norm("in2")

            n0 = tile0["in2"]
            nc.vector.memset(UP[:, :, 0:16], 0.0)
            nc.vector.memset(CS[:, :, 0:2], 0.0)
            nc.vector.memset(CC_[:, :, 0:30], 0.0).then_inc(S["pads_ready"], 1)
            for j in range(2):
                last = nc.vector.tensor_tensor(LAMP[:, j, :], par("lam", 64 * j, 32), par("lam", 64 * j + 32, 32), ALU.mult)
            link(last)
            nc.vector.tensor_reduce(LAMS, LAMP[:, :, :], axis=AX.X, op=ALU.add).then_inc(S["lam_prod"], 1)
            dve.wait_ge(S["bias_ps"], 1)
            nc.vector.tensor_tensor(BROW, PS[:, 4:8, :], over(TABLE[:, 2 * SEQ:], MH), ALU.add).then_inc(S["bias_row"], 1)
            taps = [(b, j) for j in range(31) for b in range(2)]

            def conf_tap(b, j):
                w = par("conf_w", 31 * b + j, 1)
                x = CC_[:, b, j:j + SEQ]
                if j == 0:
                    return nc.vector.tensor_scalar(CV[:, b, :], x, w, par("conf_b", b, 1), ALU.mult, ALU.add)
                return nc.vector.scalar_tensor_tensor(out=CV[:, b, :], in0=x, scalar=w, in1=CV[:, b, :], op0=ALU.mult, op1=ALU.add)

            for t in range(9):
                w_lo(n0 + t + RING)
                if t < 1:
                    continue
                if t == 1:
                    dve.wait_ge(S["in2_evac"], 2)
                    link(nc.vector.tensor_tensor(CC_[:, :, 30:30 + SEQ], CA_, CG_, ALU.mult))
                for _ in range(7):
                    if taps:
                        b, j = taps.pop(0)
                        link(conf_tap(b, j))
            while taps:
                b, j = taps.pop(0)
                last = conf_tap(b, j)
                if taps:
                    link(last)
            last.then_inc(S["conf_ready"], 1)
            dve.wait_ge(S["in2_evac"], 9)
            link(nc.vector.tensor_tensor(CS[:, :, 2:2 + SEQ], SC_, SH_, ALU.mult))
            for tap in range(3):
                for b in range(2):
                    w, x = par("sconv", 3 * b + tap, 1), CS[:, b, tap:tap + SEQ]
                    if tap == 0:
                        last = nc.vector.tensor_scalar(SC_[:, b, :], x, w, None, ALU.mult)
                    else:
                        last = nc.vector.scalar_tensor_tensor(out=SC_[:, b, :], in0=x, scalar=w, in1=SC_[:, b, :],
                                                              op0=ALU.mult, op1=ALU.add)
                link(last)
            nc.vector.tensor_tensor(T8[:, 2:4, :], SC_, SB_, ALU.mult)
            dve.wait_ge(S["conf_mean"], 1)
            nc.vector.tensor_tensor(XC, CV, over(MN, 2), ALU.subtract).then_inc(S["conf_xc"], 1)
            dve.wait_ge(S["pool_ps"], 1)
            for b in range(2):
                nc.vector.tensor_scalar(T8[:, b, :], bank(4)[:, b * SEQ:(b + 1) * SEQ], par("pool_scale", b, 1), None, ALU.mult)
            dve.wait_ge(S["conf_sd"], 1)
            link(nc.vector.reciprocal(RS[:, :], SD[:, :]))
            for b in range(2):
                last = nc.vector.scalar_tensor_tensor(out=XC[:, b, :], in0=XC[:, b, :], scalar=par("ln_g", b, 1), in1=RS[:, :],
                                                      op0=ALU.mult, op1=ALU.mult)
            last.then_inc(S["conf_y"], 1)
            dve.wait_ge(S["qk2_sd"], 1)
            link(nc.vector.reciprocal(ZS, ZS))
            for j, g in enumerate(("q_g", "k_g")):
                v = ZQ[:, 2 * j:2 * j + 2, :]
                last = nc.vector.scalar_tensor_tensor(out=v, in0=v, scalar=par(g), in1=ZS[:, 2 * j:2 * j + 2, :],
                                                      op0=ALU.mult, op1=ALU.mult)
            last.then_inc(S["qk2_ready"], 1)
            dve.wait_ge(S["lam_exp"], 1)
            link(nc.vector.tensor_tensor(NLAM, LAM2[:, 1:2], LAM2[:, 0:1], ALU.subtract))
            link(nc.vector.tensor_scalar(NLAM, NLAM, -LAM_INIT, None, ALU.add))
            dve.wait_ge(S["bias_ready"], 32)
            attention("diff")
            poke(S["att_done"], 1)
            dve.wait_ge(S["sub_sd"], 1)
            link(nc.vector.reciprocal(XC, XC))
            v = T8[:, 6:8, :]
            link(nc.vector.scalar_tensor_tensor(out=v, in0=v, scalar=par("subln"), in1=XC, op0=ALU.mult, op1=ALU.mult))
            link(nc.vector.tensor_scalar(v, v, 1.0 - LAM_INIT, None, ALU.mult))
            dve.wait_ge(S["conf_out"], 2)
            poke(S["t8_ready"], 4)
            operand_lo_all("out2")
            out_linear("out2")
            norm("ffn4")
            ffn(4, "ffn4")

        @block.tensor
        def _(pe):
            def f32mm(o, w, a, start=True, stop=True):
                return nc.tensor.matmul(o, w, a, start=start, stop=stop, skip_group_check=True)

            def norm(name):
                k = norm_no[name]
                for p in range(4):
                    pe.wait_ge(S["norm_sq"], 4 * k + p + 1)
                    for b in (2 * p, 2 * p + 1):
                        last = f32mm(bank(7, SEQ), con("ones"), T8[:, b, :], b == 0, b == KB - 1)
                last.then_inc(S["norm_ms"], 1)

            def tile_ready(n, i=None):
                pe.wait_ge(S["w_split"], n + 1 + (0 if i is None else i * 6))

            def w_at(n, at):
                s = slice(at, at + P)
                return WH[:, n % RING, s], WL[:, n % RING, s]

            def operand(name, kb):
                if name is not None and kb % 2 == 0:
                    pe.wait_ge(S["act_ready"], 4 * version[name] + kb // 2 + 1)

            def by_feature(n, b, first=None, outs=None, blocks=2, i=None, row=CW):
                tile_ready(n, i)
                for f in range(blocks):
                    o = outs[f] if outs else bank(b)[:, f * SEQ:(f + 1) * SEQ]
                    for kb in range(KB):
                        if f == 0:
                            operand(first, kb)
                        last = matmul3(o, *w_at(n, kb * row + f * P), XH[:, kb, :], XL[:, kb, :], kb == 0, kb == KB - 1)
                return last.then_inc(S["tile_used"], 1)

            def by_token(n, b, cols, first=None):
                tile_ready(n)
                for tb in range(TB):
                    o = bank(b)[:, tb * cols:(tb + 1) * cols]
                    t = slice(tb * P, (tb + 1) * P)
                    for kb in range(KB):
                        if tb == 0:
                            operand(first, kb)
                        s = slice(kb * cols, (kb + 1) * cols)
                        last = matmul3_tok(o, XH[:, kb, t], XL[:, kb, t], WH[:, n % RING, s], WL[:, n % RING, s],
                                           kb == 0, kb == KB - 1)
                return last.then_inc(S["tile_used"], 1)

            def matmul3_tok(o, a_hi, a_lo, w_hi, w_lo, start, stop):
                nc.tensor.matmul(o, a_hi, w_hi, start=start, stop=False, skip_group_check=True)
                nc.tensor.matmul(o, a_hi, w_lo, start=False, stop=False, skip_group_check=True)
                return nc.tensor.matmul(o, a_lo, w_hi, start=False, stop=stop, skip_group_check=True)

            def ffn(f, name):
                n0 = tile0[name]

                def gate_up(s, first=None, i=None):
                    n = n0 if s == 0 else n0 + 3 * s - 1
                    if f or not (isinstance(s, int) and s == 0 and i is None):
                        pe.wait_ge(S["glu_free"], STEPS * f + s + (0 if i is None else i * 2))
                    for k in range(2):
                        by_feature(n + k, None, first if k == 0 else None,
                                   outs=[PS[:, 4 + b, k * SEQ:(k + 1) * SEQ] for b in range(2)], i=i)

                def down(s, n, i=None, stop_=False):
                    tile_ready(n, i)
                    pe.wait_ge(S["h_ready"], STEPS * f + s + 1 + (0 if i is None else i * 2))
                    for j in range(2):
                        for nb in range(KB):
                            h = 2 * (s % 2) + j
                            last = matmul3(PS[:, nb // 2, (nb % 2) * SEQ:(nb % 2 + 1) * SEQ], *w_at(n, j * D + nb * P),
                                           HH[:, h, :], HL[:, h, :], False, stop_ and j == 1 and nb % 2 == 1)
                    last.then_inc(S["tile_used"], 1)

                for b in range(4):
                    nc.tensor.matmul(bank(b), ZB[:, 0:P], ZB[:, :], start=True, stop=False, skip_group_check=True)
                gate_up(0, name)
                loops = loops_of(name)
                with nc.tensor.Fori(0, loops) as i:
                    for s in (1, 2):
                        gate_up(s, None, i)
                        down(s - 1, n0 + 3 * s + 1, i)
                for s in range(2 * loops + 1, STEPS):
                    gate_up(s)
                    down(s - 1, n0 + 3 * s + 1)
                down(STEPS - 1, n0 + 3 * STEPS - 1, None, True)

            def out_linear(name):
                for t in range(4):
                    by_feature(tile0[name] + t, t, name if t == 0 else None)

            def attention(ph):
                u0, m0, g0 = att0[ph]
                kind, n = att_of[ph]
                maps = 2 if kind == "diff" else 1
                sc, pt = att_work(ph)
                per = 1 if kind == "mla" else 2

                def scores(u):
                    need = m0 if u < 2 else m0 + (u - 1) * maps
                    if need:
                        pe.wait_ge(S["att_e"], need)
                    for m in range(maps):
                        for q in range(TB):
                            o = PS[:, 2 * (u % 2) + m, q * SEQ:(q + 1) * SEQ]
                            t = slice(q * P, (q + 1) * P)
                            if kind == "mem":
                                r = slice(64 * (u % 2), 64 * (u % 2) + 64)
                                last = f32mm(o, QM[r, u // 2, t], KM[0 if ph == "mem0" else 1][r, u // 2, :])
                            elif kind == "mla":
                                f32mm(o, QQ[:, u, 0, t], KN[:, u, :], True, False)
                                last = f32mm(o, QQ[:, u, 1, t], KR, False, True)
                            else:
                                a = 64 * (u % 2) + 32 * m
                                r = slice(a, a + 32)
                                last = f32mm(o, ZQ[r, u // 2, t], ZQ[r, 2 + u // 2, :])
                        last.then_inc(S["att_s"], 1)

                def turn(u):
                    pe.wait_ge(S["att_p"], u0 + u + 1)
                    if u0 + u >= 2:
                        pe.wait_ge(S["att_pt"], u0 + u - 1)
                    for kb in range(TB):
                        for q in range(TB):
                            last = nc.tensor.transpose(bank(4 + u % 2)[:, kb * SEQ + q * P:kb * SEQ + (q + 1) * P],
                                                       sc[u % 2][0][:, q, kb * P:(kb + 1) * P], con("ident"))
                    last.then_inc(S["att_t"], 1)

                def values(u):
                    g = u // per
                    pe.wait_ge(S["att_pt"], u0 + u + 1)
                    if u % per == 0 and g0 + g >= 2:
                        pe.wait_ge(S["att_oe"], g0 + g - 1)
                    for kb in range(TB):
                        if kind == "mla":
                            v, o = VM[:, kb, u, :], bank(6 + g % 2, SEQ)
                        else:
                            r = slice(64 * (u % 2), 64 * (u % 2) + 64)
                            src = ZV if kind == "diff" else VM2[0 if ph == "mem0" else 1]
                            v, o = src[:, kb, 64 * u:64 * u + 64], PS[r, 6 + g % 2, 0:SEQ]
                        last = f32mm(o, v, pt[u % 2][:, kb, :], kb == 0, kb == TB - 1)
                    if u % per == per - 1:
                        last.then_inc(S["att_o"], 1)

                scores(0)
                for u in range(n):
                    if u + 1 < n:
                        scores(u + 1)
                    turn(u)
                    values(u)

            def latent(r):
                pe.wait_ge(S["lat_sq"], r + 1)
                for b in range(2):
                    last = f32mm(bank(7, SEQ), con("ones"), LSQ[:, b, :], b == 0, b == 1)
                last.then_inc(S["lat_sum"], 1)

            pe.wait_ge(S["inputs_loaded"], 64)
            norm("mem")
            for t in range(4):
                if t % 2 == 0:
                    by_feature(t, t, "mem" if t == 0 else None)
                else:
                    by_token(t, t, CW)
            norm("ffn0")
            pe.wait_ge(S["mem_evac"], 4)
            pe.wait_ge(S["zeros_ready"], 1)
            ffn(0, "ffn0")
            norm("ain")

            n0 = tile0["ain"]
            by_token(n0, 6, 2 * AH, "ain")
            for t in range(12):
                if t >= 4:
                    pe.wait_ge(S["ain_evac"], t - 3)
                by_feature(n0 + 1 + t, t % 4)
            pe.wait_ge(S["ain_evac"], 9)
            by_feature(n0 + 13, 0)
            pe.wait_ge(S["ain_evac"], 12)
            pe.wait_ge(S["qm_ready"], 1)
            for j in range(6):
                pe.wait_ge(S["l2_sq"], j + 1)
                f32mm(bank(j), con("ones"), QKS[:, 2 * j:2 * j + 2, :]).then_inc(S["l2_sum"], 1)
            pe.wait_ge(S["decay_g_ready"], 1)
            for tb in range(TB):
                f32mm(PS[:, 6, 64 + AH * tb:64 + AH * tb + AH], con("tri"), GG[:, tb, :])
            for tb in range(TB):
                last = f32mm(PS[:, 6, 96 + AH * tb:96 + AH * tb + AH], con("after"), GG[:, tb, :])
            last.then_inc(S["gcol_ps"], 1)
            pe.wait_ge(S["l2_sd"], 6)
            for src, mat, b0 in ((GG, "tri", 0), (BETA, "ident", 3)):
                if b0:
                    pe.wait_ge(S["beta_ready"], 1)
                for h in range(AH):
                    for tb in range(TB):
                        last = f32mm(PS[:, b0 + h // 2, (h % 2) * SEQ + tb * P:(h % 2) * SEQ + (tb + 1) * P],
                                     src[:, tb, h:h + 1].broadcast_to([P, P]), con(mat))
                    if h % 2:
                        last.then_inc(S["rows_ps"], 1)
            pe.wait_ge(S["silu_done"], 9)
            pe.wait_ge(S["kb_ready"], 3)
            for m in range(TB * AH):
                tb, h = divmod(m, AH)
                last = nc.tensor.transpose(PS[:, 3 + m // 4, (m % 4) * P:(m % 4 + 1) * P], Yv[:, h, tb * P:(tb + 1) * P], con("ident"))
            last.then_inc(S["tok_ps"], 1)
            pe.wait_ge(S["qk_ready"], 6)
            pe.wait_ge(S["rows_sb"], 6)
            for m in range(TB * AH):
                tb, h = divmod(m, AH)
                last = nc.tensor.transpose(PS[:, m // 4, (m % 4) * P:(m % 4 + 1) * P], Yk[:, h, tb * P:(tb + 1) * P], con("ident"))
            last.then_inc(S["tok_ps"], 1)
            pe.wait_ge(S["vb_ready"], 1)
            for m in range(TB * AH):
                tb, h = divmod(m, AH)
                t = slice(tb * P, (tb + 1) * P)
                last = f32mm(PS[:, 3 + m // 4, (m % 4) * P:(m % 4 + 1) * P], Yk[:, h, t], KBT[:, h, t])
            last.then_inc(S["kkt_ps"], 1)
            pe.wait_ge(S["kdec_ready"], 1)
            for m in range(TB * AH):
                tb, h = divmod(m, AH)
                t = slice(tb * P, (tb + 1) * P)
                last = f32mm(PS[:, m // 4, (m % 4) * P:(m % 4 + 1) * P], Yk[:, h, t], Yq[:, h, t])
            last.then_inc(S["qkt_ps"], 1)
            pe.wait_ge(S["lvl_init"], 1)
            for s in range(LEVELS):
                for g in range(3):
                    pe.wait_ge(S["lvl_m"], 3 * s + g + 1)
                    if s:
                        pe.wait_ge(S["lvl_x"], 3 * (s - 1) + g + 1)
                        pe.wait_ge(S["lvl_xt"], 3 * (s - 1) + g + 1)
                    for m in range(4 * g, 4 * g + 4):
                        last = f32mm(PS[:, g, (m % 4) * P:(m % 4 + 1) * P], MT[:, m, :], XM[:, m, :])
                    last.then_inc(S["lvl_p1"], 1)
                for g in range(3):
                    pe.wait_ge(S["lvl_p1sb"], 3 * s + g + 1)
                    if s < LEVELS - 1:
                        for m in range(4 * g, 4 * g + 4):
                            f32mm(PS[:, 3 + g, (m % 4) * P:(m % 4 + 1) * P], XT[:, m, :], P1[:, m, :])
                    for m in range(4 * g, 4 * g + 4):
                        last = f32mm(PS[:, g, (m % 4) * P:(m % 4 + 1) * P], P1[:, m, :], XT[:, m, :])
                    last.then_inc(S["lvl_zt"], 1)
            pe.wait_ge(S["lvl_xt"], 3 * LEVELS)
            pe.wait_ge(S["scaled"], 1)
            for c in range(NCHUNK):
                tb, hf = divmod(c, 2)
                if c:
                    pe.wait_ge(S["s_ready"], c)
                    for h in range(AH):
                        last = f32mm(PS[:, 3 + h // 3, (h % 3) * P:(h % 3 + 1) * P], KBT[:, h, tb * P:(tb + 1) * P], ST[:, h, :])
                    last.then_inc(S["ks_ps"], 1)
                pe.wait_ge(S["r_ready"], c + 1)
                if c:
                    pe.wait_ge(S["vn_sb"], c)
                for h in range(AH):
                    last = f32mm(PS[:, 5 + h // 3, (h % 3) * P:(h % 3 + 1) * P], XT[:, tb * AH + h, :], RR[:, h, :])
                last.then_inc(S["vn_ps"], 1)
                pe.wait_ge(S["vn_sb"], c + 1)
                for h in range(AH):
                    o = PS[:, h // 2, (h % 2) * SEQ + CHUNK * c:(h % 2) * SEQ + CHUNK * (c + 1)]
                    if c:
                        f32mm(o, ST[:, h, :], Yq[:, h, CHUNK * c:CHUNK * (c + 1)], True, False)
                    last = f32mm(o, VN[hf][:, h, :], QD[:, tb * AH + h, CHUNK * hf:CHUNK * (hf + 1)], c == 0, True)
                if c == NCHUNK - 1:
                    last.then_inc(S["o_ps"], 1)
                    break
                for h in range(AH):
                    last = f32mm(PS[:, 3 + h // 3, (h % 3) * P:(h % 3 + 1) * P], KD[:, tb, h, :], VN[hf][:, h, :])
                last.then_inc(S["su_ps"], 1)
            for j in range(3):
                pe.wait_ge(S["o_sq"], j + 1)
                f32mm(bank(3 + j), con("ones"), OSQ[:, 2 * j:2 * j + 2, :]).then_inc(S["o_sum"], 1)
            pe.wait_ge(S["o_sd"], 3)
            attention("mem0")
            out_linear("out0")
            norm("ffn1")
            ffn(1, "ffn1")

            norm("dkv")
            n0 = tile0["dkv"]
            by_feature(n0, 0, "dkv")
            by_feature(n0 + 1, 1, blocks=1, row=P)
            latent(0)
            pe.wait_ge(S["rope_in"], 1)
            f32mm(bank(2, SEQ), con("swap"), KR).then_inc(S["rope_ps"], 1)
            pe.wait_ge(S["lat_ready"], 1)
            pe.wait_ge(S["rope_done"], 1)
            n0 = tile0["ukv"]
            for t in range(2):
                tile_ready(n0 + t)
                for hh in range(3):
                    for kb in range(2):
                        matmul3(PS[:, 4 * t + hh // 2, (hh % 2) * SEQ:(hh % 2 + 1) * SEQ], *w_at(n0 + t, kb * 768 + hh * 2 * P),
                                HH[:, kb, :], HL[:, kb, :], kb == 0, kb == 1)
                    for tb in range(TB):
                        for kb in range(2):
                            q = slice(tb * P, (tb + 1) * P)
                            last = matmul3_tok(PS[:, 4 * t + 2 + tb, hh * P:(hh + 1) * P], HH[:, kb, q], HL[:, kb, q],
                                               *w_at(n0 + t, kb * 768 + hh * 2 * P + P), kb == 0, kb == 1)
                last.then_inc(S["tile_used"], 1)
            pe.wait_ge(S["ukv_evac"], 2)
            norm("ffn2")
            ffn(2, "ffn2")

            norm("bin")
            n0 = tile0["bin"]
            by_feature(n0, 0, "bin")
            by_feature(n0 + 1, 1)
            latent(1)
            pe.wait_ge(S["qm_ready"], 2)
            pe.wait_ge(S["lat_ready"], 2)
            n0 = tile0["uq"]
            for t in range(2):
                tile_ready(n0 + t)
                for hh in range(3):
                    for part in range(2):
                        for kb in range(2):
                            last = matmul3(PS[:, 3 * t + hh, part * SEQ:(part + 1) * SEQ],
                                           *w_at(n0 + t, kb * 768 + (2 * hh + part) * P), HH[:, kb, :], HL[:, kb, :],
                                           kb == 0, kb == 1)
                last.then_inc(S["tile_used"], 1)
            pe.wait_ge(S["uq_evac"], 2)
            for j in range(3):
                f32mm(pairs(bank((6 + j) % 8)), con("swap"), QQ[:, 2 * j:2 * j + 2, 1, :]).then_inc(S["uq_ps"], 1)
            pe.wait_ge(S["rope_done"], 2)
            attention("mem1")
            attention("mla")
            out_linear("out1")
            norm("ffn3")
            ffn(3, "ffn3")
            norm("final")
            norm("in2")

            n0 = tile0["in2"]
            pe.wait_ge(S["table_loaded"], 32)
            pe.wait_ge(S["norm_sd"], norm_no["in2"] + 1)
            for h in range(MH):
                last = f32mm(bank(4 + h), RELB[:, h:h + 1].broadcast_to([32, P]), TABLE[0:32, 0:2 * SEQ])
            last.then_inc(S["bias_ps"], 1)
            for t in range(9):
                if t >= 4:
                    pe.wait_ge(S["in2_evac"], t - 3)
                if t < 8:
                    by_feature(n0 + t, t % 4, "in2" if t == 0 else None)
                else:
                    by_token(n0 + t, t % 4, CW)
            pe.wait_ge(S["bias_row"], 1)
            pe.wait_ge(S["pooled_ready"], 1)
            for b in range(2):
                last = f32mm(bank(4)[:, b * SEQ:(b + 1) * SEQ], par("pool_w", b * P, P), PL[:, b, :])
            last.then_inc(S["pool_ps"], 1)
            pe.wait_ge(S["conf_ready"], 1)
            for b in range(2):
                last = f32mm(bank(5, SEQ), con("ones"), CV[:, b, :], b == 0, b == 1)
            last.then_inc(S["conf_mean_ps"], 1)
            pe.wait_ge(S["in2_evac"], 9)
            pe.wait_ge(S["qk2_sq"], 1)
            for j in range(2):
                last = f32mm(pairs(bank(j)), con("seg32"), ZS[:, 2 * j:2 * j + 2, :])
            last.then_inc(S["qk2_ps"], 1)
            pe.wait_ge(S["conf_sq"], 1)
            for b in range(2):
                last = f32mm(bank(6, SEQ), con("ones"), CVS[:, b, :], b == 0, b == 1)
            last.then_inc(S["conf_var_ps"], 1)
            pe.wait_ge(S["conf_sd"], 1)
            pe.wait_ge(S["pool_ps"], 1)
            pe.wait_ge(S["conf_y"], 1)
            pe.wait_ge(S["qk2_ready"], 1)
            attention("diff")
            pe.wait_ge(S["sub_sq"], 1)
            f32mm(pairs(bank(5)), con("seg64"), CVS).then_inc(S["sub_ps"], 1)
            out_linear("out2")
            norm("ffn4")
            ffn(4, "ffn4")

        @block.gpsimd
        def _(pool):
            step = [0]

            def link(ins):
                step[0] += 1
                ins.then_inc(S["pool_step"], 1)
                pool.wait_ge(S["pool_step"], step[0])

            pool.wait_ge(S["tile_used"], tile0["in2"])
            pool.dma_start(RELB[:, :], d["rel_bias"]).then_inc(S["table_loaded"], 16)
            pool.dma_start(TABLE, d["rel_table"]).then_inc(S["table_loaded"], 16)
            pool.wait_ge(S["bias_row"], 1)
            pool.dma_start(bass.AP(bias_rows, 0, [[ROW + 1, P], [2 * SEQ, MH], [1, 2 * SEQ]]), BROW).then_inc(S["bias_dma"], 16)
            pool.wait_ge(S["bias_dma"], 16)
            for tb in range(TB):
                src = bass.AP(bias_rows, SEQ - 1 - tb * P, [[ROW, P], [2 * SEQ, MH], [1, SEQ]])
                pool.dma_start(BIAS[:, tb, :, :], src).then_inc(S["bias_ready"], 16)
            pool.wait_ge(S["in2_evac"], 3)
            E = SEQ + 16
            link(nc.gpsimd.tensor_tensor(S2[:, :, 2:E], UP[:, :, 2:E], UP[:, :, 1:E - 1], ALU.add))
            link(nc.gpsimd.tensor_tensor(S4[:, :, 4:E], S2[:, :, 4:E], S2[:, :, 2:E - 2], ALU.add))
            link(nc.gpsimd.tensor_tensor(S8[:, :, 8:E], S4[:, :, 8:E], S4[:, :, 4:E - 4], ALU.add))
            link(nc.gpsimd.tensor_tensor(S2[:, 1, 16:E], S8[:, 1, 16:E], S8[:, 1, 8:E - 8], ALU.add))
            for b, rows, src in ((0, slice(0, 64), S2), (0, slice(64, P), S4), (1, slice(0, 64), S8), (1, slice(64, P), S2)):
                lo, hi = CC["inv_win"]
                link(nc.gpsimd.tensor_scalar(PL[rows, b, :], src[rows, b, 16:E], CON[rows, lo + b:lo + b + 1], None, ALU.mult))
                lo, hi = CC["inv_cnt"]
                link(nc.gpsimd.tensor_tensor(PL[rows, b, 0:16], src[rows, b, 16:32], CON[rows, lo + 16 * b:lo + 16 * b + 16], ALU.mult))
            nc.gpsimd.tensor_tensor(PL, PL, UP[:, :, 16:E], ALU.subtract).then_inc(S["pooled_ready"], 1)


def layout(a):
    import numpy as np
    f = np.float32

    def cols(v, n=P):
        return v.reshape(-1, n).T

    def rows(v):
        return np.broadcast_to(v.reshape(1, -1), (P, v.size))

    def taps(w):
        k, n = w.shape
        return w.T.reshape(n // P, P, k).transpose(1, 0, 2).reshape(P, -1)

    pool_w = np.zeros((P, 2, P), f)
    for g in range(4):
        r = slice(64 * (g % 2), 64 * (g % 2) + 64)
        pool_w[r, g // 2, r] = a["pool_w_2"][0, g]
    params = {
        "ffn1_norm0": cols(a["ffn1_norm"][0]), "ffn1_norm1": cols(a["ffn1_norm"][1]),
        "ffn2_norm0": cols(a["ffn2_norm"][0]), "ffn2_norm1": cols(a["ffn2_norm"][1]),
        "mix_norm0": cols(a["mix_norm"][0]), "mix_norm1": cols(a["mix_norm"][1]),
        "mem_norm": cols(a["mem_norm"]), "kv_in_norm": cols(a["kv_in_norm"]), "final_norm": cols(a["final_norm"]),
        "norm1_2": cols(a["norm1_g_2"]), "norm2_2": cols(a["norm2_g_2"]), "b_q_norm": cols(a["b_q_norm"]),
        "kv_lat_norm": cols(a["kv_lat_norm"]), "a_out_norm": cols(a["a_out_norm"]), "a_conv": taps(a["a_conv"][0]),
        "pool_scale": cols(a["pool_scale_2"]), "sconv": taps(a["sconv_w_2"][0]), "conf_w": taps(a["conf_dw_w_2"][0]),
        "conf_b": cols(a["conf_dw_b_2"]), "ln_g": cols(a["conf_ln_g_2"]), "ln_b": cols(a["conf_ln_b_2"]),
        "q_g": np.tile(a["q_norm_g_2"].reshape(-1, 1), (4, 1)), "k_g": np.tile(a["k_norm_g_2"].reshape(-1, 1), (4, 1)),
        "subln": np.tile(a["subln_g_2"].reshape(-1, 1), (2, 1)), "A_log": rows(a["a_A_log"]), "dt_bias": rows(a["a_dt_bias"]),
        "lam": rows(np.concatenate([a[f"lam_{n}_2"].reshape(-1) for n in ("q1", "k1", "q2", "k2")])),
        "pool_w": pool_w.reshape(P, -1),
    }
    j, i = np.arange(P)[:, None], np.arange(P)[None, :]
    same = j // CHUNK == i // CHUNK
    level = np.stack([(i // s % 2 == 1) & (j // s == i // s - 1) for s in (1, 2, 4, 8, 16, 32)], 1)
    window = np.array([2, 4, 8, 16])[(np.arange(2)[None, :] * 2 + np.arange(P)[:, None] // 64)]
    count = np.minimum(np.arange(1, 17)[None, None, :], window[:, :, None])
    q = np.arange(SEQ).reshape(2, P).T
    future = np.arange(SEQ)[None, None, :] // CHUNK > (q // CHUNK)[:, :, None]
    inv = (10000.0 ** -(np.arange(0, ROPE, 2) / ROPE)).astype(f)
    consts = {
        "ident": j == i, "ones": np.ones((P, P)), "seg32": j // 32 == i // 32, "seg64": j // 64 == i // 64,
        "swap": 1.0 * ((j == i - 32) & (i % 64 >= 32)) - 1.0 * ((j == i + 32) & (i % 64 < 32)),
        "tri": same & (j <= i), "after": same & (j > i), "level": level.reshape(P, -1),
        "half": np.arange(P)[:, None] < 64, "inv_win": 1.0 / window, "inv_cnt": (1.0 / count).reshape(P, -1),
        "inv_freq": np.tile(inv, 4).reshape(P, 1), "mla_mask": np.where(future, NEG, 0.0).reshape(P, -1),
    }
    dist = SEQ - 1 - np.arange(2 * SEQ)
    n = np.maximum(dist, 0)
    large = 16 + (np.log(np.maximum(n, 1).astype(f) / f(16)) / f(np.log(8.0)) * f(16)).astype(np.int32)
    bucket = np.where(n < 16, n, np.minimum(large, 31))
    rel_table = np.concatenate([np.arange(P)[:, None] == bucket[None, :],
                                np.broadcast_to(np.where(dist < 0, NEG, 0.0), (P, 2 * SEQ))], 1).astype(f)

    def packed(table, parts):
        assert [(k, v.shape[1]) for k, v in parts.items()] == sorted(table, key=lambda t: list(parts).index(t[0]))
        return np.concatenate([parts[k].astype(f, copy=False) for k, _ in table], 1)

    w_uq = a["b_w_uq"][0].reshape(2 * P, BH, P + ROPE)
    out = {
        "x": a["x"][0].T, "mem": a["mem"][0].T, "positions": np.broadcast_to(a["positions"].reshape(1, SEQ), (P, SEQ)),
        "params": packed(PARAMS, params), "consts": packed(CONSTS, consts), "rel_table": rel_table, "rel_bias": a["rel_bias_2"],
        "w_dkv": np.concatenate([a["w_dkv"], a["w_dkv"][:, 2 * P:]], 1),
        "b_w_uq": np.concatenate([w_uq, w_uq[:, :, P:]], 2).reshape(2 * P, -1),
    }
    for name in ("ffn1_w_gu", "ffn1_w_down", "ffn2_w_gu", "ffn2_w_down", "w_out", "w_mem_kv", "a_w_in", "b_w_in", "w_ukv",
                 "w_in_2", "w_out_2", "w_gate_2", "w_up_2", "w_down_2"):
        out[name] = a[name]
    return {k: np.ascontiguousarray(v) for k, v in out.items()}

def kernel(**inputs):
    import numpy as np
    import concourse.bacc as bacc
    from concourse.bass_utils import run_bass_kernel_spmd

    nc = bacc.Bacc("TRN2", target_bir_lowering=False, num_devices=1)
    arrays = layout({k: np.asarray(v) for k, v in inputs.items()})
    d = {name: nc.dram_tensor(f"in_{name}", a.shape, mybir.dt.from_np(a.dtype), kind="ExternalInput").ap()
         for name, a in arrays.items()}
    out = nc.dram_tensor("out_t", (D, SEQ), mybir.dt.float32, kind="ExternalOutput").ap()
    program(nc, d, out)
    r = run_bass_kernel_spmd(nc, [{f"in_{k}": a for k, a in arrays.items()}], core_ids=[0])
    return np.ascontiguousarray(r.results[0]["out_t"].T).reshape(1, SEQ, D)
```

```python
import concourse.bass as bass
from concourse import mybir
from contextlib import ExitStack

P = 128
SEQ = 256
TB = SEQ // P
D = 1024
KB = D // P
FF = 2816
CW = 256
STEPS = FF // CW
TILE = KB * CW
RING = 3
EPS = 1e-6
NEG = -1e30
CHUNK = 64
NCHUNK = SEQ // CHUNK
AH = 6
BH = 6
MH = 4
LEVELS = 6
ROPE = 64
LAM_INIT = 0.2
TWO_PI = (6.28125, 0.0019350051879882812, 3.0199159819e-07)
ROUND = 12582912.0

PARAMS = [("ffn1_norm0", 8), ("ffn1_norm1", 8), ("ffn2_norm0", 8), ("ffn2_norm1", 8), ("mix_norm0", 8),
          ("mix_norm1", 8), ("mem_norm", 8), ("kv_in_norm", 8), ("final_norm", 8), ("norm1_2", 8),
          ("norm2_2", 8), ("b_q_norm", 2), ("kv_lat_norm", 2), ("a_out_norm", 1), ("a_conv", 72),
          ("pool_scale", 2), ("sconv", 6), ("conf_w", 62), ("conf_b", 2), ("ln_g", 2), ("ln_b", 2),
          ("q_g", 1), ("k_g", 1), ("subln", 1), ("A_log", 6), ("dt_bias", 6), ("lam", 128), ("pool_w", 256)]
CONSTS = [("ident", 128), ("ones", 128), ("seg32", 128), ("seg64", 128), ("swap", 128), ("tri", 128),
          ("after", 128), ("level", LEVELS * 128), ("half", 1), ("inv_win", 2), ("inv_cnt", 32),
          ("inv_freq", 1), ("mla_mask", 512), ("pick", 23)]

SEMS = """x_loaded par_loaded con_loaded mem_loaded down_done w_loaded0 w_loaded1 w_loaded2 w_hi w_split tile_used
x_ready g_scaled h_raw norm_sq norm_ms norm_sd t8_ready hi_ready act_ready zeros_ready pads_ready act_step
dve_step pool_step mem_evac sg_ready glu_free h_hi h_ready ain_evac conv_done silu_done l2_sq l2_sum l2_sd
qk_ready ba_ready g_shifted l2_rc o_rc o_bc l2_bc o_gated beta_rows g_softplus beta_ready decay_g_ready
gcol_ps rows_ps gcol_sb rows_sb kb_ready d_pre d_exp kkt_ps qkt_ps qd_ready tok_ps vb_ready kdec_ready lvl_m
lvl_p1 lvl_p1sb lvl_x lvl_zt lvl_xt vn_zeroed qm_ready pos_loaded att_done table_loaded scaled ks_ps r_ready
vn_ps vn_sb su_ps s_ready o_ps o_sb o_sq o_sum o_sd att_s att_nm att_e att_p att_t att_pt att_o att_oe lat_sb
lat_sq lat_sum lat_sd lat_f lat_hi lat_ready rope_in rope_ps rope_done rope_ang rope_tab ukv_evac uq_ps
uq_evac in2_evac pooled_ready pool_ps conf_ready conf_pool conf_in conf_mean_ps conf_mean conf_xc conf_sq
conf_var_ps conf_sd conf_y conf_out qk2_sq qk2_ps qk2_sd qk2_ready lam_prod lam_exp bias_ps bias_row bias_dma
bias_ready sub_sq sub_ps sub_sd out_done""".split()


def columns(table):
    at, where = 0, {}
    for name, width in table:
        where[name] = (at, at + width)
        at += width
    return where, at


PHASES = [("ffn0", 33), ("mem", 4), ("ain", 14), ("out0", 4), ("ffn1", 33), ("dkv", 2), ("ukv", 2),
          ("ffn2", 33), ("bin", 2), ("uq", 2), ("out1", 4), ("ffn3", 33), ("in2", 9), ("out2", 4), ("ffn4", 33)]
VERSIONS = ["ffn0", "mem", "ain", "out0", "ffn1", "dkv", "ffn2", "bin", "out1", "ffn3", "in2", "out2", "ffn4"]
NORMS = ["ffn0", "mem", "ain", "ffn1", "dkv", "ffn2", "bin", "ffn3", "final", "in2", "ffn4"]
NORM_GAIN = ["ffn1_norm0", "mem_norm", "mix_norm0", "ffn2_norm0", "kv_in_norm", "ffn1_norm1", "mix_norm1",
             "ffn2_norm1", "final_norm", "norm1_2", "norm2_2"]
IN2_ORDER = [4, 5, 0, 1, 2, 3, 6, 7, 8]
POOL_TAP = 18
ADEPTH = 3
ATT = [("mem0", "mem", MH), ("mem1", "mem", MH), ("mla", "mla", BH), ("diff", "diff", MH)]


def program(nc, d, out):
    f32, f32r, bf16, i32 = mybir.dt.float32, mybir.dt.float32r, mybir.dt.bfloat16, mybir.dt.int32
    ACT, ALU, AX = mybir.ActivationFunctionType, mybir.AluOpType, mybir.AxisListType
    PC, n_par = columns(PARAMS)
    CC, n_con = columns(CONSTS)
    tile0, n_tiles = {}, 0
    for name, n in PHASES:
        tile0[name] = n_tiles
        n_tiles += n
    version = {name: v for v, name in enumerate(VERSIONS)}
    norm_no = {name: k for k, name in enumerate(NORMS)}
    x_no = {name: k for k, name in enumerate(n for n in NORMS if n != "mem")}
    free_at = {}
    ends = {name: tile0[name] + n for name, n in PHASES}
    for before, name in zip(VERSIONS, VERSIONS[1:]):
        free_at[name] = ends[before] - (2 if before.startswith("ffn") else 0)

    ROW = MH * 2 * SEQ
    bias_rows = nc.dram_tensor("bias_rows", [P * (ROW + 1)], f32, kind="Internal")

    with ExitStack() as ctx:
        enter = ctx.enter_context

        def sb(name, shape, dt=f32):
            return enter(nc.sbuf_tensor(name, shape, dt))

        S = {n: enter(nc.semaphore(n)) for n in SEMS}
        w_loaded = [S["w_loaded0"], S["w_loaded1"], S["w_loaded2"]]

        RAW = sb("w_raw", [P, RING, TILE])
        WH = sb("w_hi_part", [P, RING, TILE], f32r)
        WL = sb("w_lo_part", [P, RING, TILE], f32r)
        X = sb("x_res", [P, KB, SEQ])
        T8 = sb("t8", [P, KB, SEQ])
        XH = sb("x_hi", [P, KB, SEQ], f32r)
        XL = sb("x_lo", [P, KB, SEQ], f32r)
        HH = sb("h_hi_part", [P, 4, SEQ], f32r)
        HL = sb("h_lo_part", [P, 4, SEQ], f32r)
        PAR = sb("params", [P, n_par])
        CON = sb("consts", [P, n_con])
        ZB = sb("zeros_bf", [P, 512], bf16)
        SD = sb("norm_dev", [P, SEQ])
        RS = sb("norm_rs", [P, SEQ])
        MEM_K = [sb(f"mem_k{l}", [P, 2, SEQ]) for l in range(2)]
        MEM_V = [sb(f"mem_v{l}", [P, TB, 2 * P]) for l in range(2)]
        QM = sb("mem_q", [P, 2, SEQ])
        SMALL = sb("small", [P, 128])
        ATTS = sb("att_small", [P, 64])
        LAMP = sb("lam_products", [P, 2, 32])
        RELB = sb("rel_bias", [32, MH])
        AR_N = 17 * 1024
        AR = sb("arena", [P, AR_N])
        PS = enter(nc.psum_tensor("ps", [P, 8, 512], f32))

        def par(name, a=0, n=None):
            lo, hi = PC[name]
            return PAR[:, lo + a:(hi if n is None else lo + a + n)]

        def con(name, a=0, n=None):
            lo, hi = CC[name]
            return CON[:, lo + a:(hi if n is None else lo + a + n)]

        def area(at, *dims):
            n = 1
            for x in dims:
                n *= x
            assert at + n <= AR_N, (at, dims)
            v = AR[:, at:at + n]
            if len(dims) == 2:
                v = v.rearrange("p (a b) -> p a b", b=dims[1])
            if len(dims) == 3:
                v = v.rearrange("p (a b c) -> p a b c", b=dims[1], c=dims[2])
            return v

        def bank(b, w=512):
            return PS[:, b, 0:w]

        def pairs(v):
            return v.rearrange("p (a b) -> p a b", b=SEQ)

        def pick(j, n):
            return con("pick", 11 - j, n)

        def spread(j, n):
            return con("ident")[0:n, j:j + 1].broadcast_to([n, P])

        def over(v, n):
            return v.unsqueeze(1).broadcast_to([v.shape[0], n, v.shape[1]])

        U = AH * SEQ
        SQ = area(AR_N - KB * SEQ, KB, SEQ)
        MEMT = area(4 * SEQ, KB, SEQ)
        SG = area(0, 2, SEQ)
        HF = area(2 * SEQ, 2, SEQ)
        PAD = 3
        YQKV = area(0, 18, SEQ)
        Yq, Yk, Yv = (area(i * U, AH, SEQ) for i in range(3))
        CB = area(3 * U, 18, SEQ + PAD)
        KBT = area(3 * U, AH, SEQ)
        GROW = area(3 * U + 18 * (SEQ + PAD) + 10 + 2 * U, AH, SEQ)
        SPLIT0 = 3 * U + 18 * (SEQ + PAD) + 10
        QKS = area(SPLIT0, 12, SEQ)
        EGROW = area(SPLIT0 + 3 * U, AH, SEQ)
        BETAROW = area(SPLIT0 + 4 * U, AH, SEQ)
        VB = area(SPLIT0, TB, AH, P)
        KD = area(SPLIT0 + U, TB, AH, P)
        LT = area(SPLIT0 + 2 * U, TB * AH, P)
        XT = area(5 * U, TB * AH, P)
        MT = area(SPLIT0 + 4 * U, TB * AH, P)
        DT = area(2 * U, TB * AH, P)
        QD = area(4 * U, TB * AH, P)
        XM = area(U, TB * AH, P)
        P1 = area(2 * U, TB * AH, P)
        ST = area(U, AH, P)
        RR = area(U + AH * P, AH, P)
        VN = [area(SPLIT0 + 4 * U + h * AH * P, AH, P) for h in range(2)]
        OB = area(2 * U, AH, SEQ)
        OSQ = area(SPLIT0 + 2 * U, AH, SEQ)
        KN = area(4 * SEQ, BH, SEQ)
        VM = area(4 * SEQ + U, TB, BH, P)
        KR = area(4 * SEQ + 2 * U, SEQ)
        COS = area(5 * SEQ + 2 * U, SEQ)
        SIN = area(6 * SEQ + 2 * U, SEQ)
        LATE = 7 * SEQ + 2 * U
        LAT = area(LATE, 2, SEQ)
        LSQ = area(LATE + 2 * SEQ, 2, SEQ)
        QQ = area(LATE + 4 * SEQ, BH, 2, SEQ)
        ROT = area(LATE + 4 * SEQ + 2 * U, BH, SEQ)
        UP = area(0, 2, SEQ + 16)
        S2 = area(544, 2, SEQ + 16)
        S4 = area(1088, 2, SEQ + 16)
        S8 = area(1632, 2, SEQ + 16)
        PL = area(2176, 2, SEQ)
        SB_, SC_, SH_, CA_, CG_ = (area(2688 + 512 * i, 2, SEQ) for i in range(5))
        CS = area(5248, 2, SEQ + 2)
        CC_ = area(5764, 2, SEQ + 30)
        CV = area(6336, 2, SEQ)
        ZQ = area(6848, 4, SEQ)
        ZS = area(7872, 4, SEQ)
        ZV = area(8896, TB, 2 * P)
        XC = area(9408, 2, SEQ)
        CVS = area(9920, 2, SEQ)
        MN = area(10432, SEQ)
        BIAS = area(10688, TB, MH, SEQ)
        TABLE = area(10688, 2 * 2 * SEQ)
        BROW = area(11712, MH, 2 * SEQ)
        ATT_AT = {"mem0": 0, "mem1": LATE + 4 * SEQ + 3 * U, "mla": LATE + 4 * SEQ + 3 * U, "diff": 12736}

        def att_work(phase):
            at = ATT_AT[phase]
            sc = [[area(at + (2 * q + m) * 512, 2, SEQ) for m in range(2)] for q in range(ADEPTH)]
            pt = [area(at + 1024 * ADEPTH + q * 512, 2, SEQ) for q in range(2)]
            return sc, pt

        def loops_of(name):
            return (STEPS - 1) // 2 - (tile0[name] + 33 == n_tiles)

        def ffn_scale(name):
            return 1.0 if name == "ffn4" else 0.5

        BA = SMALL[:, 0:24].rearrange("p (a b) -> p a b", a=TB)
        BETA, GG, G1, G2, GC, ED = (SMALL[:, 24 + 12 * k:36 + 12 * k].rearrange("p (a b) -> p a b", a=TB) for k in range(6))
        EA = SMALL[:, 96:102]
        LAMS, LAM2, NLAM = SMALL[:, 104:106], SMALL[:, 106:108], SMALL[:, 108:109]
        POSI = area(LATE + 4 * SEQ, SEQ).bitcast(i32)
        ANG, TURN, ANG_S, ANG_C = (area(LATE + 5 * SEQ + k * SEQ, SEQ) for k in range(4))
        PI, PI_IN = 3.141592653589793, 3.1415925
        MEM_SCALE, MLA_SCALE, DIFF_SCALE = 64 ** -0.5, (P + ROPE) ** -0.5, 32 ** -0.5

        MEM_BANK = (4, 5, 6, 4)
        ROW_BANK = (4, 5, 7)
        KLEN_BANK, QLEN_BANK, KTOK_BANK, QK_BANK, KK_BANK = (1, 2, 3), (0, 6, 7), (1, 2, 3), (0, 6, 7), (4, 5, 1)
        def s_bank(maps, u, m):
            return maps * (u % ADEPTH) + m

        def t_bank(maps, u):
            return 4 + u % 2 if maps == 1 else 6

        def o_bank(maps, g):
            return 6 + g % 2 if maps == 1 else 7

        def stat(k, u, m):
            at = 4 * ADEPTH * k + 4 * (u % ADEPTH) + TB * m
            return ATTS[:, at:at + TB]

        def MX(u, m):
            return stat(0, u, m)

        def NM2(u, m):
            return stat(1, u, m)

        def NM(u, m, q):
            return stat(1, u, m)[:, q:q + 1]

        def SUM2(u, m):
            return stat(2, u, m)

        def SUM(u, m, q):
            return stat(2, u, m)[:, q:q + 1]

        def RC2(u, m):
            return stat(3, u, m)

        def RC(u, m, q):
            return stat(3, u, m)[:, q:q + 1]

        att0, att_of, u, m, g = {}, {}, 0, 0, 0
        for ph, kind, n in ATT:
            att0[ph], att_of[ph] = (u, m, g), (kind, n)
            u, m, g = u + n, m + n * (2 if kind == "diff" else 1), g + (n if kind == "mla" else n // 2)

        def matmul3(o, w_hi, w_lo, a_hi, a_lo, start, stop):
            nc.tensor.matmul(o, w_hi, a_hi, start=start, stop=False, skip_group_check=True)
            nc.tensor.matmul(o, w_hi, a_lo, start=False, stop=False, skip_group_check=True)
            return nc.tensor.matmul(o, w_lo, a_hi, start=False, stop=stop, skip_group_check=True)

        def width(n):
            if n == tile0["ain"]:
                return KB * 2 * AH
            if n == tile0["dkv"] + 1:
                return KB * P
            if tile0["ukv"] <= n < tile0["ukv"] + 2 or tile0["uq"] <= n < tile0["uq"] + 2:
                return 2 * 768
            return TILE

        block = enter(nc.Block())

        @block.sync
        def _(sp):
            def slot_free(n, more=0):
                if n >= RING or not isinstance(more, int):
                    sp.wait_ge(S["w_split"], n - RING + 1 + more)

            def load(n, src, kb, cols):
                slot_free(n)
                dst = RAW[:, n % RING, 0:kb * cols].rearrange("p (k c) -> p k c", c=cols)
                sp.dma_start(dst, src).then_inc(w_loaded[n % RING], 16)

            def wide(w):
                return w.rearrange("(k p) n -> p k n", p=P)

            def load_columns(n0, w, start, count):
                v = wide(w)
                for t in range(count):
                    load(n0 + t, v[:, :, start + t * CW:start + (t + 1) * CW], KB, CW)

            def load_ffn(name, w_gate, gate_at, w_up, up_at, w_down):
                n0 = tile0[name]
                wg, wu = wide(w_gate), wide(w_up)
                wd = w_down.rearrange("(s j p) n -> s p j n", j=2, p=P)
                load(n0, wg[:, :, gate_at:gate_at + CW], KB, CW)
                load(n0 + 1, wu[:, :, up_at:up_at + CW], KB, CW)
                def two_steps(i):
                    for j in range(2):
                        n = n0 + 2 + 3 * j
                        at = i * (2 * CW) + (j + 1) * CW
                        for k in range(3):
                            m = n + k
                            slot_free(m, i * 6)
                            dst = RAW[:, m % RING, :]
                            if k < 2:
                                src = (wg, wu)[k][:, :, bass.ds((gate_at, up_at)[k] + at, CW)]
                                dst = dst.rearrange("p (k c) -> p k c", c=CW)
                            else:
                                src = wd[bass.ds(i * 2 + j, 1), :, :, :].rearrange("s p j n -> p (s j) n")
                                dst = dst.rearrange("p (k c) -> p k c", c=D)
                            sp.dma_start(dst, src).then_inc(w_loaded[m % RING], 16)

                first = 1 if n0 == 0 else 0
                if first:
                    two_steps(0)
                with nc.sync.Fori(first, (STEPS - 1) // 2) as i:
                    two_steps(i)
                load(n0 + 32, wd[STEPS - 1], 2, D)

            load_ffn("ffn0", d["ffn1_w_gu"][0], 0, d["ffn1_w_gu"][0], FF, d["ffn1_w_down"][0])
            for l in range(2):
                load_columns(tile0["mem"] + 2 * l, d["w_mem_kv"][l], 0, 2)
            n = tile0["ain"]
            w = d["a_w_in"][0]
            load(n, wide(w)[:, :, 4 * AH * P:4 * AH * P + 2 * AH], KB, 2 * AH)
            load_columns(n + 1, w, 0, 12)
            load_columns(n + 13, w, 4 * AH * P + 2 * AH, 1)
            load_columns(tile0["out0"], d["w_out"][0], 0, 4)
            load_ffn("ffn1", d["ffn2_w_gu"][0], 0, d["ffn2_w_gu"][0], FF, d["ffn2_w_down"][0])
            load_columns(tile0["dkv"], d["w_dkv"], 0, 1)
            load(tile0["dkv"] + 1, wide(d["w_dkv"])[:, :, CW:CW + P], KB, P)
            for t in range(2):
                load(tile0["ukv"] + t, wide(d["w_ukv"])[:, :, t * 768:(t + 1) * 768], 2, 768)
            load_ffn("ffn2", d["ffn1_w_gu"][1], 0, d["ffn1_w_gu"][1], FF, d["ffn1_w_down"][1])
            load_columns(tile0["bin"], d["b_w_in"][0], 0, 2)
            for t in range(2):
                load(tile0["uq"] + t, wide(d["b_w_uq"])[:, :, t * 768:(t + 1) * 768], 2, 768)
            load_columns(tile0["out1"], d["w_out"][1], 0, 4)
            load_ffn("ffn3", d["ffn2_w_gu"][1], 0, d["ffn2_w_gu"][1], FF, d["ffn2_w_down"][1])
            for t, part in enumerate(IN2_ORDER):
                load(tile0["in2"] + t, wide(d["w_in_2"][0])[:, :, part * CW:(part + 1) * CW], KB, CW)
            load_columns(tile0["out2"], d["w_out_2"][0], 0, 4)
            load_ffn("ffn4", d["w_gate_2"][0], 0, d["w_up_2"][0], 0, d["w_down_2"][0])
            for p in range(4):
                sp.wait_ge(S["x_ready"], 4 * len(x_no) + p + 1)
                sp.dma_start(out.rearrange("(k p) t -> p k t", p=P)[:, 2 * p:2 * p + 2, :],
                             X[:, 2 * p:2 * p + 2, :]).then_inc(S["out_done"], 16)
            sp.wait_ge(S["out_done"], 64)

        @block.scalar
        def _(act):
            step = [0]

            def link(ins):
                step[0] += 1
                ins.then_inc(S["act_step"], 1)
                act.wait_ge(S["act_step"], step[0])

            def w_hi(n, i=None):
                if n >= n_tiles:
                    return
                turn = 0 if i is None else i * 6
                act.wait_ge(w_loaded[n % RING], 16 * (n // RING + 1) + (0 if i is None else i * 32))
                if n >= RING:
                    act.wait_ge(S["tile_used"], n - RING + 1 + turn)
                w = width(n)
                nc.scalar.activation(WH[:, n % RING, 0:w], RAW[:, n % RING, 0:w], ACT.Copy).then_inc(S["w_hi"], 1)

            def square(name, p, src=X):
                if name != "mem":
                    act.wait_ge(S["x_ready"], 4 * x_no[name] + p + 1)
                nc.scalar.activation(SQ[:, 2 * p:2 * p + 2, :], src[:, 2 * p:2 * p + 2, :],
                                     ACT.Square).then_inc(S["norm_sq"], 1)

            def deviation(name):
                act.wait_ge(S["norm_ms"], norm_no[name] + 1)
                nc.scalar.activation(SD[:, :], bank(7, SEQ), ACT.Sqrt, bias=EPS, scale=1.0 / D).then_inc(S["norm_sd"], 1)

            def norm(name, src=X):
                for p in range(4):
                    square(name, p, src)
                deviation(name)

            def operand_hi(name, deferred=False):
                v = version[name]
                if v:
                    act.wait_ge(S["tile_used"], free_at[name])
                for p in range(4):
                    if deferred:
                        square(name, p)
                    act.wait_ge(S["t8_ready"], 4 * v + p + 1)
                    nc.scalar.activation(XH[:, 2 * p:2 * p + 2, :], T8[:, 2 * p:2 * p + 2, :],
                                         ACT.Copy).then_inc(S["hi_ready"], 1)

            def ffn(f, name, before=None):
                n0 = tile0[name]

                def gate(s, i=None):
                    turn = 0 if i is None else i * 2
                    act.wait_ge(S["g_scaled"], STEPS * f + s + 1 + turn)
                    nc.scalar.activation(SG, SG, ACT.Silu).then_inc(S["sg_ready"], 1)

                def hidden_hi(s, i=None):
                    turn = 0 if i is None else i * 2
                    act.wait_ge(S["h_raw"], STEPS * f + s + 1 + turn)
                    nc.scalar.activation(HH[:, 2 * (s % 2):2 * (s % 2) + 2, :], HF, ACT.Copy).then_inc(S["h_hi"], 1)

                def one(s, i=None):
                    w_hi(n0 + 3 * s + 2, i)
                    gate(s, i)
                    w_hi(n0 + 3 * s + 3, i)
                    hidden_hi(s, i)
                    w_hi(n0 + 3 * s + 4, i)

                w_hi(n0 + 3)
                deviation(name)
                gate(0)
                hidden_hi(0)
                w_hi(n0 + 4)
                loops = loops_of(name)
                if before:
                    before()
                with nc.scalar.Fori(0, loops) as i:
                    one(1, i)
                    one(2, i)
                for s in range(2 * loops + 1, STEPS):
                    one(s)

            def out_linear(name):
                for t in range(4):
                    w_hi(tile0[name] + t + RING)

            def attention(ph):
                u0, m0, g0 = att0[ph]
                kind, n = att_of[ph]
                maps = 2 if kind == "diff" else 1
                sc, pt = att_work(ph)
                for u in range(n + 1):
                    if u < n:
                        for m in range(maps):
                            act.wait_ge(S["att_nm"], m0 + u * maps + m + 1)
                            if u >= ADEPTH and kind == "mem":
                                act.wait_ge(S["att_t"], u0 + u - ADEPTH + 1)
                            for q in range(TB):
                                src = PS[:, s_bank(maps, u, m), q * SEQ:(q + 1) * SEQ] if kind == "mem" else sc[u % ADEPTH][m][:, q, :]
                                last = nc.scalar.activation(
                                    sc[u % ADEPTH][m][:, q, :], src, ACT.Exp, bias=NM(u, m, q),
                                    scale=(MEM_SCALE if kind == "mem" else 1.0), accum_out=SUM(u, m, q))
                            last.then_inc(S["att_e"], 1)
                    if u >= 1:
                        act.wait_ge(S["att_t"], u0 + u)
                        nc.scalar.activation(pt[(u - 1) % 2], pairs(bank(t_bank(maps, u - 1))), ACT.Copy).then_inc(S["att_pt"], 1)

            def latent(r, n):
                act.wait_ge(S["lat_sb"], r + 1)
                nc.scalar.activation(LSQ, LAT, ACT.Square).then_inc(S["lat_sq"], 1)

            def latent_rest(r):
                act.wait_ge(S["lat_sum"], r + 1)
                nc.scalar.activation(SD[:, :], bank(7, SEQ), ACT.Sqrt, bias=EPS, scale=1.0 / (2 * P)).then_inc(S["lat_sd"], 1)
                act.wait_ge(S["lat_f"], r + 1)
                nc.scalar.activation(HH[:, 0:2, :], LAT, ACT.Copy).then_inc(S["lat_hi"], 1)

            act.dma_start(X[:, :, :], d["x"].rearrange("(k p) t -> p k t", p=P)).then_inc(S["x_loaded"], 16)
            act.dma_start(PAR[:, :], d["params"]).then_inc(S["par_loaded"], 16)
            act.dma_start(CON[:, :], d["consts"]).then_inc(S["con_loaded"], 16)
            act.dma_start(MEMT, d["mem"].rearrange("(k p) t -> p k t", p=P)).then_inc(S["mem_loaded"], 16)
            w_hi(0)
            operand_hi("ffn0", True)
            w_hi(1)
            w_hi(2)

            def mem_squares():
                act.wait_ge(S["mem_loaded"], 16)
                for p in range(4):
                    square("mem", p, MEMT)

            ffn(0, "ffn0", mem_squares)

            deviation("mem")
            operand_hi("mem")
            w_hi(tile0["mem"] + 2)
            for p in range(4):
                square("ain", p)
            n0 = tile0["mem"]
            for t in range(4):
                act.wait_ge(S["tile_used"], n0 + t + 1)
                dst = (MEM_K, MEM_V)[t % 2][t // 2]
                nc.scalar.activation(dst[:, :, :], pairs(bank(MEM_BANK[t])), ACT.Copy).then_inc(S["mem_evac"], 1)
                w_hi(n0 + t + RING)
                if t == 0:
                    deviation("ain")
            operand_hi("ain")

            n0 = tile0["ain"]
            act.wait_ge(S["tile_used"], n0 + 1)
            nc.scalar.activation(BA, PS[:, 6, 0:TB * 2 * AH].rearrange("p (a b) -> p a b", a=TB), ACT.Copy).then_inc(S["ba_ready"], 1)
            w_hi(n0 + RING)

            def silu_block(j):
                act.wait_ge(S["conv_done"], j + 1)
                v = YQKV[:, 2 * j:2 * j + 2, :]
                nc.scalar.activation(v, v, ACT.Silu).then_inc(S["silu_done"], 1)

            for t in range(9):
                act.wait_ge(S["tile_used"], n0 + t + 2)
                if t == 0:
                    act.wait_ge(S["pads_ready"], 1)
                nc.scalar.activation(CB[:, 2 * t:2 * t + 2, PAD:PAD + SEQ], pairs(bank(t % 4)), ACT.Copy).then_inc(S["ain_evac"], 1)
                w_hi(n0 + t + 1 + RING)
                if t == 0:
                    act.wait_ge(S["ba_ready"], 1)
                    nc.scalar.activation(EA, par("A_log"), ACT.Exp)
                    nc.scalar.activation(BETA, BA[:, :, 0:AH], ACT.Exp, scale=-1.0)
                    act.wait_ge(S["g_shifted"], 1)
                    link(nc.scalar.activation(G2, G1, ACT.Abs))
                    link(nc.scalar.activation(G2, G2, ACT.Exp, scale=-1.0))
                    nc.scalar.activation(G2, G2, ACT.Ln, bias=1.0).then_inc(S["g_softplus"], 1)
                else:
                    silu_block(t - 1)
                if t == 3:
                    act.wait_ge(S["gcol_ps"], 1)
                    nc.scalar.activation(GC, PS[:, 6, 64:76].rearrange("p (a b) -> p a b", a=TB), ACT.Copy).then_inc(S["gcol_sb"], 1)
                    nc.scalar.activation(ED, PS[:, 6, 96:108].rearrange("p (a b) -> p a b", a=TB), ACT.Exp)
                    for j in range(3):
                        act.wait_ge(S["rows_ps"], j + 1)
                        nc.scalar.activation(EGROW[:, 2 * j:2 * j + 2, :], pairs(bank(ROW_BANK[j])), ACT.Exp).then_inc(S["rows_sb"], 1)
                    for j in range(3):
                        nc.scalar.activation(GROW[:, 2 * j:2 * j + 2, :], pairs(bank(ROW_BANK[j])), ACT.Copy).then_inc(S["rows_sb"], 1)
                if t == 5:
                    for j in range(3):
                        act.wait_ge(S["rows_ps"], 4 + j)
                        nc.scalar.activation(BETAROW[:, 2 * j:2 * j + 2, :], pairs(bank(ROW_BANK[j])), ACT.Copy).then_inc(S["beta_rows"], 1)
                if t >= 7:
                    for j in range(3 * (t - 7), 3 * (t - 7) + 3):
                        act.wait_ge(S["silu_done"], j + 1)
                        nc.scalar.activation(QKS[:, 2 * j:2 * j + 2, :], YQKV[:, 2 * j:2 * j + 2, :], ACT.Square).then_inc(S["l2_sq"], 1)
            for t in range(9, 12):
                act.wait_ge(S["tile_used"], n0 + t + 2)
                nc.scalar.activation(T8[:, 2 * (t - 9):2 * (t - 9) + 2, :], pairs(bank(t % 4)), ACT.Silu).then_inc(S["ain_evac"], 1)
                w_hi(n0 + t + 1 + RING)
                if t == 9:
                    silu_block(8)
                if t == 10:
                    act.wait_ge(S["l2_sum"], 1)
                    nc.scalar.activation(SD[0:2 * AH, :], PS[0:2 * AH, 6, SEQ:2 * SEQ], ACT.Sqrt, bias=EPS).then_inc(S["l2_sd"], 1)
            act.wait_ge(S["d_pre"], 1)
            nc.scalar.activation(DT, DT, ACT.Exp).then_inc(S["d_exp"], 1)
            act.wait_ge(S["tile_used"], n0 + 14)
            nc.scalar.activation(QM[:, :, :], pairs(bank(0)), ACT.Copy).then_inc(S["qm_ready"], 1)
            w_hi(n0 + 13 + RING)
            act.wait_ge(S["tok_ps"], 2)
            for m in range(TB * AH):
                tb, h = divmod(m, AH)
                last = nc.scalar.activation(KD[:, tb, h, :], PS[:, KTOK_BANK[m // 4], (m % 4) * P:(m % 4 + 1) * P], ACT.Copy,
                                            scale=ED[:, tb, h:h + 1])
            last.then_inc(S["kdec_ready"], 1)
            act.wait_ge(S["qd_ready"], 1)
            for s in range(1, LEVELS):
                for g in range(3):
                    act.wait_ge(S["lvl_p1"], 3 * s + g + 1)
                    if s > 1:
                        act.wait_ge(S["lvl_zt"], 3 * (s - 2) + g + 1)
                    nc.scalar.activation(P1[:, 4 * g:4 * g + 4, :], bank(g).rearrange("p (a b) -> p a b", b=P),
                                         ACT.Copy).then_inc(S["lvl_p1sb"], 1)
            for c in range(NCHUNK):
                r = slice(CHUNK * (c % 2), CHUNK * (c % 2) + CHUNK)
                act.wait_ge(S["vn_ps"], c + 1)
                if c == 0:
                    act.wait_ge(S["vn_zeroed"], 1)
                for b in range(2):
                    last = nc.scalar.activation(VN[c % 2][r, 3 * b:3 * b + 3, :],
                                                PS[r, 5 + b, 0:3 * P].rearrange("p (a b) -> p a b", b=P), ACT.Copy)
                last.then_inc(S["vn_sb"], 1)
            act.wait_ge(S["o_ps"], 1)
            for j in range(3):
                nc.scalar.activation(OB[:, 2 * j:2 * j + 2, :], pairs(bank(j)), ACT.Copy).then_inc(S["o_sb"], 1)
                nc.scalar.activation(OSQ[:, 2 * j:2 * j + 2, :], pairs(bank(j)), ACT.Square).then_inc(S["o_sq"], 1)
            act.wait_ge(S["o_sum"], 1)
            nc.scalar.activation(SD[0:AH, :], PS[0:AH, 6, 0:SEQ], ACT.Sqrt, bias=EPS, scale=1.0 / P).then_inc(S["o_sd"], 1)
            attention("mem0")
            operand_hi("out0")
            out_linear("out0")
            operand_hi("ffn1", True)
            act.dma_start(POSI, d["positions"]).then_inc(S["pos_loaded"], 16)

            def sines():
                act.wait_ge(S["rope_ang"], 1)
                nc.scalar.activation(SIN, ANG_S, ACT.Sin).then_inc(S["rope_tab"], 1)
                nc.scalar.activation(COS, ANG_C, ACT.Sin).then_inc(S["rope_tab"], 1)

            ffn(1, "ffn1", sines)

            operand_hi("dkv", True)
            w_hi(tile0["dkv"] + 2)
            n0 = tile0["dkv"]
            deviation("dkv")
            w_hi(n0 + RING)
            latent(0, n0)
            w_hi(n0 + 1 + RING)
            latent_rest(0)
            n0 = tile0["ukv"]
            for t in range(2):
                act.wait_ge(S["tile_used"], n0 + t + 1)
                nc.scalar.activation(KN[:, 3 * t:3 * t + 2, :], pairs(bank(4 * t)), ACT.Copy)
                nc.scalar.activation(KN[:, 3 * t + 2, :], bank(4 * t + 1, SEQ), ACT.Copy)
                for tb in range(TB):
                    last = nc.scalar.activation(VM[:, tb, 3 * t:3 * t + 3, :],
                                                bank(4 * t + 2 + tb, 3 * P).rearrange("p (a b) -> p a b", b=P), ACT.Copy)
                last.then_inc(S["ukv_evac"], 1)
                w_hi(n0 + t + RING)
            operand_hi("ffn2", True)
            ffn(2, "ffn2")

            operand_hi("bin", True)
            w_hi(tile0["bin"] + 2)
            n0 = tile0["bin"]
            deviation("bin")
            w_hi(n0 + RING)
            latent(1, n0)
            w_hi(n0 + 1 + RING)
            latent_rest(1)
            n0 = tile0["uq"]
            for t in range(2):
                act.wait_ge(S["tile_used"], n0 + t + 1)
                nc.scalar.activation(QQ[:, 3 * t:3 * t + 3, :, :].rearrange("p a b c -> p a (b c)"),
                                     PS[:, 3 * t:3 * t + 3, :], ACT.Copy).then_inc(S["uq_evac"], 1)
                w_hi(n0 + t + RING)
            attention("mem1")
            attention("mla")
            operand_hi("out1")
            out_linear("out1")
            operand_hi("ffn3", True)
            ffn(3, "ffn3")
            norm("final")
            norm("in2")
            operand_hi("in2")
            w_hi(tile0["in2"] + 2)

            n0 = tile0["in2"]
            dst = [CA_, CG_, UP[:, :, 16:16 + SEQ], SB_, SC_, SH_, ZQ[:, 0:2, :], ZQ[:, 2:4, :], ZV]
            act.wait_ge(S["pads_ready"], 2)
            for t in range(9):
                act.wait_ge(S["tile_used"], n0 + t + 1)
                nc.scalar.activation(dst[t], pairs(bank(t % 4)), ACT.Sigmoid if t == 1 else ACT.Copy).then_inc(S["in2_evac"], 1)
                w_hi(n0 + t + RING)
            act.wait_ge(S["in2_evac"], 9)
            nc.scalar.activation(ZS, ZQ, ACT.Square).then_inc(S["qk2_sq"], 1)
            act.wait_ge(S["qk2_ps"], 1)
            nc.scalar.activation(ZS, PS[:, 0:2, :].rearrange("p a (b c) -> p (a b) c", c=SEQ), ACT.Sqrt, bias=EPS,
                                 scale=1.0 / 32).then_inc(S["qk2_sd"], 1)
            act.wait_ge(S["conf_mean_ps"], 1)
            nc.scalar.activation(MN, bank(5, SEQ), ACT.Copy, scale=1.0 / (2 * P)).then_inc(S["conf_mean"], 1)
            act.wait_ge(S["conf_xc"], 1)
            nc.scalar.activation(CVS, XC, ACT.Square).then_inc(S["conf_sq"], 1)
            act.wait_ge(S["conf_var_ps"], 1)
            nc.scalar.activation(SD[:, :], bank(6, SEQ), ACT.Sqrt, bias=EPS, scale=1.0 / (2 * P)).then_inc(S["conf_sd"], 1)
            act.wait_ge(S["lam_prod"], 1)
            nc.scalar.activation(LAM2, LAMS, ACT.Exp).then_inc(S["lam_exp"], 1)
            act.wait_ge(S["conf_y"], 1)
            for b in range(2):
                nc.scalar.activation(T8[:, 4 + b, :], XC[:, b, :], ACT.Silu, bias=par("ln_b", b, 1)).then_inc(S["conf_out"], 1)
            attention("diff")
            act.wait_ge(S["att_done"], 1)
            nc.scalar.activation(CVS, T8[:, 6:8, :], ACT.Square).then_inc(S["sub_sq"], 1)
            act.wait_ge(S["sub_ps"], 1)
            nc.scalar.activation(XC, pairs(bank(5)), ACT.Sqrt, bias=EPS, scale=1.0 / 64).then_inc(S["sub_sd"], 1)
            operand_hi("out2")
            out_linear("out2")
            operand_hi("ffn4", True)
            ffn(4, "ffn4")

        @block.vector
        def _(dve):
            step = [0]

            def link(ins):
                step[0] += 1
                ins.then_inc(S["dve_step"], 1)
                dve.wait_ge(S["dve_step"], step[0])

            def poke(sem, n):
                link(nc.vector.memset(SMALL[:, 127:128], 0.0))
                nc.vector.memset(SMALL[:, 127:128], 0.0).then_inc(sem, n)

            def w_lo(n, i=None):
                if n >= n_tiles:
                    return
                dve.wait_ge(S["w_hi"], n + 1 + (0 if i is None else i * 6))
                w = width(n)
                nc.vector.tensor_tensor(WL[:, n % RING, 0:w], RAW[:, n % RING, 0:w], WH[:, n % RING, 0:w],
                                        ALU.subtract).then_inc(S["w_split"], 1)

            def operand_lo(name, p):
                dve.wait_ge(S["hi_ready"], 4 * version[name] + p + 1)
                nc.vector.tensor_tensor(XL[:, 2 * p:2 * p + 2, :], T8[:, 2 * p:2 * p + 2, :],
                                        XH[:, 2 * p:2 * p + 2, :], ALU.subtract).then_inc(S["act_ready"], 1)

            def operand_lo_all(name):
                for p in range(4):
                    operand_lo(name, p)

            def norm(name, src=X, split=True):
                k = norm_no[name]
                dve.wait_ge(S["norm_sd"], k + 1)
                link(nc.vector.reciprocal(RS[:, :], SD[:, :]))
                if name != "final":
                    dve.wait_ge(S["act_ready"], 4 * version[name])
                for p in range(4):
                    for b in (2 * p, 2 * p + 1):
                        last = nc.vector.scalar_tensor_tensor(
                            out=(X if name == "final" else T8)[:, b, :], in0=src[:, b, :],
                            scalar=par(NORM_GAIN[k], b, 1), in1=RS[:, :], op0=ALU.mult, op1=ALU.mult)
                    if name == "final":
                        last.then_inc(S["x_ready"], 1)
                        continue
                    last.then_inc(S["t8_ready"], 1)
                    if p and split:
                        operand_lo(name, p - 1)
                if name != "final" and split:
                    operand_lo(name, 3)

            def ffn(f, name, after=None, before=None):
                n0 = tile0[name]

                def count(sem, s, i, n=1):
                    dve.wait_ge(S[sem], STEPS * f + s + n + (0 if i is None else i * 2))

                def used(n, i):
                    dve.wait_ge(S["tile_used"], n + 1 + (0 if i is None else i * 6))

                def gate(s, n, i=None):
                    used(n, i)
                    if f or s or i is not None:
                        count("h_raw", s, i, 0)
                    nc.vector.tensor_tensor(SG, pairs(bank(4)), over(RS[:, :], 2), ALU.mult).then_inc(S["g_scaled"], 1)

                def up(s, n, i=None):
                    used(n, i)
                    if f or s or i is not None:
                        count("h_ready", s, i, 0)
                    nc.vector.tensor_tensor(HF, pairs(bank(5)), over(RS[:, :], 2), ALU.mult).then_inc(S["glu_free"], 1)
                    count("sg_ready", s, i)
                    count("glu_free", s, i)
                    nc.vector.tensor_tensor(HF, SG, HF, ALU.mult).then_inc(S["h_raw"], 1)

                def hidden_lo(s, i=None):
                    count("h_hi", s, i)
                    half = slice(2 * (s % 2), 2 * (s % 2) + 2)
                    nc.vector.tensor_tensor(HL[:, half, :], HF, HH[:, half, :], ALU.subtract).then_inc(S["h_ready"], 1)

                def one(s, i=None):
                    gate(s, n0 + 3 * s - 1, i)
                    w_lo(n0 + 3 * s + 2, i)
                    up(s, n0 + 3 * s, i)
                    w_lo(n0 + 3 * s + 3, i)
                    hidden_lo(s, i)
                    w_lo(n0 + 3 * s + 4, i)

                w_lo(n0 + 3)
                dve.wait_ge(S["norm_sd"], norm_no[name] + 1)
                link(nc.vector.reciprocal(RS[:, :], SD[:, :]))
                gate(0, n0)
                up(0, n0 + 1)
                hidden_lo(0)
                w_lo(n0 + 4)
                if before:
                    before()
                loops = loops_of(name)
                with nc.vector.Fori(0, loops) as i:
                    one(1, i)
                    one(2, i)
                for s in range(2 * loops + 1, STEPS):
                    one(s)
                if after:
                    after()

            def add_ffn(name, p):
                f = int(name[3:])
                if p < 3:
                    dve.wait_ge(S["down_done"], 3 * f + p + 1)
                else:
                    dve.wait_ge(S["tile_used"], tile0[name] + 3 * STEPS)
                nc.vector.scalar_tensor_tensor(out=X[:, 2 * p:2 * p + 2, :], in0=pairs(bank(p)), scalar=ffn_scale(name),
                                               in1=X[:, 2 * p:2 * p + 2, :], op0=ALU.mult, op1=ALU.add).then_inc(S["x_ready"], 1)

            def add_ffn_all(name):
                for p in range(4):
                    add_ffn(name, p)

            def add_linear(name, t):
                dve.wait_ge(S["tile_used"], tile0[name] + t + 1)
                nc.vector.tensor_tensor(X[:, 2 * t:2 * t + 2, :], X[:, 2 * t:2 * t + 2, :], pairs(bank(t)),
                                        ALU.add).then_inc(S["x_ready"], 1)
                w_lo(tile0[name] + t + RING)

            def gained(name, add=None, early=None):
                k, v = norm_no[name], version[name]
                for p in range(4):
                    if add:
                        add(p)
                    if p == 1 and early:
                        early()
                    if p == 0 and v:
                        dve.wait_ge(S["act_ready"], 4 * v)
                    dve.wait_ge(S["x_ready"], 4 * x_no[name] + p + 1)
                    for b in (2 * p, 2 * p + 1):
                        last = nc.vector.tensor_scalar(T8[:, b, :], X[:, b, :], par(NORM_GAIN[k], b, 1), None, ALU.mult)
                    last.then_inc(S["t8_ready"], 1)
                    if p:
                        operand_lo(name, p - 1)
                operand_lo(name, 3)

            def deviations_inverted(name):
                dve.wait_ge(S["norm_sd"], norm_no[name] + 1)
                link(nc.vector.reciprocal(RS[:, :], SD[:, :]))

            def scaled_out(name, t, dst, sem, blocks=2):
                dve.wait_ge(S["tile_used"], tile0[name] + t + 1)
                if blocks == 2:
                    nc.vector.tensor_tensor(dst, pairs(bank(t)), over(RS[:, :], 2), ALU.mult).then_inc(sem, 1)
                else:
                    nc.vector.tensor_tensor(dst, bank(t, SEQ), RS[:, :], ALU.mult).then_inc(sem, 1)

            def attention(ph):
                u0, m0, g0 = att0[ph]
                kind, n = att_of[ph]
                maps = 2 if kind == "diff" else 1
                sc, pt = att_work(ph)

                def maxima(u):
                    for m in range(maps):
                        s = sc[u % ADEPTH][m]
                        dve.wait_ge(S["att_s"], m0 + u * maps + m + 1)
                        ps = pairs(bank(s_bank(maps, u, m)))
                        if kind == "mem":
                            link(nc.vector.tensor_reduce(MX(u, m), ps, axis=AX.X, op=ALU.max))
                            nc.vector.tensor_scalar(NM2(u, m), MX(u, m), -MEM_SCALE, None, ALU.mult).then_inc(S["att_nm"], 1)
                            continue
                        if u >= ADEPTH:
                            dve.wait_ge(S["att_t"], u0 + u - ADEPTH + 1)
                        added = (con("mla_mask").rearrange("p (a b) -> p a b", b=SEQ) if kind == "mla" else BIAS[:, :, u, :])
                        link(nc.vector.scalar_tensor_tensor(out=s, in0=ps, scalar=(MLA_SCALE if kind == "mla" else DIFF_SCALE),
                                                            in1=added, op0=ALU.mult, op1=ALU.add))
                        link(nc.vector.tensor_reduce(MX(u, m), s, axis=AX.X, op=ALU.max))
                        nc.vector.tensor_scalar(NM2(u, m), MX(u, m), -1.0, None, ALU.mult).then_inc(S["att_nm"], 1)

                def normalise(u):
                    dve.wait_ge(S["att_e"], m0 + (u + 1) * maps)
                    for m in range(maps):
                        link(nc.vector.reciprocal(RC2(u, m), SUM2(u, m)))
                    if kind == "diff":
                        link(nc.vector.tensor_scalar(RC2(u, 1), RC2(u, 1), NLAM, None, ALU.mult))
                    a, b = sc[u % ADEPTH]
                    for q in range(TB):
                        last = nc.vector.tensor_scalar(a[:, q, :], a[:, q, :], RC(u, 0, q), None, ALU.mult)
                        if kind == "diff":
                            link(last)
                            last = nc.vector.scalar_tensor_tensor(out=a[:, q, :], in0=b[:, q, :], scalar=RC(u, 1, q),
                                                                  in1=a[:, q, :], op0=ALU.mult, op1=ALU.add)
                    last.then_inc(S["att_p"], 1)

                def evac(g):
                    dve.wait_ge(S["att_o"], g0 + g + 1)
                    nc.vector.tensor_copy(T8[:, (g if kind == "mla" else 6 + g), :], bank(o_bank(maps, g), SEQ)).then_inc(S["att_oe"], 1)

                per = 1 if kind == "mla" else 2
                maxima(0)
                for u in range(n):
                    if u + 1 < n:
                        maxima(u + 1)
                    normalise(u)
                    if u >= 1 and (u % per) == 0:
                        evac(u // per - 1)
                evac(n // per - 1)

            def latent(r, gain):
                dve.wait_ge(S["lat_sd"], r + 1)
                dve.wait_ge(*((S["rope_in"], 1) if r == 0 else (S["qm_ready"], 2)))
                link(nc.vector.reciprocal(RS[:, :], SD[:, :]))
                for b in range(2):
                    last = nc.vector.scalar_tensor_tensor(out=LAT[:, b, :], in0=LAT[:, b, :], scalar=par(gain, b, 1),
                                                          in1=RS[:, :], op0=ALU.mult, op1=ALU.mult)
                last.then_inc(S["lat_f"], 1)
                dve.wait_ge(S["lat_hi"], r + 1)
                nc.vector.tensor_tensor(HL[:, 0:2, :], LAT, HH[:, 0:2, :], ALU.subtract).then_inc(S["lat_ready"], 1)

            nc.vector.memset(ZB[:, :], 0.0).then_inc(S["zeros_ready"], 1)
            dve.wait_ge(S["x_loaded"], 16)
            poke(S["x_ready"], 4)
            dve.wait_ge(S["par_loaded"], 16)
            gained("ffn0", early=lambda: w_lo(0))
            w_lo(1)
            w_lo(2)
            ffn(0, "ffn0", lambda: norm("mem", MEMT))
            add_ffn_all("ffn0")
            w_lo(tile0["mem"] + 2)
            w_lo(tile0["mem"] + RING)
            norm("ain", split=False)
            for t in range(1, 4):
                w_lo(tile0["mem"] + t + RING)
            operand_lo_all("ain")

            n0 = tile0["ain"]
            w_lo(n0 + RING)
            nc.vector.memset(CB[:, :, 0:PAD], 0.0).then_inc(S["pads_ready"], 1)
            for t in range(9):
                w_lo(n0 + t + 1 + RING)
                dve.wait_ge(S["ain_evac"], t + 1)
                for tap in range(4):
                    for b in (2 * t, 2 * t + 1):
                        w = par("a_conv", 4 * b + tap, 1)
                        x = CB[:, b, tap:tap + SEQ]
                        if tap == 0:
                            last = nc.vector.tensor_scalar(YQKV[:, b, :], x, w, None, ALU.mult)
                        else:
                            last = nc.vector.scalar_tensor_tensor(out=YQKV[:, b, :], in0=x, scalar=w, in1=YQKV[:, b, :],
                                                                  op0=ALU.mult, op1=ALU.add)
                    if tap < 3:
                        link(last)
                last.then_inc(S["conv_done"], 1)
                if t == 0:
                    dve.wait_ge(S["ba_ready"], 1)
                    nc.vector.tensor_tensor(G1, BA[:, :, AH:2 * AH], over(par("dt_bias"), TB), ALU.add).then_inc(S["g_shifted"], 1)
                if t == 1:
                    dve.wait_ge(S["g_softplus"], 1)
                    link(nc.vector.tensor_scalar(BETA, BETA, 1.0, None, ALU.add))
                    nc.vector.reciprocal(BETA, BETA).then_inc(S["beta_ready"], 1)
                    link(nc.vector.tensor_scalar(G1, G1, 0.0, None, ALU.max))
                    link(nc.vector.tensor_tensor(G1, G1, G2, ALU.add))
                    nc.vector.scalar_tensor_tensor(out=GG, in0=G1, scalar=-1.0, in1=over(EA, TB), op0=ALU.mult,
                                                   op1=ALU.mult).then_inc(S["decay_g_ready"], 1)
            for t in range(9, 11):
                w_lo(n0 + t + 1 + RING)
            dve.wait_ge(S["l2_sd"], 1)
            nc.vector.reciprocal(RS[0:2 * AH, :], SD[0:2 * AH, :]).then_inc(S["l2_rc"], 1)
            dve.wait_ge(S["gcol_sb"], 1)
            dve.wait_ge(S["rows_sb"], 6)
            dve.wait_ge(S["tok_ps"], 1)
            for m in range(TB * AH):
                tb, h = divmod(m, AH)
                last = nc.vector.tensor_scalar(DT[:, m, :], GROW[:, h, tb * P:(tb + 1) * P], GC[:, tb, h:h + 1], 0.0,
                                               ALU.subtract, ALU.min)
            last.then_inc(S["d_pre"], 1)
            dve.wait_ge(S["beta_ready"], 1)
            for m in range(TB * AH):
                tb, h = divmod(m, AH)
                last = nc.vector.tensor_scalar(VB[:, tb, h, :], PS[:, ROW_BANK[m // 4], (m % 4) * P:(m % 4 + 1) * P],
                                               BETA[:, tb, h:h + 1], None, ALU.mult)
            last.then_inc(S["vb_ready"], 1)
            w_lo(n0 + 12 + RING)
            dve.wait_ge(S["d_exp"], 1)
            nc.vector.tensor_tensor(DT, DT, over(con("tri"), TB * AH), ALU.mult)
            for j in (3, 4, 5, 0, 1, 2):
                y = YQKV[:, 2 * j:2 * j + 2, :]
                b = (QLEN_BANK + KLEN_BANK)[j]
                dve.wait_ge(S["l2_bc"], (j - 3 if j >= 3 else j + 3) + 1)
                nc.vector.scalar_tensor_tensor(out=y, in0=y, scalar=(P ** -0.5 if j < 3 else 1.0), in1=pairs(bank(b)),
                                               op0=ALU.mult, op1=ALU.mult).then_inc(S["qk_ready"], 1)
                if j == 5:
                    dve.wait_ge(S["qk_ready"], 3)
                    dve.wait_ge(S["beta_rows"], 3)
                    nc.vector.tensor_tensor(KBT, Yk, BETAROW, ALU.mult).then_inc(S["kb_ready"], 1)
            w_lo(n0 + 13 + RING)
            dve.wait_ge(S["qkt_ps"], 1)
            for j in range(3):
                last = nc.vector.tensor_tensor(QD[:, 4 * j:4 * j + 4, :], DT[:, 4 * j:4 * j + 4, :],
                                               bank(QK_BANK[j]).rearrange("p (a b) -> p a b", b=P), ALU.mult)
            last.then_inc(S["qd_ready"], 1)
            dve.wait_ge(S["kkt_ps"], 1)
            for j in range(3):
                last = nc.vector.tensor_tensor(LT[:, 4 * j:4 * j + 4, :], DT[:, 4 * j:4 * j + 4, :],
                                               bank(KK_BANK[j]).rearrange("p (a b) -> p a b", b=P), ALU.mult)
            link(last)
            for s in range(LEVELS):
                level = con("level", s * P, P)
                for g in range(3):
                    r = slice(4 * g, 4 * g + 4)
                    if s:
                        dve.wait_ge(S["lvl_p1"], 3 * (s - 1) + g + 1)
                    if s == 1:
                        dve.wait_ge(S["lvl_xt"], g + 1)
                    nc.vector.tensor_tensor(MT[:, r, :], LT[:, r, :], over(level, 4), ALU.mult).then_inc(S["lvl_m"], 1)
                if s == 0:
                    for g in range(3):
                        r = slice(4 * g, 4 * g + 4)
                        dve.wait_ge(S["lvl_m"], g + 1)
                        nc.vector.tensor_tensor(XT[:, r, :], over(con("ident"), 4), MT[:, r, :], ALU.subtract).then_inc(S["lvl_xt"], 1)
                    for g in range(3):
                        r = slice(4 * g, 4 * g + 4)
                        dve.wait_ge(S["lvl_p1"], g + 1)
                        nc.vector.tensor_tensor(XM[:, r, :], over(con("ident"), 4), bank(g).rearrange("p (a b) -> p a b", b=P),
                                                ALU.subtract).then_inc(S["lvl_x"], 1)
                    continue
                if s == 1:
                    nc.vector.tensor_tensor(KBT, KBT, EGROW, ALU.mult)
                    nc.vector.tensor_tensor(Yq, Yq, EGROW, ALU.mult).then_inc(S["scaled"], 1)
                for g in range(3):
                    r = slice(4 * g, 4 * g + 4)
                    dve.wait_ge(S["lvl_zt"], 3 * (s - 1) + g + 1)
                    if s < LEVELS - 1:
                        nc.vector.tensor_tensor(XM[:, r, :], XM[:, r, :], bank(3 + g).rearrange("p (a b) -> p a b", b=P),
                                                ALU.subtract).then_inc(S["lvl_x"], 1)
                    nc.vector.tensor_tensor(XT[:, r, :], XT[:, r, :], bank(g).rearrange("p (a b) -> p a b", b=P),
                                            ALU.subtract).then_inc(S["lvl_xt"], 1)
            for v in VN:
                last = nc.vector.memset(v, 0.0)
            last.then_inc(S["vn_zeroed"], 1)
            for c in range(NCHUNK):
                tb, hf = divmod(c, 2)
                r = slice(CHUNK * hf, CHUNK * hf + CHUNK)
                if c == 0:
                    dve.wait_ge(S["vb_ready"], 1)
                    nc.vector.tensor_copy(RR, VB[:, 0, :, :]).then_inc(S["r_ready"], 1)
                else:
                    dve.wait_ge(S["ks_ps"], c)
                    for b in range(2):
                        last = nc.vector.tensor_tensor(RR[r, 3 * b:3 * b + 3, :], VB[r, tb, 3 * b:3 * b + 3, :],
                                                       PS[r, 3 + b, 0:3 * P].rearrange("p (a b) -> p a b", b=P), ALU.subtract)
                    last.then_inc(S["r_ready"], 1)
                if c == NCHUNK - 1:
                    break
                dve.wait_ge(S["su_ps"], c + 1)
                for h in range(AH):
                    su = PS[:, 3 + h // 3, (h % 3) * P:(h % 3 + 1) * P]
                    if c == 0:
                        last = nc.vector.tensor_copy(ST[:, h, :], su)
                    else:
                        last = nc.vector.scalar_tensor_tensor(out=ST[:, h, :], in0=ST[:, h, :],
                                                              scalar=EGROW[:, h, CHUNK * (c + 1) - 1:CHUNK * (c + 1)], in1=su,
                                                              op0=ALU.mult, op1=ALU.add)
                last.then_inc(S["s_ready"], 1)
            for j in range(3):
                dve.wait_ge(S["o_sb"], j + 1)
                o, t = OB[:, 2 * j:2 * j + 2, :], T8[:, 2 * j:2 * j + 2, :]
                nc.vector.scalar_tensor_tensor(out=t, in0=o, scalar=par("a_out_norm"), in1=t, op0=ALU.mult,
                                               op1=ALU.mult).then_inc(S["o_gated"], 1)
            dve.wait_ge(S["o_sd"], 1)
            nc.vector.reciprocal(RS[0:AH, :], SD[0:AH, :]).then_inc(S["o_rc"], 1)
            dve.wait_ge(S["o_gated"], 3)
            for j in range(3):
                t = T8[:, 2 * j:2 * j + 2, :]
                dve.wait_ge(S["o_bc"], j + 1)
                last = nc.vector.tensor_tensor(t, t, pairs(bank(3 + j)), ALU.mult)
            link(last)
            attention("mem0")
            poke(S["t8_ready"], 4)
            operand_lo_all("out0")
            gained("ffn1", lambda t: add_linear("out0", t))

            def angles():
                dve.wait_ge(S["pos_loaded"], 16)
                link(nc.vector.tensor_copy(ANG, POSI))
                link(nc.vector.tensor_scalar(ANG, ANG, con("inv_freq"), None, ALU.mult))
                link(nc.vector.tensor_scalar(TURN, ANG, 1.0 / (2 * PI), ROUND, ALU.mult, ALU.add))
                link(nc.vector.tensor_scalar(TURN, TURN, -ROUND, None, ALU.add))
                for part in TWO_PI:
                    link(nc.vector.scalar_tensor_tensor(out=ANG, in0=TURN, scalar=-part, in1=ANG, op0=ALU.mult, op1=ALU.add))
                link(nc.vector.tensor_scalar(ANG_S, ANG, PI_IN, -PI_IN, ALU.min, ALU.max))
                link(nc.vector.tensor_scalar(ANG_C, ANG_S, PI / 2, None, ALU.add))
                link(nc.vector.tensor_scalar(TURN, ANG_C, PI, -2 * PI, ALU.is_gt, ALU.mult))
                link(nc.vector.tensor_tensor(ANG_C, ANG_C, TURN, ALU.add))
                nc.vector.tensor_scalar(ANG_C, ANG_C, PI_IN, -PI_IN, ALU.min, ALU.max).then_inc(S["rope_ang"], 1)

            ffn(1, "ffn1", before=angles)

            gained("dkv", lambda p: add_ffn("ffn1", p))
            w_lo(tile0["dkv"] + 2)
            poke(S["x_ready"], 4)
            n0 = tile0["dkv"]
            w_lo(n0 + RING)
            deviations_inverted("dkv")
            scaled_out("dkv", 0, LAT, S["lat_sb"])
            w_lo(n0 + 1 + RING)
            scaled_out("dkv", 1, KR, S["rope_in"], 1)
            latent(0, "kv_lat_norm")
            dve.wait_ge(S["rope_tab"], 2)
            dve.wait_ge(S["rope_ps"], 1)
            nc.vector.tensor_tensor(ROT[:, 0, :], SIN, bank(2, SEQ), ALU.mult)
            link(nc.vector.tensor_tensor(KR, KR, COS, ALU.mult))
            link(nc.vector.tensor_tensor(KR, KR, ROT[:, 0, :], ALU.add))
            nc.vector.tensor_scalar(KR, KR, con("half"), None, ALU.mult).then_inc(S["rope_done"], 1)
            n0 = tile0["ukv"]
            for t in range(2):
                w_lo(n0 + t + RING)
            gained("ffn2")
            ffn(2, "ffn2")

            gained("bin", lambda p: add_ffn("ffn2", p))
            w_lo(tile0["bin"] + 2)
            n0 = tile0["bin"]
            w_lo(n0 + RING)
            deviations_inverted("bin")
            scaled_out("bin", 0, LAT, S["lat_sb"])
            w_lo(n0 + 1 + RING)
            scaled_out("bin", 1, QM[:, :, :], S["qm_ready"])
            latent(1, "b_q_norm")
            n0 = tile0["uq"]
            for t in range(2):
                w_lo(n0 + t + RING)
            for j in range(3):
                dve.wait_ge(S["uq_ps"], j + 1)
                last = nc.vector.tensor_tensor(ROT[:, 2 * j:2 * j + 2, :], pairs(bank((6 + j) % 8)), over(SIN, 2), ALU.mult)
            q = QQ[:, :, 1, :]
            link(nc.vector.tensor_tensor(q, q, over(COS, BH), ALU.mult))
            nc.vector.tensor_tensor(q, q, ROT, ALU.add).then_inc(S["rope_done"], 1)
            attention("mem1")
            attention("mla")
            poke(S["t8_ready"], 4)
            operand_lo_all("out1")
            gained("ffn3", lambda t: add_linear("out1", t))
            ffn(3, "ffn3")
            add_ffn_all("ffn3")
            norm("final")
            norm("in2")
            w_lo(tile0["in2"] + 2)

            n0 = tile0["in2"]
            nc.vector.memset(UP[:, :, 0:16], 0.0)
            nc.vector.memset(CS[:, :, 0:2], 0.0)
            nc.vector.memset(CC_[:, :, 0:30], 0.0).then_inc(S["pads_ready"], 1)
            for j in range(2):
                last = nc.vector.tensor_tensor(LAMP[:, j, :], par("lam", 64 * j, 32), par("lam", 64 * j + 32, 32), ALU.mult)
            link(last)
            nc.vector.tensor_reduce(LAMS, LAMP[:, :, :], axis=AX.X, op=ALU.add).then_inc(S["lam_prod"], 1)
            dve.wait_ge(S["bias_ps"], 1)
            nc.vector.tensor_tensor(BROW, PS[:, 4:8, :], over(TABLE[:, 2 * SEQ:], MH), ALU.add).then_inc(S["bias_row"], 1)
            taps = [(b, j) for j in range(31) for b in range(2) if b == 0 or j < POOL_TAP]

            def conf_tap(b, j):
                w = par("conf_w", 31 * b + j, 1)
                x = CC_[:, b, j:j + SEQ]
                if j == 0:
                    return nc.vector.tensor_scalar(CV[:, b, :], x, w, par("conf_b", b, 1), ALU.mult, ALU.add)
                return nc.vector.scalar_tensor_tensor(out=CV[:, b, :], in0=x, scalar=w, in1=CV[:, b, :], op0=ALU.mult, op1=ALU.add)

            for t in range(9):
                w_lo(n0 + t + RING)
                if t < 1:
                    continue
                if t == 1:
                    dve.wait_ge(S["in2_evac"], 2)
                    nc.vector.tensor_tensor(CC_[:, :, 30:30 + SEQ], CA_, CG_, ALU.mult).then_inc(S["conf_in"], 1)
                    dve.wait_ge(S["conf_in"], 1)
                for _ in range(6):
                    if len(taps) > 1:
                        b, j = taps.pop(0)
                        link(conf_tap(b, j))
            while taps:
                b, j = taps.pop(0)
                link(conf_tap(b, j))
            dve.wait_ge(S["conf_pool"], 1)
            nc.vector.tensor_tensor(CV[:, 1, :], CV[:, 1, :], S4[:, 0, 0:SEQ], ALU.add).then_inc(S["conf_ready"], 1)
            dve.wait_ge(S["in2_evac"], 9)
            link(nc.vector.tensor_tensor(CS[:, :, 2:2 + SEQ], SC_, SH_, ALU.mult))
            for tap in range(3):
                for b in range(2):
                    w, x = par("sconv", 3 * b + tap, 1), CS[:, b, tap:tap + SEQ]
                    if tap == 0:
                        last = nc.vector.tensor_scalar(SC_[:, b, :], x, w, None, ALU.mult)
                    else:
                        last = nc.vector.scalar_tensor_tensor(out=SC_[:, b, :], in0=x, scalar=w, in1=SC_[:, b, :],
                                                              op0=ALU.mult, op1=ALU.add)
                link(last)
            nc.vector.tensor_tensor(T8[:, 2:4, :], SC_, SB_, ALU.mult)
            dve.wait_ge(S["qk2_sd"], 1)
            link(nc.vector.reciprocal(ZS, ZS))
            for j, g in enumerate(("q_g", "k_g")):
                v = ZQ[:, 2 * j:2 * j + 2, :]
                last = nc.vector.scalar_tensor_tensor(out=v, in0=v, scalar=par(g), in1=ZS[:, 2 * j:2 * j + 2, :],
                                                      op0=ALU.mult, op1=ALU.mult)
            last.then_inc(S["qk2_ready"], 1)
            dve.wait_ge(S["conf_mean"], 1)
            nc.vector.tensor_tensor(XC, CV, over(MN, 2), ALU.subtract).then_inc(S["conf_xc"], 1)
            dve.wait_ge(S["pool_ps"], 1)
            for b in range(2):
                nc.vector.tensor_scalar(T8[:, b, :], bank(4)[:, b * SEQ:(b + 1) * SEQ], par("pool_scale", b, 1), None, ALU.mult)
            dve.wait_ge(S["conf_sd"], 1)
            link(nc.vector.reciprocal(RS[:, :], SD[:, :]))
            for b in range(2):
                last = nc.vector.scalar_tensor_tensor(out=XC[:, b, :], in0=XC[:, b, :], scalar=par("ln_g", b, 1), in1=RS[:, :],
                                                      op0=ALU.mult, op1=ALU.mult)
            last.then_inc(S["conf_y"], 1)
            dve.wait_ge(S["lam_exp"], 1)
            link(nc.vector.tensor_tensor(NLAM, LAM2[:, 1:2], LAM2[:, 0:1], ALU.subtract))
            link(nc.vector.tensor_scalar(NLAM, NLAM, -LAM_INIT, None, ALU.add))
            dve.wait_ge(S["bias_ready"], 32)
            attention("diff")
            poke(S["att_done"], 1)
            dve.wait_ge(S["sub_sd"], 1)
            link(nc.vector.reciprocal(XC, XC))
            v = T8[:, 6:8, :]
            link(nc.vector.scalar_tensor_tensor(out=v, in0=v, scalar=par("subln"), in1=XC, op0=ALU.mult, op1=ALU.mult))
            link(nc.vector.tensor_scalar(v, v, 1.0 - LAM_INIT, None, ALU.mult))
            dve.wait_ge(S["conf_out"], 2)
            poke(S["t8_ready"], 4)
            operand_lo_all("out2")
            gained("ffn4", lambda t: add_linear("out2", t))
            ffn(4, "ffn4")
            add_ffn_all("ffn4")

        @block.tensor
        def _(pe):
            def f32mm(o, w, a, start=True, stop=True):
                return nc.tensor.matmul(o, w, a, start=start, stop=stop, skip_group_check=True)

            def norm(name):
                k = norm_no[name]
                for p in range(4):
                    pe.wait_ge(S["norm_sq"], 4 * k + p + 1)
                    for b in (2 * p, 2 * p + 1):
                        last = f32mm(bank(7, SEQ), con("ones"), SQ[:, b, :], b == 0, b == KB - 1)
                last.then_inc(S["norm_ms"], 1)

            def tile_ready(n, i=None):
                pe.wait_ge(S["w_split"], n + 1 + (0 if i is None else i * 6))

            def w_at(n, at):
                s = slice(at, at + P)
                return WH[:, n % RING, s], WL[:, n % RING, s]

            def operand(name, kb):
                if name is not None and kb % 2 == 0:
                    pe.wait_ge(S["act_ready"], 4 * version[name] + kb // 2 + 1)

            def by_feature(n, b, first=None, outs=None, blocks=2, i=None, row=CW):
                tile_ready(n, i)
                for f in range(blocks):
                    o = outs[f] if outs else bank(b)[:, f * SEQ:(f + 1) * SEQ]
                    for kb in range(KB):
                        if f == 0:
                            operand(first, kb)
                        last = matmul3(o, *w_at(n, kb * row + f * P), XH[:, kb, :], XL[:, kb, :], kb == 0, kb == KB - 1)
                return last.then_inc(S["tile_used"], 1)

            def by_token(n, b, cols, first=None):
                tile_ready(n)
                for tb in range(TB):
                    o = bank(b)[:, tb * cols:(tb + 1) * cols]
                    t = slice(tb * P, (tb + 1) * P)
                    for kb in range(KB):
                        if tb == 0:
                            operand(first, kb)
                        s = slice(kb * cols, (kb + 1) * cols)
                        last = matmul3_tok(o, XH[:, kb, t], XL[:, kb, t], WH[:, n % RING, s], WL[:, n % RING, s],
                                           kb == 0, kb == KB - 1)
                return last.then_inc(S["tile_used"], 1)

            def matmul3_tok(o, a_hi, a_lo, w_hi, w_lo, start, stop):
                nc.tensor.matmul(o, a_hi, w_hi, start=start, stop=False, skip_group_check=True)
                nc.tensor.matmul(o, a_hi, w_lo, start=False, stop=False, skip_group_check=True)
                return nc.tensor.matmul(o, a_lo, w_hi, start=False, stop=stop, skip_group_check=True)

            def ffn(f, name):
                n0 = tile0[name]

                def gate_up(s, first=None, i=None):
                    n = n0 if s == 0 else n0 + 3 * s - 1
                    for k, free in enumerate(("g_scaled", "glu_free")):
                        if f or s or i is not None:
                            pe.wait_ge(S[free], STEPS * f + s + (0 if i is None else i * 2))
                        by_feature(n + k, 4 + k, first if k == 0 else None, i=i)
                        if first and k == 0:
                            if name == "ffn0":
                                pe.wait_ge(S["con_loaded"], 16)
                            norm(name)

                def down(s, n, i=None, closing=False):
                    tile_ready(n, i)
                    pe.wait_ge(S["h_ready"], STEPS * f + s + 1 + (0 if i is None else i * 2))
                    order = [(j, nb) for nb in range(KB) for j in range(2)] if closing else [(j, nb) for j in range(2) for nb in range(KB)]
                    for j, nb in order:
                        h = 2 * (s % 2) + j
                        done = closing and j == 1 and nb % 2 == 1
                        last = matmul3(PS[:, nb // 2, (nb % 2) * SEQ:(nb % 2 + 1) * SEQ], *w_at(n, j * D + nb * P),
                                       HH[:, h, :], HL[:, h, :], False, done)
                        if done and nb < KB - 1:
                            last.then_inc(S["down_done"], 1)
                    last.then_inc(S["tile_used"], 1)

                gate_up(0, name)
                for b in range(4):
                    nc.tensor.matmul(bank(b), ZB[:, 0:P], ZB[:, :], start=True, stop=False, skip_group_check=True)
                loops = loops_of(name)
                with nc.tensor.Fori(0, loops) as i:
                    for s in (1, 2):
                        gate_up(s, None, i)
                        down(s - 1, n0 + 3 * s + 1, i)
                for s in range(2 * loops + 1, STEPS):
                    gate_up(s)
                    down(s - 1, n0 + 3 * s + 1)
                if name == "ffn0":
                    norm("mem")
                down(STEPS - 1, n0 + 3 * STEPS - 1, None, True)

            def out_linear(name):
                for t in range(4):
                    by_feature(tile0[name] + t, t, name if t == 0 else None)

            def attention(ph):
                u0, m0, g0 = att0[ph]
                kind, n = att_of[ph]
                maps = 2 if kind == "diff" else 1
                sc, pt = att_work(ph)
                per = 1 if kind == "mla" else 2

                def scores(u):
                    need = m0 + max(0, u - ADEPTH + 1) * maps
                    if need:
                        pe.wait_ge(S["att_e"], need)
                    for m in range(maps):
                        for q in range(TB):
                            o = PS[:, s_bank(maps, u, m), q * SEQ:(q + 1) * SEQ]
                            t = slice(q * P, (q + 1) * P)
                            if kind == "mem":
                                r = slice(64 * (u % 2), 64 * (u % 2) + 64)
                                last = f32mm(o, QM[r, u // 2, t], MEM_K[0 if ph == "mem0" else 1][r, u // 2, :])
                            elif kind == "mla":
                                f32mm(o, QQ[:, u, 0, t], KN[:, u, :], True, False)
                                last = f32mm(o, QQ[:, u, 1, t], KR, False, True)
                            else:
                                a = 64 * (u % 2) + 32 * m
                                r = slice(a, a + 32)
                                last = f32mm(o, ZQ[r, u // 2, t], ZQ[r, 2 + u // 2, :])
                        last.then_inc(S["att_s"], 1)

                def turn(u):
                    pe.wait_ge(S["att_p"], u0 + u + 1)
                    if u0 + u >= 2:
                        pe.wait_ge(S["att_pt"], u0 + u - (1 if maps == 1 else 0))
                    for kb in range(TB):
                        for q in range(TB):
                            last = nc.tensor.transpose(bank(t_bank(maps, u))[:, kb * SEQ + q * P:kb * SEQ + (q + 1) * P],
                                                       sc[u % ADEPTH][0][:, q, kb * P:(kb + 1) * P], con("ident"))
                    last.then_inc(S["att_t"], 1)

                def values(u):
                    g = u // per
                    pe.wait_ge(S["att_pt"], u0 + u + 1)
                    if u % per == 0 and g0 + g >= 2:
                        pe.wait_ge(S["att_oe"], g0 + g - (1 if maps == 1 else 0))
                    for kb in range(TB):
                        if kind == "mla":
                            v, o = VM[:, kb, u, :], bank(o_bank(maps, g), SEQ)
                        else:
                            r = slice(64 * (u % 2), 64 * (u % 2) + 64)
                            src = ZV if kind == "diff" else MEM_V[0 if ph == "mem0" else 1]
                            v, o = src[:, kb, 64 * u:64 * u + 64], PS[r, o_bank(maps, g), 0:SEQ]
                        last = f32mm(o, v, pt[u % 2][:, kb, :], kb == 0, kb == TB - 1)
                    if u % per == per - 1:
                        last.then_inc(S["att_o"], 1)

                for u in range(ADEPTH - 1):
                    scores(u)
                for u in range(n):
                    if u + ADEPTH - 1 < n:
                        scores(u + ADEPTH - 1)
                    turn(u)
                    values(u)

            def latent(r):
                pe.wait_ge(S["lat_sq"], r + 1)
                for b in range(2):
                    last = f32mm(bank(7, SEQ), con("ones"), LSQ[:, b, :], b == 0, b == 1)
                last.then_inc(S["lat_sum"], 1)

            pe.wait_ge(S["zeros_ready"], 1)
            ffn(0, "ffn0")
            for t in range(4):
                if t == 3:
                    pe.wait_ge(S["mem_evac"], 1)
                if t % 2 == 0:
                    by_feature(tile0["mem"] + t, MEM_BANK[t], "mem" if t == 0 else None)
                else:
                    by_token(tile0["mem"] + t, MEM_BANK[t], CW)
                if t == 0:
                    norm("ain")
            pe.wait_ge(S["mem_evac"], 4)

            n0 = tile0["ain"]
            by_token(n0, 6, 2 * AH, "ain")
            for t in range(12):
                if t >= 4:
                    pe.wait_ge(S["ain_evac"], t - 3)
                by_feature(n0 + 1 + t, t % 4)
                if t == 2:
                    pe.wait_ge(S["decay_g_ready"], 1)
                    for tb in range(TB):
                        f32mm(PS[:, 6, 64 + AH * tb:64 + AH * tb + AH], con("tri"), GG[:, tb, :])
                    for tb in range(TB):
                        last = f32mm(PS[:, 6, 96 + AH * tb:96 + AH * tb + AH], con("after"), GG[:, tb, :])
                    last.then_inc(S["gcol_ps"], 1)
                if t in (2, 4):
                    src, mat = (GG, "tri") if t == 2 else (BETA, "ident")
                    if t == 4:
                        pe.wait_ge(S["beta_ready"], 1)
                        pe.wait_ge(S["rows_sb"], 6)
                    for h in range(AH):
                        for tb in range(TB):
                            o = PS[:, ROW_BANK[h // 2], (h % 2) * SEQ + tb * P:(h % 2) * SEQ + (tb + 1) * P]
                            last = f32mm(o, src[:, tb, h:h + 1].broadcast_to([P, P]), con(mat))
                        if h % 2:
                            last.then_inc(S["rows_ps"], 1)
                if t == 10:
                    pe.wait_ge(S["l2_sq"], 6)
                    for j in range(2 * AH):
                        last = f32mm(PS[0:2 * AH, 6, SEQ:2 * SEQ], pick(j, 2 * AH), QKS[:, j, :], j == 0, j == 2 * AH - 1)
                    last.then_inc(S["l2_sum"], 1)
                    pe.wait_ge(S["silu_done"], 9)
                    pe.wait_ge(S["beta_rows"], 3)
                    for m in range(TB * AH):
                        tb, h = divmod(m, AH)
                        last = nc.tensor.transpose(PS[:, ROW_BANK[m // 4], (m % 4) * P:(m % 4 + 1) * P],
                                                   Yv[:, h, tb * P:(tb + 1) * P], con("ident"))
                    last.then_inc(S["tok_ps"], 1)
            pe.wait_ge(S["ain_evac"], 9)
            by_feature(n0 + 13, 0)
            pe.wait_ge(S["ain_evac"], 12)
            pe.wait_ge(S["l2_rc"], 1)
            for j in (3, 4, 5, 0, 1, 2):
                if j == 0:
                    pe.wait_ge(S["qm_ready"], 1)
                    pe.wait_ge(S["vb_ready"], 1)
                b = (QLEN_BANK + KLEN_BANK)[j]
                for k in range(2):
                    last = f32mm(PS[:, b, k * SEQ:(k + 1) * SEQ], spread(2 * j + k, 2 * AH), RS[0:2 * AH, :])
                last.then_inc(S["l2_bc"], 1)
            pe.wait_ge(S["qk_ready"], 3)
            for m in range(TB * AH):
                tb, h = divmod(m, AH)
                last = nc.tensor.transpose(PS[:, KTOK_BANK[m // 4], (m % 4) * P:(m % 4 + 1) * P],
                                           Yk[:, h, tb * P:(tb + 1) * P], con("ident"))
            last.then_inc(S["tok_ps"], 1)
            pe.wait_ge(S["qk_ready"], 6)
            for banks, a, done in ((QK_BANK, Yq, S["qkt_ps"]), (KK_BANK, KBT, S["kkt_ps"])):
                if a is KBT:
                    pe.wait_ge(S["kb_ready"], 1)
                    pe.wait_ge(S["kdec_ready"], 1)
                for m in range(TB * AH):
                    tb, h = divmod(m, AH)
                    t = slice(tb * P, (tb + 1) * P)
                    last = f32mm(PS[:, banks[m // 4], (m % 4) * P:(m % 4 + 1) * P], Yk[:, h, t], a[:, h, t])
                last.then_inc(done, 1)
            for s in range(LEVELS):
                for g in range(3):
                    pe.wait_ge(S["lvl_m"], 3 * s + g + 1)
                    if s:
                        pe.wait_ge(S["lvl_x"], 3 * (s - 1) + g + 1)
                        pe.wait_ge(S["lvl_xt"], 3 * (s - 1) + g + 1)
                    elif g == 0:
                        pe.wait_ge(S["qd_ready"], 1)
                    for m in range(4 * g, 4 * g + 4):
                        o = PS[:, g, (m % 4) * P:(m % 4 + 1) * P]
                        last = f32mm(o, MT[:, m, :], XM[:, m, :]) if s else nc.tensor.transpose(o, MT[:, m, :], con("ident"))
                    last.then_inc(S["lvl_p1"], 1)
                if s == 0:
                    continue
                for g in range(3):
                    pe.wait_ge(S["lvl_p1sb"], 3 * (s - 1) + g + 1)
                    if s < LEVELS - 1:
                        for m in range(4 * g, 4 * g + 4):
                            f32mm(PS[:, 3 + g, (m % 4) * P:(m % 4 + 1) * P], XT[:, m, :], P1[:, m, :])
                    for m in range(4 * g, 4 * g + 4):
                        last = f32mm(PS[:, g, (m % 4) * P:(m % 4 + 1) * P], P1[:, m, :], XT[:, m, :])
                    last.then_inc(S["lvl_zt"], 1)
            pe.wait_ge(S["lvl_xt"], 3 * LEVELS)
            pe.wait_ge(S["scaled"], 1)
            for c in range(NCHUNK):
                tb, hf = divmod(c, 2)
                if c:
                    pe.wait_ge(S["s_ready"], c)
                    for h in range(AH):
                        last = f32mm(PS[:, 3 + h // 3, (h % 3) * P:(h % 3 + 1) * P], KBT[:, h, tb * P:(tb + 1) * P], ST[:, h, :])
                    last.then_inc(S["ks_ps"], 1)
                pe.wait_ge(S["r_ready"], c + 1)
                if c:
                    pe.wait_ge(S["vn_sb"], c)
                for h in range(AH):
                    last = f32mm(PS[:, 5 + h // 3, (h % 3) * P:(h % 3 + 1) * P], XT[:, tb * AH + h, :], RR[:, h, :])
                last.then_inc(S["vn_ps"], 1)
                pe.wait_ge(S["vn_sb"], c + 1)
                for h in range(AH):
                    o = PS[:, h // 2, (h % 2) * SEQ + CHUNK * c:(h % 2) * SEQ + CHUNK * (c + 1)]
                    if c:
                        f32mm(o, ST[:, h, :], Yq[:, h, CHUNK * c:CHUNK * (c + 1)], True, False)
                    last = f32mm(o, VN[hf][:, h, :], QD[:, tb * AH + h, CHUNK * hf:CHUNK * (hf + 1)], c == 0, True)
                if c == NCHUNK - 1:
                    last.then_inc(S["o_ps"], 1)
                    break
                for h in range(AH):
                    last = f32mm(PS[:, 3 + h // 3, (h % 3) * P:(h % 3 + 1) * P], KD[:, tb, h, :], VN[hf][:, h, :])
                last.then_inc(S["su_ps"], 1)
            pe.wait_ge(S["o_sq"], 3)
            for j in range(AH):
                last = f32mm(PS[0:AH, 6, 0:SEQ], pick(j, AH), OSQ[:, j, :], j == 0, j == AH - 1)
            last.then_inc(S["o_sum"], 1)
            pe.wait_ge(S["o_rc"], 1)
            for j in range(3):
                for k in range(2):
                    last = f32mm(PS[:, 3 + j, k * SEQ:(k + 1) * SEQ], spread(2 * j + k, AH), RS[0:AH, :])
                last.then_inc(S["o_bc"], 1)
            attention("mem0")
            out_linear("out0")
            ffn(1, "ffn1")

            n0 = tile0["dkv"]
            by_feature(n0, 0, "dkv")
            norm("dkv")
            by_feature(n0 + 1, 1, blocks=1, row=P)
            latent(0)
            pe.wait_ge(S["rope_in"], 1)
            f32mm(bank(2, SEQ), con("swap"), KR).then_inc(S["rope_ps"], 1)
            pe.wait_ge(S["lat_ready"], 1)
            pe.wait_ge(S["rope_done"], 1)
            n0 = tile0["ukv"]
            for t in range(2):
                tile_ready(n0 + t)
                for hh in range(3):
                    for kb in range(2):
                        matmul3(PS[:, 4 * t + hh // 2, (hh % 2) * SEQ:(hh % 2 + 1) * SEQ], *w_at(n0 + t, kb * 768 + hh * 2 * P),
                                HH[:, kb, :], HL[:, kb, :], kb == 0, kb == 1)
                    for tb in range(TB):
                        for kb in range(2):
                            q = slice(tb * P, (tb + 1) * P)
                            last = matmul3_tok(PS[:, 4 * t + 2 + tb, hh * P:(hh + 1) * P], HH[:, kb, q], HL[:, kb, q],
                                               *w_at(n0 + t, kb * 768 + hh * 2 * P + P), kb == 0, kb == 1)
                last.then_inc(S["tile_used"], 1)
            pe.wait_ge(S["ukv_evac"], 2)
            ffn(2, "ffn2")

            n0 = tile0["bin"]
            by_feature(n0, 0, "bin")
            norm("bin")
            by_feature(n0 + 1, 1)
            latent(1)
            pe.wait_ge(S["qm_ready"], 2)
            pe.wait_ge(S["lat_ready"], 2)
            n0 = tile0["uq"]
            for t in range(2):
                tile_ready(n0 + t)
                for hh in range(3):
                    for part in range(2):
                        for kb in range(2):
                            last = matmul3(PS[:, 3 * t + hh, part * SEQ:(part + 1) * SEQ],
                                           *w_at(n0 + t, kb * 768 + (2 * hh + part) * P), HH[:, kb, :], HL[:, kb, :],
                                           kb == 0, kb == 1)
                last.then_inc(S["tile_used"], 1)
            pe.wait_ge(S["uq_evac"], 2)
            for j in range(3):
                f32mm(pairs(bank((6 + j) % 8)), con("swap"), QQ[:, 2 * j:2 * j + 2, 1, :]).then_inc(S["uq_ps"], 1)
            pe.wait_ge(S["rope_done"], 2)
            attention("mem1")
            attention("mla")
            out_linear("out1")
            ffn(3, "ffn3")
            norm("final")
            norm("in2")

            n0 = tile0["in2"]
            pe.wait_ge(S["table_loaded"], 32)
            pe.wait_ge(S["norm_sd"], norm_no["in2"] + 1)
            for h in range(MH):
                last = f32mm(bank(4 + h), RELB[:, h:h + 1].broadcast_to([32, P]), TABLE[0:32, 0:2 * SEQ])
            last.then_inc(S["bias_ps"], 1)
            for t in range(9):
                if t >= 4:
                    pe.wait_ge(S["in2_evac"], t - 3)
                if t < 8:
                    by_feature(n0 + t, t % 4, "in2" if t == 0 else None)
                else:
                    by_token(n0 + t, t % 4, CW)
            pe.wait_ge(S["in2_evac"], 9)
            pe.wait_ge(S["qk2_sq"], 1)
            for j in range(2):
                last = f32mm(pairs(bank(j)), con("seg32"), ZS[:, 2 * j:2 * j + 2, :])
            last.then_inc(S["qk2_ps"], 1)
            pe.wait_ge(S["bias_row"], 1)
            pe.wait_ge(S["pooled_ready"], 1)
            for b in range(2):
                last = f32mm(bank(4)[:, b * SEQ:(b + 1) * SEQ], par("pool_w", b * P, P), PL[:, b, :])
            last.then_inc(S["pool_ps"], 1)
            pe.wait_ge(S["conf_ready"], 1)
            for b in range(2):
                last = f32mm(bank(5, SEQ), con("ones"), CV[:, b, :], b == 0, b == 1)
            last.then_inc(S["conf_mean_ps"], 1)
            pe.wait_ge(S["conf_sq"], 1)
            for b in range(2):
                last = f32mm(bank(6, SEQ), con("ones"), CVS[:, b, :], b == 0, b == 1)
            last.then_inc(S["conf_var_ps"], 1)
            pe.wait_ge(S["conf_sd"], 1)
            pe.wait_ge(S["pool_ps"], 1)
            pe.wait_ge(S["conf_y"], 1)
            pe.wait_ge(S["qk2_ready"], 1)
            attention("diff")
            pe.wait_ge(S["sub_sq"], 1)
            f32mm(pairs(bank(5)), con("seg64"), CVS).then_inc(S["sub_ps"], 1)
            out_linear("out2")
            ffn(4, "ffn4")

        @block.gpsimd
        def _(pool):
            step = [0]

            def link(ins):
                step[0] += 1
                ins.then_inc(S["pool_step"], 1)
                pool.wait_ge(S["pool_step"], step[0])

            pool.wait_ge(S["tile_used"], tile0["in2"])
            pool.dma_start(RELB[:, :], d["rel_bias"]).then_inc(S["table_loaded"], 16)
            pool.dma_start(TABLE, d["rel_table"]).then_inc(S["table_loaded"], 16)
            pool.wait_ge(S["bias_row"], 1)
            pool.dma_start(bass.AP(bias_rows, 0, [[ROW + 1, P], [2 * SEQ, MH], [1, 2 * SEQ]]), BROW).then_inc(S["bias_dma"], 16)
            pool.wait_ge(S["bias_dma"], 16)
            for tb in range(TB):
                src = bass.AP(bias_rows, SEQ - 1 - tb * P, [[ROW, P], [2 * SEQ, MH], [1, SEQ]])
                pool.dma_start(BIAS[:, tb, :, :], src).then_inc(S["bias_ready"], 16)
            pool.wait_ge(S["in2_evac"], 3)
            E = SEQ + 16
            link(nc.gpsimd.tensor_tensor(S2[:, :, 2:E], UP[:, :, 2:E], UP[:, :, 1:E - 1], ALU.add))
            link(nc.gpsimd.tensor_tensor(S4[:, :, 4:E], S2[:, :, 4:E], S2[:, :, 2:E - 2], ALU.add))
            link(nc.gpsimd.tensor_tensor(S8[:, :, 8:E], S4[:, :, 8:E], S4[:, :, 4:E - 4], ALU.add))
            link(nc.gpsimd.tensor_tensor(S2[:, 1, 16:E], S8[:, 1, 16:E], S8[:, 1, 8:E - 8], ALU.add))
            for b, rows, src in ((0, slice(0, 64), S2), (0, slice(64, P), S4), (1, slice(0, 64), S8), (1, slice(64, P), S2)):
                lo, hi = CC["inv_win"]
                link(nc.gpsimd.tensor_scalar(PL[rows, b, :], src[rows, b, 16:E], CON[rows, lo + b:lo + b + 1], None, ALU.mult))
                lo, hi = CC["inv_cnt"]
                link(nc.gpsimd.tensor_tensor(PL[rows, b, 0:16], src[rows, b, 16:32], CON[rows, lo + 16 * b:lo + 16 * b + 16], ALU.mult))
            nc.gpsimd.tensor_tensor(PL, PL, UP[:, :, 16:E], ALU.subtract).then_inc(S["pooled_ready"], 1)
            pool.wait_ge(S["pooled_ready"], 1)
            pool.wait_ge(S["in2_evac"], 2)
            pool.wait_ge(S["conf_in"], 1)
            part, term = S4[:, 0, 0:SEQ], S8[:, 0, 0:SEQ]
            for j in range(POOL_TAP, 31):
                lo = PC["conf_w"][0] + 31 + j
                link(nc.gpsimd.tensor_scalar(part if j == POOL_TAP else term, CC_[:, 1, j:j + SEQ], PAR[:, lo:lo + 1], None, ALU.mult))
                if j == POOL_TAP:
                    continue
                last = nc.gpsimd.tensor_tensor(part, part, term, ALU.add)
                if j < 30:
                    link(last)
            last.then_inc(S["conf_pool"], 1)


def layout(a):
    import numpy as np
    f = np.float32

    def cols(v, n=P):
        return v.reshape(-1, n).T

    def rows(v):
        return np.broadcast_to(v.reshape(1, -1), (P, v.size))

    def taps(w):
        k, n = w.shape
        return w.T.reshape(n // P, P, k).transpose(1, 0, 2).reshape(P, -1)

    pool_w = np.zeros((P, 2, P), f)
    for g in range(4):
        r = slice(64 * (g % 2), 64 * (g % 2) + 64)
        pool_w[r, g // 2, r] = a["pool_w_2"][0, g]
    params = {
        "ffn1_norm0": cols(a["ffn1_norm"][0]), "ffn1_norm1": cols(a["ffn1_norm"][1]),
        "ffn2_norm0": cols(a["ffn2_norm"][0]), "ffn2_norm1": cols(a["ffn2_norm"][1]),
        "mix_norm0": cols(a["mix_norm"][0]), "mix_norm1": cols(a["mix_norm"][1]),
        "mem_norm": cols(a["mem_norm"]), "kv_in_norm": cols(a["kv_in_norm"]), "final_norm": cols(a["final_norm"]),
        "norm1_2": cols(a["norm1_g_2"]), "norm2_2": cols(a["norm2_g_2"]), "b_q_norm": cols(a["b_q_norm"]),
        "kv_lat_norm": cols(a["kv_lat_norm"]), "a_out_norm": cols(a["a_out_norm"]), "a_conv": taps(a["a_conv"][0]),
        "pool_scale": cols(a["pool_scale_2"]), "sconv": taps(a["sconv_w_2"][0]), "conf_w": taps(a["conf_dw_w_2"][0]),
        "conf_b": cols(a["conf_dw_b_2"]), "ln_g": cols(a["conf_ln_g_2"]), "ln_b": cols(a["conf_ln_b_2"]),
        "q_g": np.tile(a["q_norm_g_2"].reshape(-1, 1), (4, 1)), "k_g": np.tile(a["k_norm_g_2"].reshape(-1, 1), (4, 1)),
        "subln": np.tile(a["subln_g_2"].reshape(-1, 1), (2, 1)), "A_log": rows(a["a_A_log"]), "dt_bias": rows(a["a_dt_bias"]),
        "lam": rows(np.concatenate([a[f"lam_{n}_2"].reshape(-1) for n in ("q1", "k1", "q2", "k2")])),
        "pool_w": pool_w.reshape(P, -1),
    }
    j, i = np.arange(P)[:, None], np.arange(P)[None, :]
    same = j // CHUNK == i // CHUNK
    level = np.stack([(i // s % 2 == 1) & (j // s == i // s - 1) for s in (1, 2, 4, 8, 16, 32)], 1)
    window = np.array([2, 4, 8, 16])[(np.arange(2)[None, :] * 2 + np.arange(P)[:, None] // 64)]
    count = np.minimum(np.arange(1, 17)[None, None, :], window[:, :, None])
    q = np.arange(SEQ).reshape(2, P).T
    future = np.arange(SEQ)[None, None, :] // CHUNK > (q // CHUNK)[:, :, None]
    inv = (10000.0 ** -(np.arange(0, ROPE, 2) / ROPE)).astype(f)
    consts = {
        "ident": j == i, "ones": np.ones((P, P)), "seg32": j // 32 == i // 32, "seg64": j // 64 == i // 64,
        "swap": 1.0 * ((j == i - 32) & (i % 64 >= 32)) - 1.0 * ((j == i + 32) & (i % 64 < 32)),
        "tri": same & (j <= i), "after": same & (j > i), "level": level.reshape(P, -1),
        "half": np.arange(P)[:, None] < 64, "inv_win": 1.0 / window, "inv_cnt": (1.0 / count).reshape(P, -1),
        "inv_freq": np.tile(inv, 4).reshape(P, 1), "mla_mask": np.where(future, NEG, 0.0).reshape(P, -1),
        "pick": np.broadcast_to(np.arange(23) == 11, (P, 23)),
    }
    dist = SEQ - 1 - np.arange(2 * SEQ)
    n = np.maximum(dist, 0)
    large = 16 + (np.log(np.maximum(n, 1).astype(f) / f(16)) / f(np.log(8.0)) * f(16)).astype(np.int32)
    bucket = np.where(n < 16, n, np.minimum(large, 31))
    rel_table = np.concatenate([np.arange(P)[:, None] == bucket[None, :],
                                np.broadcast_to(np.where(dist < 0, NEG, 0.0), (P, 2 * SEQ))], 1).astype(f)

    def packed(table, parts):
        assert [(k, v.shape[1]) for k, v in parts.items()] == sorted(table, key=lambda t: list(parts).index(t[0]))
        return np.concatenate([parts[k].astype(f, copy=False) for k, _ in table], 1)

    w_uq = a["b_w_uq"][0].reshape(2 * P, BH, P + ROPE)
    out = {
        "x": a["x"][0].T, "mem": a["mem"][0].T, "positions": np.broadcast_to(a["positions"].reshape(1, SEQ), (P, SEQ)),
        "params": packed(PARAMS, params), "consts": packed(CONSTS, consts), "rel_table": rel_table, "rel_bias": a["rel_bias_2"],
        "w_dkv": np.concatenate([a["w_dkv"], a["w_dkv"][:, 2 * P:]], 1),
        "b_w_uq": np.concatenate([w_uq, w_uq[:, :, P:]], 2).reshape(2 * P, -1),
    }
    for name in ("ffn1_w_gu", "ffn1_w_down", "ffn2_w_gu", "ffn2_w_down", "w_out", "w_mem_kv", "a_w_in", "b_w_in", "w_ukv",
                 "w_in_2", "w_out_2", "w_gate_2", "w_up_2", "w_down_2"):
        out[name] = a[name]
    return {k: np.ascontiguousarray(v) for k, v in out.items()}

def kernel(**inputs):
    import numpy as np
    import concourse.bacc as bacc
    from concourse.bass_utils import run_bass_kernel_spmd

    nc = bacc.Bacc("TRN2", target_bir_lowering=False, num_devices=1)
    arrays = layout({k: np.asarray(v) for k, v in inputs.items()})
    d = {name: nc.dram_tensor(f"in_{name}", a.shape, mybir.dt.from_np(a.dtype), kind="ExternalInput").ap()
         for name, a in arrays.items()}
    out = nc.dram_tensor("out_t", (D, SEQ), mybir.dt.float32, kind="ExternalOutput").ap()
    program(nc, d, out)
    r = run_bass_kernel_spmd(nc, [{f"in_{k}": a for k, a in arrays.items()}], core_ids=[0])
    return np.ascontiguousarray(r.results[0]["out_t"].T).reshape(1, SEQ, D)
```
